# Optimizing a Trainium2 kernel written in Bass

```python
import jax
import jax.numpy as jnp
from jax import lax
import numpy as np

D_MODEL = 1024
BATCH = 1
SEQ = 256
DEPTH = 2
DEC_BATCH = 8
DEC_SEQ = 8
PAST_LEN = 2048
PAGE_SIZE = 128

N_META = 16
MIX_WIDTH = D_MODEL
POOL_WIDTH = MIX_WIDTH // 2
CONV_WIDTH = MIX_WIDTH - POOL_WIDTH
POOL_WINDOWS = (2, 4, 8, 16)
N_POOL_GROUPS = len(POOL_WINDOWS)
POOL_GROUP = POOL_WIDTH // N_POOL_GROUPS
POOL_BUF = max(POOL_WINDOWS) - 1
CONV_KERNEL = 31
CONV_BUF = CONV_KERNEL - 1
IN_COLS = POOL_WIDTH + 2 * CONV_WIDTH
D_FF = ((8 * D_MODEL // 3 + 255) // 256) * 256
N_EXPERTS = 8
TOP_K = 2
EXPERT_FF = 7 * D_MODEL // 2
N_DENSE = (DEPTH + 1) // 2
N_MOE = DEPTH // 2
RMS_EPS = 1e-6
LN_EPS = 1e-5

kernel_name = 'hybrid_pool_conformer_conv_decoder_step'

def _rmsnorm(x, g):
    xf = x.astype(jnp.float32)
    y = xf * lax.rsqrt(jnp.mean(xf * xf, axis=-1, keepdims=True) + RMS_EPS)
    return (y * g.astype(jnp.float32)).astype(x.dtype)

def _layernorm(x, g, b):
    xf = x.astype(jnp.float32)
    mu = jnp.mean(xf, axis=-1, keepdims=True)
    var = jnp.mean(jnp.square(xf - mu), axis=-1, keepdims=True)
    y = (xf - mu) * lax.rsqrt(var + LN_EPS)
    return (y * g.astype(jnp.float32) + b.astype(jnp.float32)).astype(x.dtype)

def _pool_mixer(u_past, u_new, start_pos, w_grp, scale):
    n_past = u_past.shape[1]
    ext = jnp.concatenate([u_past.astype(u_new.dtype), u_new], axis=1)
    length = ext.shape[1]
    cs = jnp.cumsum(ext.astype(jnp.float32), axis=1)
    cs0 = jnp.pad(cs, ((0, 0), (1, 0), (0, 0)))
    rows = jnp.arange(n_past, length)
    pos = start_pos + rows
    pooled = []
    for g, win in enumerate(POOL_WINDOWS):
        ch = slice(g * POOL_GROUP, (g + 1) * POOL_GROUP)
        lo = jnp.maximum(rows + 1 - win, 0)
        s = cs0[:, rows + 1, ch] - cs0[:, lo, ch]
        cnt = jnp.minimum(pos + 1, win).astype(jnp.float32)
        pooled.append(s / cnt[None, :, None])
    pooled = jnp.concatenate(pooled, axis=-1) - u_new.astype(jnp.float32)
    b, t, _ = u_new.shape
    pg = pooled.astype(u_new.dtype).reshape(b, t, N_POOL_GROUPS, POOL_GROUP)
    out = jnp.einsum('btgc,gcd->btgd', pg, w_grp).reshape(b, t, POOL_WIDTH) * scale
    return out, ext[:, length - POOL_BUF:]

def _conv_module(a_past, z, dw_w, dw_b, ln_g, ln_b, pw_w):
    v = z[..., :CONV_WIDTH] * jax.nn.sigmoid(z[..., CONV_WIDTH:])
    ext = jnp.concatenate([a_past.astype(v.dtype), v], axis=1)
    y = lax.conv_general_dilated(
        ext, dw_w[:, None, :].astype(v.dtype), window_strides=(1,), padding='VALID',
        dimension_numbers=('NWC', 'WIO', 'NWC'), feature_group_count=CONV_WIDTH) + dw_b
    y = jax.nn.silu(_layernorm(y, ln_g, ln_b))
    return y @ pw_w, ext[:, ext.shape[1] - CONV_BUF:]

def _swiglu(x, wg, wu, wd):
    return (jax.nn.silu(x @ wg) * (x @ wu)) @ wd

def _moe(x, router_w, wg, wu, wd):
    b, t, d = x.shape
    xf = x.reshape(b * t, d)
    logits = (xf @ router_w).astype(jnp.float32)
    top_val, top_idx = lax.top_k(logits, TOP_K)
    gates = jax.nn.softmax(top_val, axis=-1)
    combine = jnp.sum(jax.nn.one_hot(top_idx, N_EXPERTS, dtype=jnp.float32) * gates[..., None], axis=1)
    y = jnp.zeros((b * t, d), jnp.float32)
    for e in range(N_EXPERTS):
        y = y + combine[:, e:e + 1] * _swiglu(xf, wg[e], wu[e], wd[e]).astype(jnp.float32)
    return y.astype(x.dtype).reshape(b, t, d)

def _trunk(h, pool_pasts, conv_pasts, pool_start, norm1_g, w_in, pool_w, pool_scale, conv_dw_w, conv_dw_b,
           conv_ln_g, conv_ln_b, conv_pw_w, w_out, norm2_g, ffn_w_gate, ffn_w_up, ffn_w_down,
           router_w, moe_w_gate, moe_w_up, moe_w_down):
    new_pool, new_conv = [], []
    for l in range(DEPTH):
        hn = _rmsnorm(h, norm1_g[l])
        u = hn @ w_in[l]
        pool_out, pool_buf = _pool_mixer(pool_pasts[l], u[..., :POOL_WIDTH], pool_start, pool_w[l], pool_scale[l])
        conv_out, conv_buf = _conv_module(conv_pasts[l], u[..., POOL_WIDTH:], conv_dw_w[l], conv_dw_b[l],
                                          conv_ln_g[l], conv_ln_b[l], conv_pw_w[l])
        h = h + jnp.concatenate([pool_out, conv_out], axis=-1) @ w_out[l]
        hn = _rmsnorm(h, norm2_g[l])
        if l % 2 == 0:
            i = l // 2
            h = h + _swiglu(hn, ffn_w_gate[i], ffn_w_up[i], ffn_w_down[i])
        else:
            i = l // 2
            h = h + _moe(hn, router_w[i], moe_w_gate[i], moe_w_up[i], moe_w_down[i])
        new_pool.append(pool_buf)
        new_conv.append(conv_buf)
    return h, jnp.stack(new_pool), jnp.stack(new_conv)

def setup_inputs(seed: int = 0) -> dict:
    key = jax.random.key(seed)
    ks = jax.random.split(key, 24)
    f32 = jnp.float32

    def nrm(k, shape, scale):
        return jax.random.normal(k, shape, f32) * scale

    return {
        'x_prompt': nrm(ks[0], (BATCH, SEQ, D_MODEL), 1.0),
        'x_sample': nrm(ks[1], (DEC_BATCH, DEC_SEQ, D_MODEL), 1.0),
        'state_pool': nrm(ks[2], (DEPTH, DEC_BATCH, POOL_BUF, POOL_WIDTH), 1.0),
        'state_conv': nrm(ks[3], (DEPTH, DEC_BATCH, CONV_BUF, CONV_WIDTH), 0.5),
        'meta_tokens': nrm(ks[4], (N_META, D_MODEL), 1.0),
        'norm1_g': 1.0 + nrm(ks[5], (DEPTH, D_MODEL), 0.02),
        'w_in': nrm(ks[6], (DEPTH, D_MODEL, IN_COLS), D_MODEL ** -0.5),
        'pool_w': nrm(ks[7], (DEPTH, N_POOL_GROUPS, POOL_GROUP, POOL_GROUP), POOL_GROUP ** -0.5),
        'pool_scale': 1.0 + nrm(ks[8], (DEPTH, POOL_WIDTH), 0.02),
        'conv_dw_w': nrm(ks[9], (DEPTH, CONV_KERNEL, CONV_WIDTH), CONV_KERNEL ** -0.5),
        'conv_dw_b': nrm(ks[10], (DEPTH, CONV_WIDTH), 0.02),
        'conv_ln_g': 1.0 + nrm(ks[11], (DEPTH, CONV_WIDTH), 0.02),
        'conv_ln_b': nrm(ks[12], (DEPTH, CONV_WIDTH), 0.02),
        'conv_pw_w': nrm(ks[13], (DEPTH, CONV_WIDTH, CONV_WIDTH), CONV_WIDTH ** -0.5),
        'w_out': nrm(ks[14], (DEPTH, MIX_WIDTH, D_MODEL), MIX_WIDTH ** -0.5),
        'norm2_g': 1.0 + nrm(ks[15], (DEPTH, D_MODEL), 0.02),
        'ffn_w_gate': nrm(ks[16], (N_DENSE, D_MODEL, D_FF), D_MODEL ** -0.5),
        'ffn_w_up': nrm(ks[17], (N_DENSE, D_MODEL, D_FF), D_MODEL ** -0.5),
        'ffn_w_down': nrm(ks[18], (N_DENSE, D_FF, D_MODEL), D_FF ** -0.5),
        'router_w': nrm(ks[19], (N_MOE, D_MODEL, N_EXPERTS), D_MODEL ** -0.5),
        'moe_w_gate': nrm(ks[20], (N_MOE, N_EXPERTS, D_MODEL, EXPERT_FF), D_MODEL ** -0.5),
        'moe_w_up': nrm(ks[21], (N_MOE, N_EXPERTS, D_MODEL, EXPERT_FF), D_MODEL ** -0.5),
        'moe_w_down': nrm(ks[22], (N_MOE, N_EXPERTS, EXPERT_FF, D_MODEL), EXPERT_FF ** -0.5),
        'final_norm_g': 1.0 + nrm(ks[23], (D_MODEL,), 0.02),
    }

def reference(x_prompt, x_sample, state_pool, state_conv, meta_tokens, norm1_g, w_in, pool_w, pool_scale,
              conv_dw_w, conv_dw_b, conv_ln_g, conv_ln_b, conv_pw_w, w_out, norm2_g, ffn_w_gate, ffn_w_up,
              ffn_w_down, router_w, moe_w_gate, moe_w_up, moe_w_down, final_norm_g):
    weights = (norm1_g, w_in, pool_w, pool_scale, conv_dw_w, conv_dw_b, conv_ln_g, conv_ln_b, conv_pw_w,
               w_out, norm2_g, ffn_w_gate, ffn_w_up, ffn_w_down, router_w, moe_w_gate, moe_w_up, moe_w_down)
    b = x_prompt.shape[0]
    meta = jnp.broadcast_to(meta_tokens[None].astype(x_prompt.dtype), (b, N_META, D_MODEL))
    hp = jnp.concatenate([meta, x_prompt], axis=1)
    zp = jnp.zeros((DEPTH, b, 0, POOL_WIDTH), x_prompt.dtype)
    zc = jnp.zeros((DEPTH, b, CONV_BUF, CONV_WIDTH), x_prompt.dtype)
    hp, new_pool_p, new_conv_p = _trunk(hp, zp, zc, 0, *weights)
    y_prompt = _rmsnorm(hp[:, N_META:], final_norm_g)
    hs, new_pool_s, new_conv_s = _trunk(x_sample, state_pool, state_conv, PAST_LEN - POOL_BUF, *weights)
    y_sample = _rmsnorm(hs, final_norm_g)
    return (y_prompt, y_sample, new_pool_p, new_conv_p, new_pool_s, new_conv_s)


_drawn_inputs = setup_inputs


def setup_inputs(seed=0):
    import zlib

    import numpy as np

    out = dict(_drawn_inputs(seed))
    spreads = {}
    factors = {}
    for name, (base, spread) in spreads.items():
        noise = np.random.default_rng([zlib.crc32(name.encode()), seed]).standard_normal(out[name].shape)
        drawn = base * np.exp(spread * noise) if base else spread * noise
        out[name] = jnp.asarray(drawn.astype(out[name].dtype))
    for name, factor in factors.items():
        out[name] = (out[name] * factor).astype(out[name].dtype)
    return out
```

```python
from contextlib import ExitStack

import concourse.bass as bass
from concourse import mybir

F32 = mybir.dt.float32
F32R = mybir.dt.float32r
I32 = mybir.dt.int32
U32 = mybir.dt.uint32
ALU = mybir.AluOpType
ACT = mybir.ActivationFunctionType
AX_X = mybir.AxisListType.X
ds = bass.ds

P = 128
MM_BANKS = 6
RAW = 6
SPLIT = 3
SLOT = 2048
RSQRT_SEED = float(0x5F3759DF)


def hybrid_trunk(nc, x_prompt, x_sample, state_pool, state_conv, meta_tokens, norm1_g, w_in, pool_w,
                 pool_scale, conv_dw_w, conv_dw_b, conv_ln_g, conv_ln_b, conv_pw_w, w_out, norm2_g,
                 ffn_w_gate, ffn_w_up, ffn_w_down, router_w, moe_w_gate, moe_w_up, moe_w_down,
                 final_norm_g, y_prompt, y_sample, pool_p, conv_p, pool_s, conv_s):
    D = x_prompt.shape[2]
    SEQ, META = x_prompt.shape[1], meta_tokens.shape[0]
    DB, DS = x_sample.shape[0], x_sample.shape[1]
    L = w_in.shape[0]
    PW = state_pool.shape[3]
    CW = state_conv.shape[3]
    PB, CB = state_pool.shape[2], state_conv.shape[2]
    TAPS = conv_dw_w.shape[1]
    FF = ffn_w_gate.shape[2]
    NE = router_w.shape[2]
    EF = moe_w_gate.shape[3]
    KD = D // P
    TP = META + SEQ
    T = TP + DB * DS
    TT = T // 3
    KC = CW // P
    NG = PW // P
    NFT = FF // P
    WINDOWS = [2 << g for g in range(NG)]
    assert (L, KD, KC, NG, T % 3) == (2, 8, 4, 4, 0) and TT <= P
    PSEG, CSEG = PB + TP, CB + TP
    PS1, CS1 = PB + DS, CB + DS
    PEXT, CEXT = PSEG + DB * PS1, CSEG + DB * CS1
    HB = DB // 2

    WIN_ORDER = [2, 4, 3, 5, 0, 1]
    MIX_SLOTS = 12
    DOWN_PARTS = [[6, 6, 5, 5], [6, 6, 5, 5], [8, 8, 6], [8, 8, 6]]
    FFN_BASE = MIX_SLOTS
    N_GU = 2 * (FF // 256)
    DOWN_BASE = FFN_BASE + N_GU
    MIX_BASE = [0, DOWN_BASE + sum(len(x) for x in DOWN_PARTS)]
    MOE_BASE = MIX_BASE[1] + MIX_SLOTS
    NJ = EF // 512
    ES = 6 * NJ
    assert MOE_BASE % RAW == 0 and ES % RAW == 0 and FFN_BASE % RAW == 0
    NSEL = NE + 6

    def gate_slot(j):
        return 0 if j == 0 else 6 * j - 2

    def up_slot(j):
        return gate_slot(j) + 2

    def down_slot(j):
        return 6 * j + 8 if j < NJ - 1 else 6 * j + 4

    GROUP = {}

    def plan(*names):
        for name in names:
            GROUP[name] = len(GROUP)

    plan(*[("x", k) for k in range(KD)], ("params",))
    for l in range(L):
        plan(*[("win", l, 2 * s + i) for s in WIN_ORDER[:2] for i in (0, 1)])
        plan(("past_pool", l), ("past_conv", l, 0), ("past_conv", l, 1))
        plan(*[("win", l, 2 * s + i) for s in WIN_ORDER[2:] for i in (0, 1)])
        plan(*[("pool", l, g) for g in range(NG)], *[("pw", l, m) for m in range(KC)])
        plan(*[("wout", l, m) for m in range(KD)])
        if l == 1:
            plan(*[("htok", t, i) for t in range(3) for i in (0, 1)])
        plan(*[("state", l, i) for i in range(5)])
        if l == 0:
            plan(*[("gu", u, i) for u in range(FF // 256) for i in range(4)])
            plan(*[("down", m) for m in range(KD)])
    N_GROUPS = len(GROUP)

    with ExitStack() as ctx:
        def sem(name):
            return ctx.enter_context(nc.semaphore(name))

        def sb(name, shape, dt=F32, at=ctx):
            return at.enter_context(nc.sbuf_tensor(name, shape, dt))

        raw = sb("raw", [P, RAW, SLOT])
        w_hi = sb("w_hi", [P, SPLIT, SLOT], F32R)
        w_lo = sb("w_lo", [P, SPLIT, SLOT], F32R)
        h = sb("h", [P, KD, T])
        ident = sb("ident", [P, P])
        ones = sb("ones", [P, P])
        before = sb("before", [P, P])
        iota_slot = sb("iota_slot", [P, P])
        iota_e = sb("iota_e", [P, NE])
        inv_cnt = sb("inv_cnt", [P, 16])
        params = sb("params", [P, 64 + L * KC * TAPS])
        rw = sb("rw", [P, KD, NE])
        rwg = sb("rwg", [P, KD, NE])
        nt = sb("nt", [P, 3, 4])
        NG1, NG2, PSC, DWB, LNG, LNB = 0, 8, 16, 20, 24, 28

        def col(l, which, k):
            c = 32 * l + which + k
            return params[:, c:c + 1]

        def tap(l, c, j):
            at = 64 + (l * KC + c) * TAPS + j
            return params[:, at:at + 1]

        dense = ExitStack()
        x_hi = sb("x_hi", [P, KD, T], F32R, dense)
        x_lo = sb("x_lo", [P, KD, T], F32R, dense)
        rstd = sb("rstd", [P, T], F32, dense)
        nrm_a = sb("nrm_a", [P, T], F32, dense)
        nrm_t = sb("nrm_t", [P, T], F32, dense)
        sqs = sb("sqs", [P, T], F32, dense)
        sq = sb("sq", [P, T], F32, dense)
        mixer = ExitStack()
        m_hi = sb("m_hi", [P, KD, T], F32R, mixer)
        m_lo = sb("m_lo", [P, KD, T], F32R, mixer)
        pool_ext = sb("pool_ext", [P, NG, PEXT], F32, mixer)
        win_sum = sb("win_sum", [P, 2, PEXT], F32, mixer)
        conv_ext = sb("conv_ext", [P, KC, CEXT], F32, mixer)
        y = sb("y", [P, KC, T], F32, mixer)
        z = sb("z", [P, 4, T], F32, mixer)
        y_pool = sb("y_pool", [P, NG, T], F32, mixer)
        state_io = sb("state_io", [DB * PB, 5, 512], F32, mixer)
        mixer.close()
        ffn = ExitStack()
        f_hi = sb("f_hi", [P, NFT, T], F32R, ffn)
        f_lo = sb("f_lo", [P, NFT, T], F32R, ffn)
        gs = sb("gs", [P, 2, T], F32, ffn)
        us = sb("us", [P, 2, T], F32, ffn)
        ffn.close()
        first = ExitStack()
        x_tok = sb("x_tok", [TT, 3, D], F32, first)
        par_rows = sb("par_rows", [64, P], F32, first)
        dw_rows = sb("dw_rows", [TAPS, L, CW], F32, first)
        first.close()
        dense.close()
        moe = ctx
        yt = sb("yt", [TT, 3, D], F32, moe)
        hn_hi = sb("hn_hi", [TT, 3, D], F32R, moe)
        hn_lo = sb("hn_lo", [TT, 3, D], F32R, moe)
        gb = sb("gb", [TT, 2, D], F32, moe)
        hn = sb("hn", [TT, 3, D], F32, moe)
        xg_hi = sb("xg_hi", [P, KD, P], F32R, moe)
        xg_lo = sb("xg_lo", [P, KD, P], F32R, moe)
        act_s = sb("act_s", [P, 512], F32, moe)
        act_f = sb("act_f", [P, 512], F32, moe)
        ft_hi = sb("ft_hi", [P, 4, P], F32R, moe)
        ft_lo = sb("ft_lo", [P, 4, P], F32R, moe)
        o_hi = sb("o_hi", [P, D], F32R, moe)
        o_lo = sb("o_lo", [P, D], F32R, moe)
        sel = sb("sel", [TT, 3, P], F32R, moe)
        sel_t = sb("sel_t", [P, T], F32R, moe)
        slot_gate = sb("slot_gate", [P, 1], F32, moe)
        lg = sb("lg", [TT, 3, NE], F32, moe)
        top = sb("top", [TT, 3, 8], F32, moe)
        top_i = sb("top_i", [TT, 3, 8], U32, moe)
        top_f = sb("top_f", [TT, 3, 2], F32, moe)
        gt = sb("gt", [TT, 3, 4], F32, moe)
        hot1 = sb("hot1", [TT, 3, NE], F32, moe)
        hot2 = sb("hot2", [TT, 3, NE], F32, moe)
        hot = sb("hot", [TT, 3, NE], F32, moe)
        gates = sb("gates", [TT, 3, 2, NE], F32, moe)
        posm = sb("posm", [TT, 3, NE], F32, moe)
        posc = sb("posc", [TT, 3, 2, NE], F32, moe)
        POS = sb("POS", [TT, 3, NSEL], F32, moe)
        GT = sb("GT", [TT, 3, NSEL], F32, moe)
        cnt = sb("cnt", [P, NE], F32, moe)
        over = sb("over", [P, 2, NE], F32, moe)
        n_chunks = sb("n_chunks", [P, NE], F32, moe)
        key = sb("key", [P, 2, NE], F32, moe)
        pick = sb("pick", [P, 6, 2 * NE], F32, moe)
        prod = sb("prod", [P, 6, 2 * NE], F32, moe)
        key_sum = sb("key_sum", [P, 1], F32, moe)
        prod3 = sb("prod3", [TT, 3, 2 * NE], F32, moe)
        eids_f = sb("eids_f", [P, 8], F32, moe)
        eids = sb("eids", [P, 8], I32, moe)

        ps = ctx.enter_context(nc.psum_tensor("ps", [P, 8, 512], F32))
        SUM_BANK = ps[:, 6, 0:T]
        G_, U_, T_, X0, X1, X2 = (ps[:, i, :] for i in (0, 1, 2, 5, 6, 7))
        D_ = ps[:, 3:5, :]

        landed = [sem(f"landed{i}") for i in range(RAW)]
        hi_done, lo_done, w_used = sem("hi_done"), sem("lo_done"), sem("w_used")
        mm_done, evac = sem("mm_done"), sem("evac")
        consts = sem("consts")
        x_landed, par_landed, past_landed = sem("x_landed"), sem("par_landed"), sem("past_landed")
        x_hi_done, x_lo_done = sem("x_hi_done"), sem("x_lo_done")
        sq_ready, sums_done, sums_read = sem("sq_ready"), sem("sums_done"), sem("sums_read")
        ext_zero = sem("ext_zero")
        z_scaled, tanh_done, v_done = sem("z_scaled"), sem("tanh_done"), sem("v_done")
        pooled, pooled_hi, pooled_lo = sem("pooled"), sem("pooled_hi"), sem("pooled_lo")
        m_hi_done = sem("m_hi_done")
        y_sum, ln_centred, ln_sq, ln_sqsum = sem("y_sum"), sem("ln_centred"), sem("ln_sq"), sem("ln_sqsum")
        ln_scaled, ln_act, ln_lo = sem("ln_scaled"), sem("ln_act"), sem("ln_lo")
        packed = sem("packed")
        rw_landed, conv_step = sem("rw_landed"), sem("conv_step")
        gate_scaled, silu_done = sem("gate_scaled"), sem("silu_done")
        f_ready, f_hi_done, f_lo_done = sem("f_ready"), sem("f_hi_done"), sem("f_lo_done")
        state_stored = sem("state_stored")
        gb_landed, hn_sq = sem("gb_landed"), sem("hn_sq")
        rwg_done, logits_done, hot_done, ranks_done = sem("rwg_done"), sem("logits_done"), sem("hot_done"), sem("ranks_done")
        gap_done, exp_done, hn_done, hn_hi_done, hn_lo_done = (sem(n) for n in ("gap_done", "exp_done", "hn_done", "hn_hi_done", "hn_lo_done"))
        routed, extra_done = sem("routed"), sem("extra_done")
        sel_ready, gather_done, xg_hi_done, xg_lo_done = (sem(n) for n in ("sel_ready", "gather_done", "xg_hi_done", "xg_lo_done"))
        g_done, u_done, e_silu, e_f, t_done, ft_hi_done, ft_lo_done, d_done = (
            sem(n) for n in ("g_done", "u_done", "e_silu", "e_f", "t_done", "ft_hi_done", "ft_lo_done", "d_done"))
        o_hi_done, o_lo_done, comb_done, comb_read = (sem(n) for n in ("o_hi_done", "o_lo_done", "comb_done", "comb_read"))
        selt_done, selt_read = sem("selt_done"), sem("selt_read")
        fin_sq, fin_out, stored = sem("fin_sq"), sem("fin_out"), sem("stored")
        dve_step, act_step, pool_step = sem("dve_step"), sem("act_step"), sem("pool_step")

        def h_group(i, k):
            return GROUP[[("x", k), ("wout", 0, k), ("down", k)][i]] + 1

        def token_pieces():
            out = []
            for name, start, n in (("meta", 0, META), ("prompt", META, SEQ), ("sample", TP, DB * DS)):
                at = start
                while at < start + n:
                    m = min(start + n, (at // TT + 1) * TT) - at
                    out.append((at // TT, at % TT, m, name, at - start))
                    at += m
            return out

        PIECES = token_pieces()
        SRC = {"meta": meta_tokens, "prompt": x_prompt[0], "sample": x_sample.rearrange("a b d -> (a b) d")}
        DST = {"prompt": y_prompt[0], "sample": y_sample.rearrange("a b d -> (a b) d")}

        def samples(ap):
            return ap.rearrange("p (b t) -> p b t", b=DB)

        def state_dsts(l):
            return [(pool_s[l].rearrange("b r d -> (b r) d"), DB * PB),
                    (conv_s[l, 0:HB].rearrange("b r d -> (b r) d"), DB * PB),
                    (conv_s[l, HB:DB].rearrange("b r d -> (b r) d"), DB * PB),
                    (pool_p[l, 0], PB), (conv_p[l, 0], CB)]

        SUMS = {name: i for i, name in enumerate(
            [("norm", 0), ("mean", 0), ("var", 0), ("norm", 1), ("norm", 2), ("mean", 1), ("var", 1)])}

        def raw_slot(i):
            return raw[:, i % RAW, :]

        def blk(w, k0, nk, c0, nc_):
            return w[k0 * P:(k0 + nk) * P, c0:c0 + nc_].rearrange("(k p) n -> p k n", p=P), nk, nc_

        def dense_slots():
            out = []
            for l in range(L):
                out += [blk(w_in[l], 0, KD, 256 * s, 256) for s in WIN_ORDER]
                out.append((pool_w[l].rearrange("g p n -> p g n"), NG, P))
                out.append(blk(conv_pw_w[l], 0, KC, 0, CW))
                out += [blk(w_out[l], 0, KD, 256 * s, 256) for s in range(4)]
                if l == 0:
                    for u in range(FF // 256):
                        out.append(blk(ffn_w_gate[0], 0, KD, 256 * u, 256))
                        out.append(blk(ffn_w_up[0], 0, KD, 256 * u, 256))
                    for c, parts in enumerate(DOWN_PARTS):
                        k0 = 0
                        for nk in parts:
                            out.append(blk(ffn_w_down[0], k0, nk, 256 * c, 256))
                            k0 += nk
            return out

        SLOTS = dense_slots()
        assert len(SLOTS) == MOE_BASE

        def slot_size(n):
            return SLOTS[n][1] * SLOTS[n][2]

        block = ctx.enter_context(nc.Block())

        @block.sync
        def _(sp):
            def reuse(n):
                sp.wait_ge(lo_done, n - RAW + 1)

            for n, (src, nk, ncol) in enumerate(SLOTS):
                if n >= RAW:
                    reuse(n)
                dst = raw[:, n % RAW, 0:nk * ncol].rearrange("p (k n) -> p k n", k=nk)
                sp.dma_start(dst, src).then_inc(landed[n % RAW], 16)

            def load_expert(p, e):
                for j in range(NJ):
                    todo = [(gate_slot(j) + i, moe_w_gate, i, j) for i in (0, 1)]
                    todo += [(up_slot(j) + i, moe_w_up, i, j) for i in (0, 1)]
                    for jj in ([j - 1] if j else []) + ([j] if j == NJ - 1 else []):
                        todo += [(down_slot(jj) + i, moe_w_down, i, jj) for i in (0, 1)]
                    for i, w, half, jj in todo:
                        reuse(MOE_BASE + ES * p + i)
                        we = w[0, ds(e, 1)]
                        if w is moe_w_down:
                            src = we[:, (4 * jj + 2 * half) * P:(4 * jj + 2 * half + 2) * P, :]
                            src = src.rearrange("a (k p) n -> p (a k) n", p=P)
                            dst = raw_slot(i).rearrange("p (k n) -> p k n", k=2)
                        else:
                            src = we[:, 4 * half * P:4 * (half + 1) * P, 512 * jj:512 * (jj + 1)]
                            src = src.rearrange("a (k p) n -> p (a k) n", p=P)
                            dst = raw_slot(i).rearrange("p (k n) -> p k n", k=4)
                        sp.dma_start(dst, src).then_inc(landed[i % RAW], 16)

            with sp.Fori(0, NE) as p:
                load_expert(p, p)
            sp.wait_ge(extra_done, 1)
            n_over = sp.value_load(eids[0:1, 6:7], min_val=0, max_val=5)
            with sp.If(n_over > 0):
                with sp.Fori(0, n_over) as i:
                    e = sp.value_load(eids[0:1, ds(i, 1)], min_val=0, max_val=NE - 1)
                    load_expert(i + NE, e)
                sp.nop()
            n_out = 0
            for t, r, m, name, row in PIECES:
                if name != "meta":
                    sp.wait_ge(fin_out, t + 1)
                    sp.dma_start(DST[name][row:row + m, :], yt[r:r + m, t, :]).then_inc(stored, 16)
                    n_out += 1
            sp.wait_ge(stored, 16 * n_out)
            sp.wait_ge(state_stored, 16 * 5 * L)

        @block.gpsimd
        def _(pool):
            step = [0]

            def link(ins):
                step[0] += 1
                ins.then_inc(pool_step, 1)
                pool.wait_ge(pool_step, step[0])

            link(nc.gpsimd.memset(ident[:], 0.0))
            link(nc.gpsimd.affine_select(out=ident[:], in_=ident[:], compare_op=ALU.not_equal, fill=1.0,
                                         base=0, pattern=[[-1, P]], channel_multiplier=1))
            link(nc.gpsimd.memset(ones[:], 1.0))
            link(nc.gpsimd.memset(before[:], 0.0))
            link(nc.gpsimd.affine_select(out=before[:], in_=before[:], compare_op=ALU.is_ge, fill=1.0,
                                         base=0, pattern=[[-1, P]], channel_multiplier=1))
            link(nc.gpsimd.iota(iota_slot[:], pattern=[[1, P]], base=0, channel_multiplier=0,
                                allow_small_or_imprecise_dtypes=True))
            link(nc.gpsimd.iota(iota_e[:], pattern=[[1, NE]], base=0, channel_multiplier=0,
                                allow_small_or_imprecise_dtypes=True))
            for t in range(16):
                link(nc.gpsimd.memset(inv_cnt[:, t:t + 1], 1.0 / (t + 1)))
            nc.gpsimd.sem_inc(consts, 1)

            def squares(i):
                if i:
                    pool.wait_ge(sums_done, SUMS[("norm", i - 1)] + 1)
                for k in range(KD):
                    pool.wait_ge(evac, h_group(i, k))
                    if k == 0:
                        link(nc.gpsimd.tensor_tensor(sqs[:], h[:, 0, :], h[:, 0, :], ALU.mult))
                        continue
                    link(nc.gpsimd.tensor_tensor(sq[:], h[:, k, :], h[:, k, :], ALU.mult))
                    link(nc.gpsimd.tensor_tensor(sqs[:], sqs[:], sq[:], ALU.add))
                pool.sem_inc(sq_ready, 1)

            def mixer_layer(l):
                if l == 0:
                    pool.wait_ge(evac, GROUP[("params",)] + 1)
                else:
                    squares(2)
                pool.dma_start(state_io[:, 0, :], state_pool[l].rearrange("b r d -> (b r) d")
                               ).then_inc(past_landed, 16)
                for i in (0, 1):
                    pool.dma_start(state_io[:, 1 + i, :],
                                   state_conv[l, HB * i:HB * (i + 1)].rearrange("b r d -> (b r) d")
                                   ).then_inc(past_landed, 16)
                link(nc.gpsimd.memset(pool_ext[:, :, 0:PB], 0.0))
                link(nc.gpsimd.memset(conv_ext[:, :, 0:CB], 0.0))
                pool.sem_inc(ext_zero, 1)
                if l == 0:
                    squares(0)
                for g in range(NG):
                    pool.wait_ge(evac, GROUP[("win", l, g)] + 1)
                    src, shift = pool_ext[:, g, :], 1
                    for s in range(g + 1):
                        dst = win_sum[:, s % 2, :]
                        lo = 2 * shift - 1
                        link(nc.gpsimd.tensor_tensor(dst[:, lo:PEXT], src[:, lo:PEXT],
                                                     src[:, lo - shift:PEXT - shift], ALU.add))
                        src, shift = dst, 2 * shift
                    mean, win = win_sum[:, (g + 1) % 2, :], WINDOWS[g]
                    link(nc.gpsimd.tensor_scalar(mean[:, PB:PEXT], src[:, PB:PEXT], 1.0 / win, 0.0,
                                                 ALU.mult, ALU.add))
                    link(nc.gpsimd.tensor_tensor(mean[:, PB:PB + win - 1], src[:, PB:PB + win - 1],
                                                 inv_cnt[:, 0:win - 1], ALU.mult))
                    link(nc.gpsimd.tensor_tensor(y_pool[:, g, 0:TP], mean[:, PB:PSEG], pool_ext[:, g, PB:PSEG],
                                                 ALU.subtract))
                    link(nc.gpsimd.tensor_tensor(samples(y_pool[:, g, TP:T])[:, :, 0:DS],
                                                 samples(mean[:, PSEG:PEXT])[:, :, PB:PS1],
                                                 samples(pool_ext[:, g, PSEG:PEXT])[:, :, PB:PS1], ALU.subtract))
                    pool.sem_inc(pooled, 1)
                for g in range(NG):
                    pool.wait_ge(pooled_hi, NG * l + g + 1)
                    nc.gpsimd.tensor_tensor(x_lo[:, 4 + g, :], y_pool[:, g, :], x_hi[:, 4 + g, :].bitcast(F32),
                                            ALU.subtract).then_inc(pooled_lo, 1)
                for c in range(1, KC):
                    pool.wait_ge(ln_sq, KC * l + c + 1)
                    link(nc.gpsimd.tensor_tensor(z[:, 0, :], z[:, 0, :], z[:, c, :], ALU.add))
                pool.sem_inc(ln_sqsum, 1)
                pool.wait_ge(ln_lo, KC * (l + 1))
                for g in range(NG):
                    link(nc.gpsimd.tensor_copy(samples(z[:, g, 0:DB * PB]),
                                               samples(pool_ext[:, g, PSEG:PEXT])[:, :, DS:PS1]))
                    link(nc.gpsimd.tensor_copy(samples(y[:, g, 0:DB * CB]),
                                               samples(conv_ext[:, g, CSEG:CEXT])[:, :, DS:CS1]))
                pool.sem_inc(packed, 1)
                if l == 0:
                    squares(1)
                else:
                    pool.wait_ge(evac, GROUP[("wout", 1, KD - 1)] + 1)
                    for i, g in enumerate((norm2_g[1:2, :], final_norm_g.rearrange("(a d) -> a d", a=1))):
                        pool.dma_start(gb[:, i, :], g.broadcast_to([TT, D])
                                       ).then_inc(gb_landed, 16)
                for i, (dst, rows) in enumerate(state_dsts(l)):
                    pool.wait_ge(evac, GROUP[("state", l, i)] + 1)
                    pool.dma_start(dst, state_io[0:rows, i, :]).then_inc(state_stored, 16)

            mixer_layer(0)
            pool.wait_ge(state_stored, 16 * 5)
            mixer_layer(1)

            def fold(x, out):
                n = 2 * NE
                while n > 2:
                    n //= 2
                    link(nc.gpsimd.tensor_tensor(x[:, :, 0:n], x[:, :, 0:n], x[:, :, n:2 * n], ALU.add))
                link(nc.gpsimd.tensor_tensor(out, x[:, :, 0], x[:, :, 1], ALU.add))

            pool.wait_ge(routed, 1)
            pool.wait_ge(state_stored, 16 * 10)
            for c in (0, 1):
                link(nc.gpsimd.tensor_scalar(over[:, c, :], cnt[:], float(P * (c + 1)), None, ALU.is_gt))
            link(nc.gpsimd.tensor_tensor(n_chunks[:], over[:, 0, :], over[:, 1, :], ALU.add))
            link(nc.gpsimd.memset(key[:, 0, 0:1], 0.0))
            for e in range(1, NE):
                link(nc.gpsimd.tensor_tensor(key[:, 0, e:e + 1], key[:, 0, e - 1:e], n_chunks[:, e - 1:e], ALU.add))
            link(nc.gpsimd.tensor_copy(key_sum[:], key[:, 0, NE - 1:NE]))
            link(nc.gpsimd.tensor_scalar(key[:, 1, :], key[:, 0, :], 2.0, None, ALU.add))
            link(nc.gpsimd.tensor_scalar(key[:, 0, :], key[:, 0, :], 1.0, None, ALU.add))
            link(nc.gpsimd.tensor_tensor(key[:], key[:], over[:], ALU.mult))
            flat = key[:].rearrange("p c e -> p (c e)")
            for i in range(6):
                link(nc.gpsimd.tensor_scalar(pick[:, i, :], flat, float(i + 1), None, ALU.is_equal))
            for i in range(6):
                for c in (0, 1):
                    link(nc.gpsimd.tensor_tensor(prod[:, i, NE * c:NE * (c + 1)], pick[:, i, NE * c:NE * (c + 1)],
                                                 iota_e[:], ALU.mult))
            fold(prod, eids_f[:, 0:6])
            link(nc.gpsimd.tensor_tensor(eids_f[:, 6:7], key_sum[:], n_chunks[:, NE - 1:NE], ALU.add))
            link(nc.gpsimd.tensor_copy(eids[:, 0:7], eids_f[:, 0:7]))
            for c in (0, 1):
                link(nc.gpsimd.tensor_scalar(posc[:, :, c, :], posm[:], 1.0 - P * (c + 1), None, ALU.add))
            for i in range(6):
                for src, dst in ((posc, POS), (gates, GT)):
                    for t in range(3):
                        link(nc.gpsimd.tensor_tensor(prod3[:, t, :], src[:, t].rearrange("p c e -> p (c e)"),
                                                     pick[0:TT, i, :], ALU.mult))
                    fold(prod3, dst[:, :, NE + i])
            link(nc.gpsimd.tensor_scalar(POS[:, :, NE:NSEL], POS[:, :, NE:NSEL], -1.0, None, ALU.add))
            pool.sem_inc(extra_done, 1)

        def dense_used():
            out, n_w = [], 0
            for n in range(MOE_BASE):
                b = next(x for x in (MIX_BASE[1], FFN_BASE, 0) if n >= x)
                if b == FFN_BASE and n >= DOWN_BASE:
                    ends = [sum(len(x) for x in DOWN_PARTS[:c + 1]) - 1 for c in range(4)]
                    if n - DOWN_BASE in ends:
                        out.append((mm_done, GROUP[("down", 2 * ends.index(n - DOWN_BASE) + 1)] + 1))
                    else:
                        n_w += 1
                        out.append((w_used, n_w))
                elif b == FFN_BASE:
                    u, i = divmod(n - b, 2)
                    out.append((mm_done, GROUP[("gu", u, 2 * i + 1)] + 1))
                else:
                    l, i = MIX_BASE.index(b), n - b
                    last = (("win", l, 2 * WIN_ORDER[i] + 1) if i < 6 else ("pool", l, NG - 1) if i == 6 else
                            ("pw", l, KC - 1) if i == 7 else ("wout", l, 2 * (i - 8) + 1))
                    out.append((mm_done, GROUP[last] + 1))
            return out, n_w

        DENSE_USED, W_BASE = dense_used()
        PASS_USED = [None] * ES
        for j in range(NJ):
            PASS_USED[gate_slot(j) + 1] = (g_done, NJ, j + 1)
            PASS_USED[up_slot(j) + 1] = (u_done, NJ, j + 1)
        PASS_USED[down_slot(NJ - 1) + 1] = (d_done, 1, 2)
        W_PASS = PASS_USED.count(None)
        N_W = 0
        for i in range(ES):
            if PASS_USED[i] is None:
                N_W += 1
                PASS_USED[i] = (w_used, W_PASS, W_BASE + N_W)

        def wait_used_dense(eng, n):
            s, v = DENSE_USED[n]
            eng.wait_ge(s, v)

        def wait_used_pass(eng, p, i):
            s, per, v = PASS_USED[i % ES]
            if i < 0:
                v -= per
            eng.wait_ge(s, p * per + v)

        def parts(n, size=SLOT):
            return raw[:, n % RAW, 0:size], w_hi[:, n % SPLIT, 0:size], w_lo[:, n % SPLIT, 0:size]

        def split_hi_dense(act, n):
            r, hi, _ = parts(n, slot_size(n))
            act.wait_ge(landed[n % RAW], 16 * (n // RAW + 1))
            if n >= SPLIT:
                wait_used_dense(act, n - SPLIT)
            nc.scalar.activation(hi, r, ACT.Copy).then_inc(hi_done, 1)

        def split_lo_dense(dve, n):
            r, hi, lo = parts(n, slot_size(n))
            dve.wait_ge(hi_done, n + 1)
            nc.vector.tensor_tensor(lo, r, hi.bitcast(F32), ALU.subtract).then_inc(lo_done, 1)

        def split_hi_pass(act, p, i):
            r, hi, _ = parts(i)
            act.wait_ge(landed[i % RAW], p * (16 * ES // RAW) + 16 * (MOE_BASE // RAW + i // RAW + 1))
            wait_used_pass(act, p, i - SPLIT)
            nc.scalar.activation(hi, r, ACT.Copy).then_inc(hi_done, 1)

        def split_lo_pass(dve, p, i):
            r, hi, lo = parts(i)
            dve.wait_ge(hi_done, p * ES + (MOE_BASE + i + 1))
            nc.vector.tensor_tensor(lo, r, hi.bitcast(F32), ALU.subtract).then_inc(lo_done, 1)

        def splitter(eng, split):
            at = [0]

            def to(n):
                while at[0] <= min(n, MOE_BASE - 1):
                    split(eng, at[0])
                    at[0] += 1

            return to, at

        FU = FF // 256
        LOOPS = FU // 3
        GU0 = GROUP[("gu", 0, 0)]

        def gu_bank(uu, x):
            return ps[:, (GU0 + 4 * uu + x) % MM_BANKS, 0:T]

        def split_hi_gu(act, i, s):
            r, hi, _ = parts(FFN_BASE + s)
            act.wait_ge(landed[(FFN_BASE + s) % RAW], i * 16 + 16 * ((FFN_BASE + s) // RAW + 1))
            act.wait_ge(mm_done, i * 12 + (GU0 + 2 * (s - SPLIT + 1)))
            nc.scalar.activation(hi, r, ACT.Copy).then_inc(hi_done, 1)

        def split_lo_gu(dve, i, s):
            r, hi, lo = parts(FFN_BASE + s)
            dve.wait_ge(hi_done, i * 6 + (FFN_BASE + s + 1))
            nc.vector.tensor_tensor(lo, r, hi.bitcast(F32), ALU.subtract).then_inc(lo_done, 1)

        @block.scalar
        def _(act):
            split_to, split_at = splitter(act, split_hi_dense)
            step = [0]

            for t, r, m, name, row in PIECES:
                act.dma_start(x_tok[r:r + m, t, :], SRC[name][row:row + m, :]).then_inc(x_landed, 16)
            for l in range(L):
                for at, n, w in ((NG1, 8, norm1_g), (NG2, 8, norm2_g), (PSC, 4, pool_scale), (DWB, 4, conv_dw_b),
                                 (LNG, 4, conv_ln_g), (LNB, 4, conv_ln_b)):
                    act.dma_start(par_rows[32 * l + at:32 * l + at + n, :], w[l].rearrange("(k p) -> k p", p=P)
                                  ).then_inc(par_landed, 16)
                act.dma_start(dw_rows[:, l, :], conv_dw_w[l]).then_inc(par_landed, 16)
            act.dma_start(rw[:], router_w[0].rearrange("(k p) e -> p k e", p=P)).then_inc(rw_landed, 16)

            def x_hi_parts(i, l, which):
                for k in range(KD):
                    if k == 0:
                        act.wait_ge(evac, max(h_group(i, 0), GROUP[("params",)] + 1))
                    act.wait_ge(evac, h_group(i, k))
                    nc.scalar.activation(x_hi[:, k, :], h[:, k, :], ACT.Copy, scale=col(l, which, k)
                                         ).then_inc(x_hi_done, 1)

            def mixer_layer(l):
                b = MIX_BASE[l]
                x_hi_parts(2 * l, l, NG1)
                split_to(b + 2)
                for half in (0, 1):
                    split_to(b + 3 + 2 * half)
                    for i in (0, 1):
                        c = 2 * half + i
                        act.wait_ge(z_scaled, KC * l + c + 1)
                        nc.scalar.activation(z[:, 2 + i, :], z[:, 2 + i, :], ACT.Tanh, scale=0.5
                                             ).then_inc(tanh_done, 1)
                split_to(b + 8)
                for g in range(NG):
                    if g == 0:
                        act.wait_ge(mm_done, GROUP[("win", l, 2 * WIN_ORDER[-1] + 1)] + 1)
                    act.wait_ge(pooled, NG * l + g + 1)
                    nc.scalar.activation(x_hi[:, 4 + g, :], y_pool[:, g, :], ACT.Copy).then_inc(pooled_hi, 1)
                for g in range(NG):
                    act.wait_ge(mm_done, GROUP[("pool", l, g)] + 1)
                    nc.scalar.activation(m_hi[:, g, :], ps[:, GROUP[("pool", l, g)] % MM_BANKS, 0:T], ACT.Copy,
                                         scale=col(l, PSC, g)).then_inc(m_hi_done, 1)
                split_to(b + 9)
                for c in range(KC):
                    act.wait_ge(ln_centred, KC * l + c + 1)
                    nc.scalar.activation(z[:, c, :], y[:, c, :], ACT.Square).then_inc(ln_sq, 1)
                for c in range(KC):
                    act.wait_ge(ln_scaled, KC * l + c + 1)
                    step[0] += 1
                    nc.scalar.activation(z[:, c, :], y[:, c, :], ACT.Silu, scale=col(l, LNG, c), bias=col(l, LNB, c)
                                         ).then_inc(act_step, 1)
                    act.wait_ge(act_step, step[0])
                    nc.scalar.activation(x_hi[:, c, :], z[:, c, :], ACT.Copy).then_inc(ln_act, 1)
                for m in range(KC):
                    act.wait_ge(mm_done, GROUP[("pw", l, m)] + 1)
                    nc.scalar.activation(m_hi[:, NG + m, :], ps[:, GROUP[("pw", l, m)] % MM_BANKS, 0:T], ACT.Copy
                                         ).then_inc(m_hi_done, 1)
                for s in range(4):
                    split_to(b + 10 + s)

            split_to(1)
            mixer_layer(0)

            x_hi_parts(1, 0, NG2)
            act.wait_ge(state_stored, 16 * 5)

            def gate_up(i, uu, split):
                u = i * 3 + uu
                split(2 * uu + 2)
                for x in (0, 1):
                    act.wait_ge(gate_scaled, u * 2 + (x + 1))
                    nc.scalar.activation(gs[:, x, :], gs[:, x, :], ACT.Silu).then_inc(silu_done, 1)
                split(2 * uu + 3)
                for x in (0, 1):
                    act.wait_ge(f_ready, u * 2 + (x + 1))
                    nc.scalar.activation(f_hi[:, ds(u * 2 + x, 1), :], us[:, x:x + 1, :], ACT.Copy
                                         ).then_inc(f_hi_done, 1)

            with act.Fori(0, LOOPS) as i:
                for uu in range(3):
                    gate_up(i, uu, lambda s, i=i: split_hi_gu(act, i, s))
            split_at[0] = FFN_BASE + 6 * LOOPS + 2
            for uu in range(FU - 3 * LOOPS):
                gate_up(LOOPS, uu, lambda s: split_to(FFN_BASE + 6 * LOOPS + s))
            split_to(MIX_BASE[1] + 1)
            mixer_layer(1)

            act.wait_ge(mm_done, N_GROUPS)
            act.wait_ge(state_stored, 16 * 10)

            def token_squares(done):
                for t in range(3):
                    if done is not None:
                        act.wait_ge(comb_read, done(t))
                    nc.scalar.activation(hn[:, t, :], yt[:, t, :], ACT.Square, accum_out=nt[0:TT, t, 3:4]
                                         ).then_inc(fin_sq if done else hn_sq, 1)

            act.wait_ge(evac, N_GROUPS)
            token_squares(None)
            act.wait_ge(gap_done, 1)
            nc.scalar.activation(gt[:, :, 1], gt[:, :, 0], ACT.Exp).then_inc(exp_done, 1)
            for t in range(3):
                act.wait_ge(hn_done, t + 1)
                nc.scalar.activation(hn_hi[:, t, :], hn[:, t, :], ACT.Copy).then_inc(hn_hi_done, 1)

            def gathered_hi(p):
                act.wait_ge(gather_done, p + 1)
                for i, x in enumerate((X0, X1)):
                    nc.scalar.activation(xg_hi[:, 4 * i:4 * i + 4, :], x.rearrange("p (k s) -> p k s", k=4), ACT.Copy
                                         ).then_inc(xg_hi_done, 1)

            def out_hi(p):
                act.wait_ge(d_done, p + 1)
                act.wait_ge(selt_read, p * 2 + 2)
                act.wait_ge(comb_read, p * 6 + 1)
                for i in (0, 1):
                    nc.scalar.activation(o_hi[:, 512 * i:512 * (i + 1)], D_[:, i, :], ACT.Copy, scale=slot_gate[:, 0:1]
                                         ).then_inc(o_hi_done, 1)

            def expert_pass(p):
                def after(i):
                    for j in range(NJ):
                        c = p * NJ + j
                        if i == gate_slot(j) + 1:
                            act.wait_ge(g_done, c + 1)
                            act.wait_ge(e_f, c + 1)
                            nc.scalar.activation(act_s[:], G_, ACT.Silu).then_inc(e_silu, 1)
                        if i == (up_slot(0) + 1 if j == 0 else down_slot(j - 1) + 1):
                            act.wait_ge(t_done, c + 2)
                            nc.scalar.activation(ft_hi[:], T_.rearrange("p (k s) -> p k s", k=4), ACT.Copy
                                                 ).then_inc(ft_hi_done, 1)
                    if i == -1:
                        out_hi(p)

                for i in range(ES):
                    split_hi_pass(act, p, i)
                    if i >= 1:
                        after(i - 2)
                gathered_hi(p + 1)

            gathered_hi(0)
            with act.Fori(0, NE) as p:
                expert_pass(p)
            act.wait_ge(extra_done, 1)
            n_over = act.value_load(eids[0:1, 6:7], min_val=0, max_val=5)
            with act.If(n_over > 0):
                with act.Fori(0, n_over) as i:
                    expert_pass(i + NE)
                act.nop()
            n_pass = n_over + NE
            out_hi(n_pass)
            token_squares(lambda t: n_pass * 6 + (2 * t + 3))

        @block.vector
        def _(dve):
            split_to, split_at = splitter(dve, split_lo_dense)
            step = [0]

            def link(ins):
                step[0] += 1
                ins.then_inc(dve_step, 1)
                dve.wait_ge(dve_step, step[0])

            def bank(name):
                return ps[:, GROUP[name] % MM_BANKS, :]

            def made(name):
                dve.wait_ge(mm_done, GROUP[name] + 1)

            def rsqrt(a, yy, tt):
                link(nc.vector.tensor_scalar(yy.bitcast(I32), a.bitcast(I32), 1, None, ALU.logical_shift_right))
                link(nc.vector.tensor_scalar(yy.bitcast(I32), yy.bitcast(I32), -1.0, RSQRT_SEED, ALU.mult, ALU.add))
                for _ in range(3):
                    link(nc.vector.tensor_tensor(tt, yy, yy, ALU.mult))
                    link(nc.vector.scalar_tensor_tensor(tt, tt, -0.5, a, ALU.mult, ALU.mult))
                    link(nc.vector.scalar_tensor_tensor(yy, tt, 1.5, yy, ALU.add, ALU.mult))

            def rstd_from_sum(name, n, eps):
                dve.wait_ge(sums_done, SUMS[name] + 1)
                link(nc.vector.tensor_scalar(nrm_a[:], SUM_BANK, 1.0 / n, eps, ALU.mult, ALU.add))
                dve.sem_inc(sums_read, 1)
                rsqrt(nrm_a[:], rstd[:], nrm_t[:])

            def x_lo_parts(i, l, which):
                for k in range(KD):
                    dve.wait_ge(x_hi_done, KD * i + k + 1)
                    nc.vector.scalar_tensor_tensor(x_lo[:, k, :], h[:, k, :], col(l, which, k),
                                                   x_hi[:, k, :].bitcast(F32), ALU.mult, ALU.subtract
                                                   ).then_inc(x_lo_done, 1)

            for k in range(KD):
                made(("x", k))
                nc.vector.tensor_copy(h[:, k, :], bank(("x", k))[:, 0:T]).then_inc(evac, 1)
            made(("params",))
            n_par = 64 + L * KC * TAPS
            nc.vector.tensor_copy(params[:], bank(("params",))[:, 0:n_par]).then_inc(evac, 1)
            dve.wait_ge(evac, GROUP[("params",)] + 1)
            dve.wait_ge(rw_landed, 16)
            for k in range(KD):
                nc.vector.tensor_scalar(rwg[:, k, :], rw[:, k, :], col(1, NG2, k), None, ALU.mult).then_inc(rwg_done, 1)

            def mixer_layer(l):
                b = MIX_BASE[l]

                n_conv = [0]

                def conv(tiles, taps):
                    for j in taps:
                        for c in tiles:
                            for src, dst in (
                                    (conv_ext[:, c, j:j + TP], y[:, c, 0:TP]),
                                    (samples(conv_ext[:, c, CSEG:CEXT])[:, :, j:j + DS], samples(y[:, c, TP:T]))):
                                if j == 0:
                                    ins = nc.vector.tensor_scalar(dst, src, tap(l, c, 0), col(l, DWB, c), ALU.mult, ALU.add)
                                else:
                                    dve.wait_ge(conv_step, conv_n[0] - 2 * len(tiles) + 1)
                                    ins = nc.vector.scalar_tensor_tensor(dst, src, tap(l, c, j), dst, ALU.mult, ALU.add)
                                ins.then_inc(conv_step, 1)
                                conv_n[0] += 1

                x_lo_parts(2 * l, l, NG1)
                split_to(b + 3)
                rstd_from_sum(("norm", 2 * l), D, 1e-6)
                for half in (0, 1):
                    s0 = 2 * half
                    split_to(b + s0 + 2)
                    for i in (0, 1):
                        g = ("win", l, 2 * WIN_ORDER[s0] + i)
                        made(g)
                        nc.vector.scalar_tensor_tensor(z[:, i, :], bank(g)[:, 0:T], 0.5, rstd[:], ALU.mult, ALU.mult
                                                       ).then_inc(evac, 1)
                    split_to(b + s0 + 3)
                    for i in (0, 1):
                        g = ("win", l, 2 * WIN_ORDER[s0 + 1] + i)
                        made(g)
                        link(nc.vector.tensor_tensor(z[:, 2 + i, :], bank(g)[:, 0:T], rstd[:], ALU.mult))
                        dve.sem_inc(z_scaled, 1)
                        dve.sem_inc(evac, 1)
                    if half == 0:
                        made(("past_pool", l))
                        nc.vector.tensor_copy(
                            pool_ext[:, :, PSEG:PEXT].rearrange("p g (b t) -> p g b t", b=DB)[:, :, :, 0:PB],
                            bank(("past_pool", l))[:, 0:NG * DB * PB].rearrange("p (g b t) -> p g b t", g=NG, b=DB)
                        ).then_inc(evac, 1)
                        for i in (0, 1):
                            made(("past_conv", l, i))
                            nc.vector.tensor_copy(
                                conv_ext[:, 2 * i:2 * i + 2, CSEG:CEXT].rearrange("p g (b t) -> p g b t", b=DB)[:, :, :, 0:CB],
                                bank(("past_conv", l, i))[:, 0:2 * DB * CB].rearrange("p (g b t) -> p g b t", g=2, b=DB)
                            ).then_inc(evac, 1)
                        if l == 0:
                            dve.wait_ge(ext_zero, 1)
                        dve.wait_ge(ext_zero, l + 1)
                    for i in (0, 1):
                        c = 2 * half + i
                        dve.wait_ge(tanh_done, KC * l + c + 1)
                        nc.vector.scalar_tensor_tensor(conv_ext[:, c, CB:CSEG], z[:, 2 + i, 0:TP], 1.0, z[:, i, 0:TP],
                                                       ALU.add, ALU.mult).then_inc(v_done, 1)
                        nc.vector.scalar_tensor_tensor(samples(conv_ext[:, c, CSEG:CEXT])[:, :, CB:CS1],
                                                       samples(z[:, 2 + i, TP:T]), 1.0, samples(z[:, i, TP:T]),
                                                       ALU.add, ALU.mult).then_inc(v_done, 1)
                    dve.wait_ge(v_done, 8 * l + 4 * (half + 1))
                    dve.wait_ge(evac, GROUP[("past_conv", l, 1)] + 1)
                    if half == 0:
                        conv((0, 1), range(0, 14))
                for s in (4, 5):
                    split_to(b + s + 2)
                    for i in (0, 1):
                        g = 2 * WIN_ORDER[s] + i
                        made(("win", l, g))
                        link(nc.vector.tensor_tensor(pool_ext[:, g, PB:PSEG], bank(("win", l, g))[:, 0:TP],
                                                     rstd[:, 0:TP], ALU.mult))
                        nc.vector.tensor_tensor(samples(pool_ext[:, g, PSEG:PEXT])[:, :, PB:PS1],
                                                samples(bank(("win", l, g))[:, TP:T]), samples(rstd[:, TP:T]),
                                                ALU.mult).then_inc(evac, 1)
                split_to(b + 8)
                conv((0, 1), range(14, TAPS))
                conv((2, 3), range(TAPS))
                dve.wait_ge(conv_step, conv_n[0])
                link(nc.vector.tensor_tensor(z[:, 0, :], y[:, 0, :], y[:, 1, :], ALU.add))
                for c in range(2, KC):
                    link(nc.vector.tensor_tensor(z[:, 0, :], z[:, 0, :], y[:, c, :], ALU.add))
                dve.sem_inc(y_sum, 1)
                for g in range(NG):
                    name = ("pool", l, g)
                    dve.wait_ge(m_hi_done, KD * l + g + 1)
                    nc.vector.scalar_tensor_tensor(m_lo[:, g, :], bank(name)[:, 0:T], col(l, PSC, g),
                                                   m_hi[:, g, :].bitcast(F32), ALU.mult, ALU.subtract).then_inc(evac, 1)
                dve.wait_ge(sums_done, SUMS[("mean", l)] + 1)
                for c in range(KC):
                    nc.vector.scalar_tensor_tensor(y[:, c, :], SUM_BANK, -1.0 / CW, y[:, c, :], ALU.mult, ALU.add
                                                   ).then_inc(ln_centred, 1)
                dve.wait_ge(ln_centred, KC * (l + 1))
                dve.sem_inc(sums_read, 1)
                split_to(b + 9)
                rstd_from_sum(("var", l), CW, 1e-5)
                for c in range(KC):
                    nc.vector.tensor_tensor(y[:, c, :], y[:, c, :], rstd[:], ALU.mult).then_inc(ln_scaled, 1)
                for c in range(KC):
                    dve.wait_ge(ln_act, KC * l + c + 1)
                    nc.vector.tensor_tensor(x_lo[:, c, :], z[:, c, :], x_hi[:, c, :].bitcast(F32), ALU.subtract
                                            ).then_inc(ln_lo, 1)
                for m in range(KC):
                    name = ("pw", l, m)
                    dve.wait_ge(m_hi_done, KD * l + NG + m + 1)
                    nc.vector.tensor_tensor(m_lo[:, NG + m, :], bank(name)[:, 0:T], m_hi[:, NG + m, :].bitcast(F32),
                                            ALU.subtract).then_inc(evac, 1)
                for s in range(4):
                    split_to(b + 10 + s)
                    for i in (0, 1):
                        name = ("wout", l, 2 * s + i)
                        made(name)
                        hh = h[:, 2 * s + i, :]
                        nc.vector.tensor_tensor(hh, hh, bank(name)[:, 0:T], ALU.add).then_inc(evac, 1)
                if l == 1:
                    for t in range(3):
                        for i in (0, 1):
                            made(("htok", t, i))
                            nc.vector.tensor_copy(yt[:, t, 512 * i:512 * (i + 1)], bank(("htok", t, i))[0:TT, :]
                                                  ).then_inc(evac, 1)
                for i, (_, rows) in enumerate(state_dsts(l)):
                    made(("state", l, i))
                    nc.vector.tensor_copy(state_io[0:rows, i, :], bank(("state", l, i))[0:rows, :]).then_inc(evac, 1)

            conv_n = [0]
            split_to(1)
            mixer_layer(0)

            x_lo_parts(1, 0, NG2)
            rstd_from_sum(("norm", 1), D, 1e-6)
            dve.wait_ge(state_stored, 16 * 5)

            def gate_up(i, uu, split):
                u = i * 3 + uu
                split(2 * uu + 2)
                for x in (0, 1):
                    dve.wait_ge(mm_done, u * 4 + (GU0 + x + 1))
                    nc.vector.tensor_tensor(gs[:, x, :], gu_bank(uu, x), rstd[:], ALU.mult).then_inc(gate_scaled, 1)
                dve.wait_ge(gate_scaled, u * 2 + 2)
                dve.sem_inc(evac, 2)
                split(2 * uu + 3)
                for x in (0, 1):
                    dve.wait_ge(mm_done, u * 4 + (GU0 + x + 3))
                    nc.vector.tensor_tensor(us[:, x, :], gu_bank(uu, 2 + x), rstd[:], ALU.mult).then_inc(evac, 1)
                dve.wait_ge(evac, u * 4 + (GU0 + 4))
                for x in (0, 1):
                    dve.wait_ge(silu_done, u * 2 + (x + 1))
                    nc.vector.tensor_tensor(us[:, x, :], us[:, x, :], gs[:, x, :], ALU.mult).then_inc(f_ready, 1)
                for x in (0, 1):
                    dve.wait_ge(f_hi_done, u * 2 + (x + 1))
                    nc.vector.tensor_tensor(f_lo[:, ds(u * 2 + x, 1), :], us[:, x:x + 1, :],
                                            f_hi[:, ds(u * 2 + x, 1), :].bitcast(F32), ALU.subtract
                                            ).then_inc(f_lo_done, 1)

            with dve.Fori(0, LOOPS) as i:
                for uu in range(3):
                    gate_up(i, uu, lambda s, i=i: split_lo_gu(dve, i, s))
            split_at[0] = FFN_BASE + 6 * LOOPS + 2
            for uu in range(FU - 3 * LOOPS):
                gate_up(LOOPS, uu, lambda s: split_to(FFN_BASE + 6 * LOOPS + s))
            n = DOWN_BASE
            for c, ks in enumerate(DOWN_PARTS):
                for _ in ks:
                    split_to(n + 2)
                    n += 1
                for i in (0, 1):
                    name = ("down", 2 * c + i)
                    made(name)
                    hh = h[:, 2 * c + i, :]
                    nc.vector.tensor_tensor(hh, hh, bank(name)[:, 0:T], ALU.add).then_inc(evac, 1)
            mixer_layer(1)

            dve.wait_ge(state_stored, 16 * 10)
            dve.wait_ge(evac, N_GROUPS)
            link(nc.vector.memset(sel_t[:].bitcast(F32), 0.0))
            link(nc.vector.memset(slot_gate[:], 0.0))
            dve.sem_inc(selt_read, 2)
            nc.vector.memset(D_, 0.0).then_inc(d_done, 1)
            for s in (e_silu, e_f, t_done, ft_lo_done, comb_read):
                dve.sem_inc(s, 1)

            def rstd_tokens():
                link(nc.vector.tensor_scalar(nt[0:TT, :, 0], nt[0:TT, :, 3], 1.0 / D, 1e-6, ALU.mult, ALU.add))
                rsqrt(nt[0:TT, :, 0], nt[0:TT, :, 1], nt[0:TT, :, 2])

            dve.wait_ge(hn_sq, 3)
            rstd_tokens()
            dve.wait_ge(logits_done, 1)
            for t in range(3):
                link(nc.vector.tensor_scalar(lg[:, t, :], ps[0:TT, 6, NE * t:NE * (t + 1)], nt[0:TT, t, 1:2], None, ALU.mult))
            for t in range(3):
                link(nc.vector.max(out=top[:, t, :], in_=lg[:, t, :]))
                link(nc.vector.max_index(out=top_i[:, t, :], in_max=top[:, t, :], in_values=lg[:, t, :]))
            link(nc.vector.tensor_copy(top_f[:], top_i[:, :, 0:2]))
            nc.vector.tensor_tensor(gt[:, :, 0], top[:, :, 1], top[:, :, 0], ALU.subtract).then_inc(gap_done, 1)
            for t in range(3):
                link(nc.vector.tensor_scalar(hot1[:, t, :], iota_e[0:TT], top_f[:, t, 0:1], None, ALU.is_equal))
                link(nc.vector.tensor_scalar(hot2[:, t, :], iota_e[0:TT], top_f[:, t, 1:2], None, ALU.is_equal))
            nc.vector.tensor_tensor(hot[:], hot1[:], hot2[:], ALU.add).then_inc(hot_done, 1)
            dve.wait_ge(hot_done, 1)
            dve.wait_ge(exp_done, 1)
            link(nc.vector.tensor_scalar(gt[:, :, 2], gt[:, :, 1], 1.0, None, ALU.add))
            link(nc.vector.reciprocal(gt[:, :, 2], gt[:, :, 2]))
            link(nc.vector.tensor_tensor(gt[:, :, 3], gt[:, :, 1], gt[:, :, 2], ALU.mult))
            for t in range(3):
                link(nc.vector.tensor_scalar(gates[:, t, 0, :], hot1[:, t, :], gt[:, t, 2:3], None, ALU.mult))
                link(nc.vector.scalar_tensor_tensor(gates[:, t, 0, :], hot2[:, t, :], gt[:, t, 3:4], gates[:, t, 0, :],
                                                    ALU.mult, ALU.add))
            link(nc.vector.tensor_copy(gates[:, :, 1, :], gates[:, :, 0, :]))
            link(nc.vector.tensor_copy(GT[:, :, 0:NE], gates[:, :, 0, :]))
            dve.wait_ge(ranks_done, 1)
            for t in range(3):
                link(nc.vector.scalar_tensor_tensor(posm[:, t, :], ps[0:TT, 7, NE * t:NE * (t + 1)], 1.0, hot[:, t, :],
                                                    ALU.add, ALU.mult))
            link(nc.vector.tensor_copy(cnt[:], ps[:, 7, 3 * NE:4 * NE]))
            link(nc.vector.tensor_scalar(posm[:], posm[:], -1.0, None, ALU.add))
            link(nc.vector.tensor_copy(POS[:, :, 0:NE], posm[:]))
            dve.sem_inc(routed, 1)

            def select(p):
                for t in range(3):
                    nc.vector.tensor_scalar(sel[:, t, :], iota_slot[0:TT, :], POS[:, t, ds(p, 1)], None, ALU.is_equal
                                            ).then_inc(sel_ready, 1)

            select(0)
            dve.wait_ge(gb_landed, 32)
            for t in range(3):
                nc.vector.scalar_tensor_tensor(hn[:, t, :], yt[:, t, :], nt[0:TT, t, 1:2], gb[:, 0, :], ALU.mult, ALU.mult
                                               ).then_inc(hn_done, 1)
            for t in range(3):
                dve.wait_ge(hn_hi_done, t + 1)
                nc.vector.tensor_tensor(hn_lo[:, t, :], hn[:, t, :], hn_hi[:, t, :].bitcast(F32), ALU.subtract
                                        ).then_inc(hn_lo_done, 1)

            def gathered_lo(p):
                for i, x in enumerate((X0, X1)):
                    dve.wait_ge(xg_hi_done, p * 2 + (i + 1))
                    nc.vector.tensor_tensor(xg_lo[:, 4 * i:4 * i + 4, :], x.rearrange("p (k s) -> p k s", k=4),
                                            xg_hi[:, 4 * i:4 * i + 4, :].bitcast(F32), ALU.subtract).then_inc(xg_lo_done, 1)

            def out_lo(p):
                for i in (0, 1):
                    dve.wait_ge(o_hi_done, p * 2 + (i + 1))
                    cols = slice(512 * i, 512 * (i + 1))
                    nc.vector.scalar_tensor_tensor(o_lo[:, cols], D_[:, i, :], slot_gate[:, 0:1],
                                                   o_hi[:, cols].bitcast(F32), ALU.mult, ALU.subtract).then_inc(o_lo_done, 1)

            def add_outputs(p):
                for i in range(6):
                    t, half = divmod(i, 2)
                    dve.wait_ge(comb_done, p * 6 + (i + 1))
                    cols = yt[:, t, 512 * half:512 * (half + 1)]
                    nc.vector.tensor_tensor(cols, cols, (X0, X1, X2)[i % 3][0:TT, :], ALU.add).then_inc(comb_read, 1)

            def expert_pass(p):
                def after(i):
                    for j in range(NJ):
                        c = p * NJ + j
                        if i == up_slot(j) + 1:
                            dve.wait_ge(u_done, c + 1)
                            dve.wait_ge(e_silu, c + 2)
                            dve.wait_ge(t_done, c + 1)
                            nc.vector.tensor_tensor(act_f[:], act_s[:], U_, ALU.mult).then_inc(e_f, 1)
                        if i == (up_slot(0) + 1 if j == 0 else down_slot(j - 1) + 1):
                            if j == 0:
                                add_outputs(p)
                            dve.wait_ge(ft_hi_done, c + 1)
                            nc.vector.tensor_tensor(ft_lo[:], T_.rearrange("p (k s) -> p k s", k=4),
                                                    ft_hi[:].bitcast(F32), ALU.subtract).then_inc(ft_lo_done, 1)
                    if i == -1:
                        out_lo(p)
                    if i == up_slot(3) + 1:
                        dve.wait_ge(selt_done, p + 1)
                        nc.vector.tensor_copy(sel_t[:], X0[:, 0:T]).then_inc(selt_read, 1)
                        nc.vector.tensor_copy(slot_gate[:], X1[:, 0:1]).then_inc(selt_read, 1)
                    if i == up_slot(4) + 1:
                        dve.wait_ge(extra_done, 1)
                        select(p + 1)

                for i in range(ES):
                    split_lo_pass(dve, p, i)
                    if i >= 1:
                        after(i - 2)
                gathered_lo(p + 1)

            gathered_lo(0)
            with dve.Fori(0, NE) as p:
                expert_pass(p)
            n_over = dve.value_load(eids[0:1, 6:7], min_val=0, max_val=5)
            with dve.If(n_over > 0):
                with dve.Fori(0, n_over) as i:
                    expert_pass(i + NE)
                dve.nop()
            n_pass = n_over + NE
            out_lo(n_pass)
            add_outputs(n_pass)
            dve.wait_ge(fin_sq, 3)
            rstd_tokens()
            for t in range(3):
                nc.vector.scalar_tensor_tensor(yt[:, t, :], yt[:, t, :], nt[0:TT, t, 1:2], gb[:, 1, :], ALU.mult, ALU.mult
                                               ).then_inc(fin_out, 1)

        @block.tensor
        def _(pe):
            def bank(name):
                return ps[:, GROUP[name] % MM_BANKS, :]

            def group(name):
                q = GROUP[name]
                if q >= MM_BANKS:
                    pe.wait_ge(evac, q - MM_BANKS + 1)
                return ps[:, q % MM_BANKS, :]

            def mm3(out, a_hi, a_lo, b_hi, b_lo, start, stop):
                nc.tensor.matmul(out, a_hi, b_hi, start=start, stop=False)
                nc.tensor.matmul(out, a_hi, b_lo, start=False, stop=False)
                return nc.tensor.matmul(out, a_lo, b_hi, start=False, stop=stop)

            def dense_slot(n, ncol):
                size = slot_size(n)
                _, hi, lo = parts(n, size)
                return (x.rearrange("p (k n) -> p k n", n=ncol) for x in (hi, lo))

            def sums(name, rhs, ready, count):
                i = SUMS[name]
                pe.wait_ge(ready, count)
                if i:
                    pe.wait_ge(sums_read, i)
                nc.tensor.matmul(SUM_BANK, ones[:], rhs, start=True, stop=True).then_inc(sums_done, 1)

            pe.wait_ge(consts, 1)
            pe.wait_ge(x_landed, 16 * len(PIECES))
            for k in range(KD):
                out = group(("x", k))
                for t in range(3):
                    ins = nc.tensor.transpose(out[:, TT * t:TT * (t + 1)], x_tok[:, t, P * k:P * (k + 1)], ident[0:TT, 0:TT])
                ins.then_inc(mm_done, 1)
            pe.wait_ge(par_landed, 16 * 7 * L)
            out = group(("params",))
            nc.tensor.transpose(out[:, 0:64], par_rows[:], ident[0:64, 0:64])
            for l in range(L):
                for c in range(KC):
                    o = 64 + (l * KC + c) * TAPS
                    ins = nc.tensor.transpose(out[:, o:o + TAPS], dw_rows[:, l, P * c:P * (c + 1)], ident[0:TAPS, 0:TAPS])
            ins.then_inc(mm_done, 1)

            def project(name_of, n, i, ncol, k_ready):
                out = group(name_of)
                hi, lo = dense_slot(n, ncol)
                nk = slot_size(n) // ncol
                for k in range(nk):
                    if k_ready:
                        k_ready(k)
                    cols = slice(P * i, P * (i + 1))
                    ins = mm3(out[:, 0:T], hi[:, k, cols], lo[:, k, cols], x_hi[:, k, :], x_lo[:, k, :],
                              k == 0, k == nk - 1)
                ins.then_inc(mm_done, 1)

            def split_ready(n):
                pe.wait_ge(lo_done, n + 1)

            def mixer_layer(l):
                b = MIX_BASE[l]

                def w_in_slot(s):
                    split_ready(b + s)
                    for i in (0, 1):
                        ready = (lambda k: pe.wait_ge(x_lo_done, KD * 2 * l + k + 1)) if s == 0 and i == 0 else None
                        project(("win", l, 2 * WIN_ORDER[s] + i), b + s, i, 256, ready)

                w_in_slot(0)
                w_in_slot(1)
                sums(("norm", 2 * l), sqs[:], sq_ready, 2 * l + 1)
                pe.wait_ge(past_landed, 16 * 3 * (l + 1))
                n_rows = DB * PB
                out = group(("past_pool", l))
                for g in range(NG):
                    ins = nc.tensor.transpose(out[:, n_rows * g:n_rows * (g + 1)], state_io[:, 0, P * g:P * (g + 1)],
                                              ident[0:n_rows, 0:n_rows])
                ins.then_inc(mm_done, 1)
                for i in (0, 1):
                    out = group(("past_conv", l, i))
                    for c in (0, 1):
                        for hb in (0, 1):
                            at = n_rows * (2 * c + hb)
                            ins = nc.tensor.transpose(out[:, at:at + n_rows],
                                                      state_io[:, 1 + hb, P * (2 * i + c):P * (2 * i + c + 1)],
                                                      ident[0:n_rows, 0:n_rows])
                    ins.then_inc(mm_done, 1)
                for s in range(2, 6):
                    w_in_slot(s)
                split_ready(b + 6)
                for g in range(NG):
                    out = group(("pool", l, g))
                    hi, lo = dense_slot(b + 6, P)
                    pe.wait_ge(pooled_lo, NG * l + g + 1)
                    mm3(out[:, 0:T], hi[:, g, :], lo[:, g, :], x_hi[:, 4 + g, :], x_lo[:, 4 + g, :], True, True
                        ).then_inc(mm_done, 1)
                sums(("mean", l), z[:, 0, :], y_sum, l + 1)
                sums(("var", l), z[:, 0, :], ln_sqsum, l + 1)
                split_ready(b + 7)
                for m in range(KC):
                    ready = (lambda k: pe.wait_ge(ln_lo, KC * l + k + 1)) if m == 0 else None
                    project(("pw", l, m), b + 7, m, CW, ready)
                pe.wait_ge(evac, GROUP[("pw", l, KC - 1)] + 1)
                for s in range(4):
                    split_ready(b + 8 + s)
                    hi, lo = dense_slot(b + 8 + s, 256)
                    for i in (0, 1):
                        out = group(("wout", l, 2 * s + i))
                        for k in range(KD):
                            cols = slice(P * i, P * (i + 1))
                            ins = mm3(out[:, 0:T], hi[:, k, cols], lo[:, k, cols], m_hi[:, k, :], m_lo[:, k, :],
                                      k == 0, k == KD - 1)
                        ins.then_inc(mm_done, 1)
                if l == 1:
                    pe.wait_ge(evac, GROUP[("wout", 1, KD - 1)] + 1)
                    for t in range(3):
                        for i in (0, 1):
                            out = group(("htok", t, i))
                            for k in range(4):
                                ins = nc.tensor.transpose(out[0:TT, P * k:P * (k + 1)],
                                                          h[:, 4 * i + k, TT * t:TT * (t + 1)], ident[:])
                            ins.then_inc(mm_done, 1)
                    pe.wait_ge(rwg_done, KD)
                    pe.wait_ge(sums_read, SUMS[("var", 1)] + 1)
                    for t in range(3):
                        for k in range(KD):
                            ins = nc.tensor.matmul(ps[0:TT, 6, NE * t:NE * (t + 1)], h[:, k, TT * t:TT * (t + 1)],
                                                   rwg[:, k, :], start=(k == 0), stop=(k == KD - 1))
                    ins.then_inc(logits_done, 1)
                pe.wait_ge(packed, l + 1)
                srcs = [lambda g: z[:, g, 0:DB * PB],
                        lambda g: y[:, g, 0:HB * CB],
                        lambda g: y[:, g, HB * CB:DB * CB],
                        lambda g: pool_ext[:, g, PSEG - PB:PSEG],
                        lambda g: conv_ext[:, g, CSEG - CB:CSEG]]
                for i, (_, rows) in enumerate(state_dsts(l)):
                    out = group(("state", l, i))
                    for g in range(NG):
                        ins = nc.tensor.transpose(out[0:rows, P * g:P * (g + 1)], srcs[i](g), ident[:])
                    ins.then_inc(mm_done, 1)

            mixer_layer(0)

            sums(("norm", 1), sqs[:], sq_ready, 2)
            pe.wait_ge(x_lo_done, KD * 2)

            def gate_up(i, uu):
                u = i * 3 + uu
                for s in (0, 1):
                    pe.wait_ge(lo_done, u * 2 + (FFN_BASE + s + 1))
                    hi, lo = dense_slot(FFN_BASE + 2 * uu + s, 256)
                    for x in (0, 1):
                        pe.wait_ge(evac, u * 4 + (GU0 + 2 * s + x - MM_BANKS + 1))
                        for k in range(KD):
                            cols = slice(P * x, P * (x + 1))
                            ins = mm3(gu_bank(uu, 2 * s + x), hi[:, k, cols], lo[:, k, cols], x_hi[:, k, :], x_lo[:, k, :],
                                      k == 0, k == KD - 1)
                        ins.then_inc(mm_done, 1)

            with pe.Fori(0, LOOPS) as i:
                for uu in range(3):
                    gate_up(i, uu)
            for uu in range(FU - 3 * LOOPS):
                gate_up(LOOPS, uu)
            n = DOWN_BASE
            for c, ks in enumerate(DOWN_PARTS):
                outs = [group(("down", 2 * c + i)) for i in (0, 1)]
                k0 = 0
                for part, nk in enumerate(ks):
                    split_ready(n)
                    hi, lo = dense_slot(n, 256)
                    pe.wait_ge(f_lo_done, min(k0 + nk, NFT))
                    for i in (0, 1):
                        for k in range(nk):
                            cols = slice(P * i, P * (i + 1))
                            ins = mm3(outs[i][:, 0:T], hi[:, k, cols], lo[:, k, cols], f_hi[:, k0 + k, :], f_lo[:, k0 + k, :],
                                      k0 + k == 0, k0 + k == NFT - 1)
                        if part == len(ks) - 1:
                            ins.then_inc(mm_done, 1)
                    if part < len(ks) - 1:
                        ins.then_inc(w_used, 1)
                    k0 += nk
                    n += 1
            mixer_layer(1)

            pe.wait_ge(hot_done, 1)
            for t in range(3):
                for u in range(t + 1):
                    nc.tensor.matmul(ps[0:TT, 7, NE * t:NE * (t + 1)], (before if u == t else ones)[0:TT, 0:TT],
                                     hot[:, u, :], start=(u == 0), stop=(u == t))
            for u in range(3):
                ins = nc.tensor.matmul(ps[:, 7, 3 * NE:4 * NE], ones[0:TT, :], hot[:, u, :], start=(u == 0), stop=(u == 2))
            ins.then_inc(ranks_done, 1)

            def gather(p):
                pe.wait_ge(sel_ready, p * 3 + 3)
                for m in range(KD):
                    for t in range(3):
                        for src in (hn_hi, hn_lo):
                            ins = nc.tensor.matmul((X0, X1)[m // 4][:, P * (m % 4):P * (m % 4 + 1)],
                                                   src[:, t, P * m:P * (m + 1)], sel[:, t, :],
                                                   start=(t == 0 and src is hn_hi), stop=(t == 2 and src is hn_lo))
                ins.then_inc(gather_done, 1)

            def combine(p):
                pe.wait_ge(o_lo_done, p * 2 + 2)
                pe.wait_ge(selt_read, p * 2 + 2)
                for i in range(6):
                    t, half = divmod(i, 2)
                    pe.wait_ge(comb_read, p * 6 + max(i - 1, 1))
                    for o in (o_hi, o_lo):
                        ins = nc.tensor.matmul((X0, X1, X2)[i % 3][0:TT, :], sel_t[:, TT * t:TT * (t + 1)],
                                               o[:, 512 * half:512 * (half + 1)], start=(o is o_hi), stop=(o is o_lo))
                    ins.then_inc(comb_done, 1)

            def expert_pass(p):
                def hidden(j, slot0, out, done):
                    for half in (0, 1):
                        i = slot0 + half
                        pe.wait_ge(lo_done, p * ES + (MOE_BASE + i + 1))
                        _, hi, lo = (x.rearrange("p (k n) -> p k n", k=4) for x in parts(i))
                        for k in range(4):
                            kk = 4 * half + k
                            ins = mm3(out, xg_hi[:, kk, :], xg_lo[:, kk, :], hi[:, k, :], lo[:, k, :], kk == 0, kk == 7)
                        ins.then_inc(done if half else w_used, 1)

                def down(j):
                    pe.wait_ge(ft_lo_done, p * NJ + (j + 2))
                    if j == 0:
                        pe.wait_ge(o_lo_done, p * 2 + 2)
                    for half in (0, 1):
                        i = down_slot(j) + half
                        pe.wait_ge(lo_done, p * ES + (MOE_BASE + i + 1))
                        _, hi, lo = (x.rearrange("p (k n) -> p k n", k=2) for x in parts(i))
                        for k in range(2):
                            for d in (0, 1):
                                cols = slice(512 * d, 512 * (d + 1))
                                kk = 2 * half + k
                                ins = mm3(D_[:, d, :], ft_hi[:, kk, :], ft_lo[:, kk, :], hi[:, k, cols], lo[:, k, cols],
                                          j == 0 and kk == 0, j == NJ - 1 and kk == 3)
                        ins.then_inc(d_done if j == NJ - 1 and half else w_used, 1)

                pe.wait_ge(xg_lo_done, p * 2 + 2)
                for j in range(NJ):
                    c = p * NJ + j
                    pe.wait_ge(e_silu, c + 1)
                    hidden(j, gate_slot(j), G_, g_done)
                    pe.wait_ge(e_f, c + 1)
                    hidden(j, up_slot(j), U_, u_done)
                    if j:
                        down(j - 1)
                    else:
                        combine(p)
                    pe.wait_ge(e_f, c + 2)
                    pe.wait_ge(ft_lo_done, c + 1)
                    for k in range(4):
                        ins = nc.tensor.transpose(T_[:, P * k:P * (k + 1)], act_f[:, P * k:P * (k + 1)], ident[:])
                    ins.then_inc(t_done, 1)
                    if j == 3:
                        pe.wait_ge(comb_read, p * 6 + 7)
                        for t in range(3):
                            nc.tensor.transpose(X0[:, TT * t:TT * (t + 1)], sel[:, t, :].bitcast(F32), ident[0:TT, 0:TT])
                        for t in range(3):
                            ins = nc.tensor.matmul(X1[:, 0:1], sel[:, t, :].bitcast(F32), GT[:, t, ds(p, 1)],
                                                   start=(t == 0), stop=(t == 2))
                        ins.then_inc(selt_done, 1)
                pe.wait_ge(selt_read, p * 2 + 4)
                gather(p + 1)
                down(NJ - 1)

            pe.wait_ge(routed, 1)
            pe.wait_ge(hn_lo_done, 3)
            gather(0)
            with pe.Fori(0, NE) as p:
                expert_pass(p)
            pe.wait_ge(extra_done, 1)
            n_over = pe.value_load(eids[0:1, 6:7], min_val=0, max_val=5)
            with pe.If(n_over > 0):
                with pe.Fori(0, n_over) as i:
                    expert_pass(i + NE)
                pe.nop()
            combine(n_over + NE)


_INS = ['x_prompt', 'x_sample', 'state_pool', 'state_conv', 'meta_tokens', 'norm1_g', 'w_in', 'pool_w', 'pool_scale',
        'conv_dw_w', 'conv_dw_b', 'conv_ln_g', 'conv_ln_b', 'conv_pw_w', 'w_out', 'norm2_g', 'ffn_w_gate', 'ffn_w_up',
        'ffn_w_down', 'router_w', 'moe_w_gate', 'moe_w_up', 'moe_w_down', 'final_norm_g']


def kernel(**inputs):
    import numpy as _np
    import concourse.bacc as _bacc
    from concourse import mybir as _mybir
    from concourse.bass_utils import run_bass_kernel_spmd as _run

    nc = _bacc.Bacc("TRN2", target_bir_lowering=False, num_devices=1)
    arrays, args = {}, []
    for name in _INS:
        a = _np.ascontiguousarray(inputs[name])
        arrays[f"in_{name}_dram"] = a
        args.append(nc.dram_tensor(f"in_{name}_dram", a.shape, _mybir.dt.from_np(a.dtype), kind="ExternalInput").ap())
    layers, prompts = inputs["w_in"].shape[0], inputs["x_prompt"].shape[0]
    pool_state, conv_state = inputs["state_pool"].shape, inputs["state_conv"].shape
    outs = [inputs["x_prompt"].shape, inputs["x_sample"].shape,
            (layers, prompts) + tuple(pool_state[2:]), (layers, prompts) + tuple(conv_state[2:]),
            pool_state, conv_state]
    for i, shape in enumerate(outs):
        args.append(nc.dram_tensor(f"out_{i}_dram", tuple(shape), _mybir.dt.float32, kind="ExternalOutput").ap())
    hybrid_trunk(nc, *args)
    r = _run(nc, [arrays], core_ids=[0])
    return tuple(r.results[0][f"out_{i}_dram"] for i in range(len(outs)))
```

```python
from contextlib import ExitStack

import concourse.bass as bass
from concourse import mybir

F32 = mybir.dt.float32
F32R = mybir.dt.float32r
I32 = mybir.dt.int32
U32 = mybir.dt.uint32
ALU = mybir.AluOpType
ACT = mybir.ActivationFunctionType
AX_X = mybir.AxisListType.X
ds = bass.ds

P = 128
MM_BANKS = 6
RAW = 6
SPLIT = 3
SLOT = 2048
RSQRT_SEED = float(0x5F3759DF)


def hybrid_trunk(nc, x_prompt, x_sample, state_pool, state_conv, meta_tokens, norm1_g, w_in, pool_w,
                 pool_scale, conv_dw_w, conv_dw_b, conv_ln_g, conv_ln_b, conv_pw_w, w_out, norm2_g,
                 ffn_w_gate, ffn_w_up, ffn_w_down, router_w, moe_w_gate, moe_w_up, moe_w_down,
                 final_norm_g, y_prompt, y_sample, pool_p, conv_p, pool_s, conv_s):
    D = x_prompt.shape[2]
    SEQ, META = x_prompt.shape[1], meta_tokens.shape[0]
    DB, DS = x_sample.shape[0], x_sample.shape[1]
    L = w_in.shape[0]
    PW = state_pool.shape[3]
    CW = state_conv.shape[3]
    PB, CB = state_pool.shape[2], state_conv.shape[2]
    TAPS = conv_dw_w.shape[1]
    FF = ffn_w_gate.shape[2]
    NE = router_w.shape[2]
    EF = moe_w_gate.shape[3]
    KD = D // P
    TP = META + SEQ
    T = TP + DB * DS
    TT = T // 3
    KC = CW // P
    NG = PW // P
    NFT = FF // P
    WINDOWS = [2 << g for g in range(NG)]
    assert (L, KD, KC, NG, T % 3) == (2, 8, 4, 4, 0) and TT <= P
    PSEG, CSEG = PB + TP, CB + TP
    PS1, CS1 = PB + DS, CB + DS
    PEXT, CEXT = PSEG + DB * PS1, CSEG + DB * CS1
    HB = DB // 2

    WIN_ORDER = [2, 4, 3, 5, 0, 1]
    PE_TILES, DVE_TILES = (0, 2), (1, 3)
    DIAG_TAPS = SLOT // P
    DIAG_PARTS = [(0, DIAG_TAPS), (DIAG_TAPS, TAPS)]
    S_DIAG, S_POOL_W, S_PW, S_OUT = 6, 10, 11, 12
    MIX_SLOTS = 16
    DOWN_PARTS = [[6, 6, 5, 5], [6, 6, 5, 5], [8, 8, 6], [8, 8, 6]]
    FFN_BASE = MIX_SLOTS
    N_GU = 2 * (FF // 256)
    DOWN_BASE = FFN_BASE + N_GU
    MIX_BASE = [0, DOWN_BASE + sum(len(x) for x in DOWN_PARTS)]
    MOE_BASE = MIX_BASE[1] + MIX_SLOTS
    NJ = EF // 512
    ES = 6 * NJ
    assert ES % RAW == 0
    NSEL = NE + 6

    def gate_slot(j):
        return 0 if j == 0 else 6 * j - 2

    def up_slot(j):
        return gate_slot(j) + 2

    def down_slot(j):
        return 6 * j + 8 if j < NJ - 1 else 6 * j + 4

    GROUP = {}

    def plan(*names):
        for name in names:
            GROUP[name] = len(GROUP)

    plan(*[("x", k) for k in range(KD)], ("params",))
    for l in range(L):
        plan(*[("win", l, 2 * s + i) for s in WIN_ORDER[:2] for i in (0, 1)])
        plan(("past_pool", l), ("past_conv", l, 0), ("past_conv", l, 1))
        plan(*[("win", l, 2 * s + i) for s in WIN_ORDER[2:] for i in (0, 1)])
        plan(*[("conv", l, c) for c in PE_TILES])
        plan(*[("pool", l, g) for g in range(NG)], *[("pw", l, m) for m in range(KC)])
        plan(*[("wout", l, m) for m in range(KD)])
        if l == 1:
            plan(*[("htok", t, i) for t in range(3) for i in (0, 1)])
        plan(*[("state", l, i) for i in range(5)])
        if l == 0:
            plan(*[("gu", u, i) for u in range(FF // 256) for i in range(4)])
            plan(*[("down", m) for m in range(KD)])
    N_GROUPS = len(GROUP)

    with ExitStack() as ctx:
        def sem(name):
            return ctx.enter_context(nc.semaphore(name))

        def sb(name, shape, dt=F32, at=ctx):
            return at.enter_context(nc.sbuf_tensor(name, shape, dt))

        raw = sb("raw", [P, RAW, SLOT])
        w_hi = sb("w_hi", [P, SPLIT, SLOT], F32R)
        w_lo = sb("w_lo", [P, SPLIT, SLOT], F32R)
        h = sb("h", [P, KD, T])
        ident = sb("ident", [P, P])
        ones = sb("ones", [P, P])
        before = sb("before", [P, P])
        iota_slot = sb("iota_slot", [P, P])
        iota_e = sb("iota_e", [P, NE])
        inv_cnt = sb("inv_cnt", [P, 16])
        state_io = sb("state_io", [DB * PB, 5, 512])
        params = sb("params", [P, 64 + L * KC * TAPS])
        rw = sb("rw", [P, KD, NE])
        rwg = sb("rwg", [P, KD, NE])
        nt = sb("nt", [P, 3, 4])
        NG1, NG2, PSC, DWB, LNG, LNB = 0, 8, 16, 20, 24, 28

        def col(l, which, k):
            c = 32 * l + which + k
            return params[:, c:c + 1]

        def tap(l, c, j):
            at = 64 + (l * KC + c) * TAPS + j
            return params[:, at:at + 1]

        dense = ExitStack()
        x_hi = sb("x_hi", [P, KD, T], F32R, dense)
        x_lo = sb("x_lo", [P, KD, T], F32R, dense)
        rstd = sb("rstd", [P, T], F32, dense)
        scratch = sb("scratch", [P, 4, T], F32, dense)
        nrm_a, nrm_t = scratch[:, 0, :], scratch[:, 1, :]
        sqs, sq = scratch[:, 2, :], scratch[:, 3, :]
        mixer = ExitStack()
        m_hi = sb("m_hi", [P, KD, T], F32R, mixer)
        m_lo = sb("m_lo", [P, KD, T], F32R, mixer)
        pool_ext = sb("pool_ext", [P, NG, PEXT], F32, mixer)
        win_sum = sb("win_sum", [P, 2, PEXT], F32, mixer)
        conv_ext = sb("conv_ext", [P, KC, CEXT], F32, mixer)
        y = sb("y", [P, KC, T], F32, mixer)
        z = sb("z", [P, 4, T], F32, mixer)
        y_pool = sb("y_pool", [P, NG, T], F32, mixer)
        mixer.close()
        e_hi = m_hi[:, KC:, :].rearrange("p k t -> p (k t)")[:, 0:2 * CEXT].rearrange("p (c t) -> p c t", c=2)
        e_lo = m_lo[:, KC:, :].rearrange("p k t -> p (k t)")[:, 0:2 * CEXT].rearrange("p (c t) -> p c t", c=2)
        ffn = ExitStack()
        f_hi = sb("f_hi", [P, NFT, T], F32R, ffn)
        f_lo = sb("f_lo", [P, NFT, T], F32R, ffn)
        gs, us = scratch[:, 0:2, :], scratch[:, 2:4, :]
        ffn.close()
        first = ExitStack()
        x_tok = sb("x_tok", [TT, 3, D], F32, first)
        par_rows = sb("par_rows", [64, P], F32, first)
        dw_rows = sb("dw_rows", [TAPS, L, CW], F32, first)
        first.close()
        dense.close()
        moe = ctx
        hn = sb("hn", [TT, 3, D], F32, moe)
        yt = sb("yt", [TT, 3, D], F32, moe)
        gb = sb("gb", [TT, 2, D], F32, moe)
        hn_hi = sb("hn_hi", [TT, 3, D], F32R, moe)
        hn_lo = sb("hn_lo", [TT, 3, D], F32R, moe)
        xg_hi = sb("xg_hi", [P, KD, P], F32R, moe)
        xg_lo = sb("xg_lo", [P, KD, P], F32R, moe)
        act_s = sb("act_s", [P, 512], F32, moe)
        act_f = sb("act_f", [P, 512], F32, moe)
        ft_hi = sb("ft_hi", [P, 4, P], F32R, moe)
        ft_lo = sb("ft_lo", [P, 4, P], F32R, moe)
        o_hi = sb("o_hi", [P, D], F32R, moe)
        o_lo = sb("o_lo", [P, D], F32R, moe)
        sel = sb("sel", [TT, 3, P], F32R, moe)
        sel_t = sb("sel_t", [P, T], F32R, moe)
        slot_gate = sb("slot_gate", [P, 1], F32, moe)
        lg = sb("lg", [TT, 3, NE], F32, moe)
        top = sb("top", [TT, 3, 8], F32, moe)
        top_i = sb("top_i", [TT, 3, 8], U32, moe)
        top_f = sb("top_f", [TT, 3, 2], F32, moe)
        gt = sb("gt", [TT, 3, 4], F32, moe)
        hot1 = sb("hot1", [TT, 3, NE], F32, moe)
        hot2 = sb("hot2", [TT, 3, NE], F32, moe)
        hot = sb("hot", [TT, 3, NE], F32, moe)
        gates = sb("gates", [TT, 3, 2, NE], F32, moe)
        posm = sb("posm", [TT, 3, NE], F32, moe)
        posc = sb("posc", [TT, 3, 2, NE], F32, moe)
        POS = sb("POS", [TT, 3, NSEL], F32, moe)
        GT = sb("GT", [TT, 3, NSEL], F32, moe)
        cnt = sb("cnt", [P, NE], F32, moe)
        over = sb("over", [P, 2, NE], F32, moe)
        n_chunks = sb("n_chunks", [P, NE], F32, moe)
        key = sb("key", [P, 2, NE], F32, moe)
        pick = sb("pick", [P, 6, 2 * NE], F32, moe)
        prod = sb("prod", [P, 6, 2 * NE], F32, moe)
        key_sum = sb("key_sum", [P, 1], F32, moe)
        prod3 = sb("prod3", [TT, 3, 2 * NE], F32, moe)
        eids_f = sb("eids_f", [P, 8], F32, moe)
        eids = sb("eids", [P, 8], I32, moe)

        ps = ctx.enter_context(nc.psum_tensor("ps", [P, 8, 512], F32))
        SUM_BANK = ps[:, 6, 0:T]
        G_, U_, T_, X0, X1, X2 = (ps[:, i, :] for i in (0, 1, 2, 5, 6, 7))
        D_ = ps[:, 3:5, :]

        landed = [sem(f"landed{i}") for i in range(RAW)]
        hi_done, lo_done, w_used = sem("hi_done"), sem("lo_done"), sem("w_used")
        mm_done, evac = sem("mm_done"), sem("evac")
        consts = sem("consts")
        x_landed, par_landed, past_landed = sem("x_landed"), sem("par_landed"), sem("past_landed")
        x_hi_done, x_lo_done = sem("x_hi_done"), sem("x_lo_done")
        sq_ready, sums_done, sums_read = sem("sq_ready"), sem("sums_done"), sem("sums_read")
        ext_zero = sem("ext_zero")
        z_scaled, tanh_done, v_done = sem("z_scaled"), sem("tanh_done"), sem("v_done")
        pooled, pooled_hi, pooled_lo = sem("pooled"), sem("pooled_hi"), sem("pooled_lo")
        m_hi_done = sem("m_hi_done")
        e_hi_done, e_lo_done, y_ready = sem("e_hi_done"), sem("e_lo_done"), sem("y_ready")
        ln_centred, ln_sq = sem("ln_centred"), sem("ln_sq")
        ln_scaled, ln_act, ln_lo = sem("ln_scaled"), sem("ln_act"), sem("ln_lo")
        packed = sem("packed")
        rw_landed, conv_step = sem("rw_landed"), sem("conv_step")
        gate_scaled, silu_done = sem("gate_scaled"), sem("silu_done")
        f_ready, f_hi_done, f_lo_done = sem("f_ready"), sem("f_hi_done"), sem("f_lo_done")
        state_stored = sem("state_stored")
        gb_landed, hn_sq = sem("gb_landed"), sem("hn_sq")
        rwg_done, logits_done, hot_done, ranks_done = sem("rwg_done"), sem("logits_done"), sem("hot_done"), sem("ranks_done")
        gap_done, exp_done, hn_done, hn_hi_done, hn_lo_done = (sem(n) for n in ("gap_done", "exp_done", "hn_done", "hn_hi_done", "hn_lo_done"))
        hn_scaled, tok_rstd = sem("hn_scaled"), sem("tok_rstd")
        routed, extra_done = sem("routed"), sem("extra_done")
        top_done, route_step = sem("top_done"), sem("route_step")
        sel_ready, gather_done, xg_hi_done, xg_lo_done = (sem(n) for n in ("sel_ready", "gather_done", "xg_hi_done", "xg_lo_done"))
        g_done, u_done, e_silu, e_f, t_done, ft_hi_done, ft_lo_done, d_done = (
            sem(n) for n in ("g_done", "u_done", "e_silu", "e_f", "t_done", "ft_hi_done", "ft_lo_done", "d_done"))
        o_hi_done, o_lo_done, comb_done, comb_read = (sem(n) for n in ("o_hi_done", "o_lo_done", "comb_done", "comb_read"))
        selt_done, selt_read = sem("selt_done"), sem("selt_read")
        fin_sq, fin_out, stored = sem("fin_sq"), sem("fin_out"), sem("stored")
        dve_step, act_step, pool_step = sem("dve_step"), sem("act_step"), sem("pool_step")

        def h_group(i, k):
            return GROUP[[("x", k), ("wout", 0, k), ("down", k)][i]] + 1

        def token_pieces():
            out = []
            for name, start, n in (("meta", 0, META), ("prompt", META, SEQ), ("sample", TP, DB * DS)):
                at = start
                while at < start + n:
                    m = min(start + n, (at // TT + 1) * TT) - at
                    out.append((at // TT, at % TT, m, name, at - start))
                    at += m
            return out

        PIECES = token_pieces()
        SRC = {"meta": meta_tokens, "prompt": x_prompt[0], "sample": x_sample.rearrange("a b d -> (a b) d")}
        DST = {"prompt": y_prompt[0], "sample": y_sample.rearrange("a b d -> (a b) d")}

        def samples(ap):
            return ap.rearrange("p (b t) -> p b t", b=DB)

        def state_dsts(l):
            return [(pool_s[l].rearrange("b r d -> (b r) d"), DB * PB),
                    (conv_s[l, 0:HB].rearrange("b r d -> (b r) d"), DB * PB),
                    (conv_s[l, HB:DB].rearrange("b r d -> (b r) d"), DB * PB),
                    (pool_p[l, 0], PB), (conv_p[l, 0], CB)]

        SUMS = {name: i for i, name in enumerate(
            [("norm", 0), ("mean", 0), ("var", 0), ("norm", 1), ("norm", 2), ("mean", 1), ("var", 1)])}

        def raw_slot(i):
            return raw[:, i % RAW, :]

        def blk(w, k0, nk, c0, nc_):
            return w[k0 * P:(k0 + nk) * P, c0:c0 + nc_].rearrange("(k p) n -> p k n", p=P), nk, nc_

        def dense_slots():
            out = []
            for l in range(L):
                out += [blk(w_in[l], 0, KD, 256 * s, 256) for s in WIN_ORDER]
                out += [(("diag", l, c, a), z - a, P) for c in PE_TILES for a, z in DIAG_PARTS]
                out.append((pool_w[l].rearrange("g p n -> p g n"), NG, P))
                out.append(blk(conv_pw_w[l], 0, KC, 0, CW))
                out += [blk(w_out[l], 0, KD, 256 * s, 256) for s in range(4)]
                if l == 0:
                    for u in range(FF // 256):
                        out.append(blk(ffn_w_gate[0], 0, KD, 256 * u, 256))
                        out.append(blk(ffn_w_up[0], 0, KD, 256 * u, 256))
                    for c, parts in enumerate(DOWN_PARTS):
                        k0 = 0
                        for nk in parts:
                            out.append(blk(ffn_w_down[0], k0, nk, 256 * c, 256))
                            k0 += nk
            return out

        SLOTS = dense_slots()
        assert len(SLOTS) == MOE_BASE

        def slot_size(n):
            return SLOTS[n][1] * SLOTS[n][2]

        block = ctx.enter_context(nc.Block())

        @block.sync
        def _(sp):
            def reuse(n):
                sp.wait_ge(lo_done, n - RAW + 1)

            for t, r, m, name, row in PIECES:
                sp.dma_start(x_tok[r:r + m, t, :], SRC[name][row:row + m, :]).then_inc(x_landed, 16)
            for n, (src, nk, ncol) in enumerate(SLOTS):
                if isinstance(src, tuple):
                    continue
                if n >= RAW:
                    reuse(n)
                dst = raw[:, n % RAW, 0:nk * ncol].rearrange("p (k n) -> p k n", k=nk)
                sp.dma_start(dst, src).then_inc(landed[n % RAW], 16)

            def load_expert(p, e):
                for j in range(NJ):
                    todo = [(gate_slot(j) + i, moe_w_gate, i, j) for i in (0, 1)]
                    todo += [(up_slot(j) + i, moe_w_up, i, j) for i in (0, 1)]
                    for jj in ([j - 1] if j else []) + ([j] if j == NJ - 1 else []):
                        todo += [(down_slot(jj) + i, moe_w_down, i, jj) for i in (0, 1)]
                    for i, w, half, jj in todo:
                        reuse(MOE_BASE + ES * p + i)
                        we = w[0, ds(e, 1)]
                        n = MOE_BASE + i
                        if w is moe_w_down:
                            src = we[:, (4 * jj + 2 * half) * P:(4 * jj + 2 * half + 2) * P, :]
                            src = src.rearrange("a (k p) n -> p (a k) n", p=P)
                            dst = raw_slot(n).rearrange("p (k n) -> p k n", k=2)
                        else:
                            src = we[:, 4 * half * P:4 * (half + 1) * P, 512 * jj:512 * (jj + 1)]
                            src = src.rearrange("a (k p) n -> p (a k) n", p=P)
                            dst = raw_slot(n).rearrange("p (k n) -> p k n", k=4)
                        sp.dma_start(dst, src).then_inc(landed[n % RAW], 16)

            with sp.Fori(0, NE) as p:
                load_expert(p, p)
            sp.wait_ge(extra_done, 1)
            n_over = sp.value_load(eids[0:1, 6:7], min_val=0, max_val=5)
            with sp.If(n_over > 0):
                with sp.Fori(0, n_over) as i:
                    e = sp.value_load(eids[0:1, ds(i, 1)], min_val=0, max_val=NE - 1)
                    load_expert(i + NE, e)
                sp.nop()
            n_out = 0
            for t, r, m, name, row in PIECES:
                if name != "meta":
                    sp.wait_ge(fin_out, t + 1)
                    sp.dma_start(DST[name][row:row + m, :], yt[r:r + m, t, :]).then_inc(stored, 16)
                    n_out += 1
            sp.wait_ge(stored, 16 * n_out)
            sp.wait_ge(state_stored, 16 * 5 * L)

        @block.gpsimd
        def _(pool):
            step = [0]

            def link(ins):
                step[0] += 1
                ins.then_inc(pool_step, 1)
                pool.wait_ge(pool_step, step[0])

            link(nc.gpsimd.memset(ident[:], 0.0))
            link(nc.gpsimd.affine_select(out=ident[:], in_=ident[:], compare_op=ALU.not_equal, fill=1.0,
                                         base=0, pattern=[[-1, P]], channel_multiplier=1))
            link(nc.gpsimd.memset(ones[:], 1.0))
            link(nc.gpsimd.memset(before[:], 0.0))
            link(nc.gpsimd.affine_select(out=before[:], in_=before[:], compare_op=ALU.is_ge, fill=1.0,
                                         base=0, pattern=[[-1, P]], channel_multiplier=1))
            link(nc.gpsimd.iota(iota_slot[:], pattern=[[1, P]], base=0, channel_multiplier=0,
                                allow_small_or_imprecise_dtypes=True))
            link(nc.gpsimd.iota(iota_e[:], pattern=[[1, NE]], base=0, channel_multiplier=0,
                                allow_small_or_imprecise_dtypes=True))
            for t in range(16):
                link(nc.gpsimd.memset(inv_cnt[:, t:t + 1], 1.0 / (t + 1)))
            nc.gpsimd.sem_inc(consts, 1)

            def squares(i):
                if i:
                    pool.wait_ge(sums_done, SUMS[("norm", i - 1)] + 1)
                for k in range(KD):
                    pool.wait_ge(evac, h_group(i, k))
                    if k == 0:
                        link(nc.gpsimd.tensor_tensor(sqs, h[:, 0, :], h[:, 0, :], ALU.mult))
                        continue
                    link(nc.gpsimd.tensor_tensor(sq, h[:, k, :], h[:, k, :], ALU.mult))
                    link(nc.gpsimd.tensor_tensor(sqs, sqs, sq, ALU.add))
                pool.sem_inc(sq_ready, 1)

            def diagonals(l, k):
                n = MIX_BASE[l] + S_DIAG + k
                (_, _, c, a), taps, _ = SLOTS[n]
                if n >= RAW:
                    pool.wait_ge(lo_done, n - RAW + 1)
                at = 64 + (l * KC + c) * TAPS + a
                nc.gpsimd.tensor_tensor(
                    raw[:, n % RAW, 0:taps * P].rearrange("p (k n) -> p k n", k=taps),
                    ident[:].unsqueeze(1).broadcast_to([P, taps, P]),
                    params[:, at:at + taps].unsqueeze(2).broadcast_to([P, taps, P]), ALU.mult
                ).then_inc(landed[n % RAW], 16)

            def mixer_layer(l):
                if l == 0:
                    pool.wait_ge(evac, GROUP[("params",)] + 1)
                else:
                    squares(2)
                pool.dma_start(state_io[:, 0, :], state_pool[l].rearrange("b r d -> (b r) d")
                               ).then_inc(past_landed, 16)
                for i in (0, 1):
                    pool.dma_start(state_io[:, 1 + i, :],
                                   state_conv[l, HB * i:HB * (i + 1)].rearrange("b r d -> (b r) d")
                                   ).then_inc(past_landed, 16)
                link(nc.gpsimd.memset(pool_ext[:, :, 0:PB], 0.0))
                link(nc.gpsimd.memset(conv_ext[:, :, 0:CB], 0.0))
                pool.sem_inc(ext_zero, 1)
                if l == 0:
                    squares(0)
                for k in range(4):
                    diagonals(l, k)
                for g in range(NG):
                    pool.wait_ge(evac, GROUP[("win", l, g)] + 1)
                    src, shift = pool_ext[:, g, :], 1
                    for s in range(g + 1):
                        dst = win_sum[:, s % 2, :]
                        lo = 2 * shift - 1
                        link(nc.gpsimd.tensor_tensor(dst[:, lo:PEXT], src[:, lo:PEXT],
                                                     src[:, lo - shift:PEXT - shift], ALU.add))
                        src, shift = dst, 2 * shift
                    mean, win = win_sum[:, (g + 1) % 2, :], WINDOWS[g]
                    link(nc.gpsimd.tensor_scalar(mean[:, PB:PEXT], src[:, PB:PEXT], 1.0 / win, 0.0,
                                                 ALU.mult, ALU.add))
                    link(nc.gpsimd.tensor_tensor(mean[:, PB:PB + win - 1], src[:, PB:PB + win - 1],
                                                 inv_cnt[:, 0:win - 1], ALU.mult))
                    link(nc.gpsimd.tensor_tensor(y_pool[:, g, 0:TP], mean[:, PB:PSEG], pool_ext[:, g, PB:PSEG],
                                                 ALU.subtract))
                    link(nc.gpsimd.tensor_tensor(samples(y_pool[:, g, TP:T])[:, :, 0:DS],
                                                 samples(mean[:, PSEG:PEXT])[:, :, PB:PS1],
                                                 samples(pool_ext[:, g, PSEG:PEXT])[:, :, PB:PS1], ALU.subtract))
                    pool.sem_inc(pooled, 1)
                for g in range(NG):
                    pool.wait_ge(pooled_hi, NG * l + g + 1)
                    nc.gpsimd.tensor_tensor(x_lo[:, 4 + g, :], y_pool[:, g, :], x_hi[:, 4 + g, :].bitcast(F32),
                                            ALU.subtract).then_inc(pooled_lo, 1)
                pool.wait_ge(ln_lo, KC * (l + 1))
                for g in range(NG):
                    link(nc.gpsimd.tensor_copy(samples(z[:, g, 0:DB * PB]),
                                               samples(pool_ext[:, g, PSEG:PEXT])[:, :, DS:PS1]))
                    link(nc.gpsimd.tensor_copy(samples(y[:, g, 0:DB * CB]),
                                               samples(conv_ext[:, g, CSEG:CEXT])[:, :, DS:CS1]))
                pool.sem_inc(packed, 1)
                if l == 0:
                    squares(1)
                else:
                    pool.wait_ge(evac, GROUP[("wout", 1, KD - 1)] + 1)
                    for i, g in enumerate((norm2_g[1:2, :], final_norm_g.rearrange("(a d) -> a d", a=1))):
                        pool.dma_start(gb[:, i, :], g.broadcast_to([TT, D])
                                       ).then_inc(gb_landed, 16)
                    pool.wait_ge(gb_landed, 32)
                    for t in range(3):
                        pool.wait_ge(hn_scaled, t + 1)
                        nc.gpsimd.tensor_tensor(hn[:, t, :], hn[:, t, :], gb[:, 0, :], ALU.mult).then_inc(hn_done, 1)
                for i, (dst, rows) in enumerate(state_dsts(l)):
                    pool.wait_ge(evac, GROUP[("state", l, i)] + 1)
                    pool.dma_start(dst, state_io[0:rows, i, :]).then_inc(state_stored, 16)

            mixer_layer(0)
            pool.wait_ge(state_stored, 16 * 5)
            mixer_layer(1)

            def fold(x, out):
                n = 2 * NE
                while n > 2:
                    n //= 2
                    link(nc.gpsimd.tensor_tensor(x[:, :, 0:n], x[:, :, 0:n], x[:, :, n:2 * n], ALU.add))
                link(nc.gpsimd.tensor_tensor(out, x[:, :, 0], x[:, :, 1], ALU.add))

            pool.wait_ge(routed, 1)
            for c in (0, 1):
                link(nc.gpsimd.tensor_scalar(over[:, c, :], cnt[:], float(P * (c + 1)), None, ALU.is_gt))
            link(nc.gpsimd.tensor_tensor(n_chunks[:], over[:, 0, :], over[:, 1, :], ALU.add))
            link(nc.gpsimd.memset(key[:, 0, 0:1], 0.0))
            for e in range(1, NE):
                link(nc.gpsimd.tensor_tensor(key[:, 0, e:e + 1], key[:, 0, e - 1:e], n_chunks[:, e - 1:e], ALU.add))
            link(nc.gpsimd.tensor_copy(key_sum[:], key[:, 0, NE - 1:NE]))
            link(nc.gpsimd.tensor_scalar(key[:, 1, :], key[:, 0, :], 2.0, None, ALU.add))
            link(nc.gpsimd.tensor_scalar(key[:, 0, :], key[:, 0, :], 1.0, None, ALU.add))
            link(nc.gpsimd.tensor_tensor(key[:], key[:], over[:], ALU.mult))
            flat = key[:].rearrange("p c e -> p (c e)")
            for i in range(6):
                link(nc.gpsimd.tensor_scalar(pick[:, i, :], flat, float(i + 1), None, ALU.is_equal))
            for i in range(6):
                for c in (0, 1):
                    link(nc.gpsimd.tensor_tensor(prod[:, i, NE * c:NE * (c + 1)], pick[:, i, NE * c:NE * (c + 1)],
                                                 iota_e[:], ALU.mult))
            fold(prod, eids_f[:, 0:6])
            link(nc.gpsimd.tensor_tensor(eids_f[:, 6:7], key_sum[:], n_chunks[:, NE - 1:NE], ALU.add))
            link(nc.gpsimd.tensor_copy(eids[:, 0:7], eids_f[:, 0:7]))
            for c in (0, 1):
                link(nc.gpsimd.tensor_scalar(posc[:, :, c, :], posm[:], 1.0 - P * (c + 1), None, ALU.add))
            for i in range(6):
                for src, dst in ((posc, POS), (gates, GT)):
                    for t in range(3):
                        link(nc.gpsimd.tensor_tensor(prod3[:, t, :], src[:, t].rearrange("p c e -> p (c e)"),
                                                     pick[0:TT, i, :], ALU.mult))
                    fold(prod3, dst[:, :, NE + i])
            link(nc.gpsimd.tensor_scalar(POS[:, :, NE:NSEL], POS[:, :, NE:NSEL], -1.0, None, ALU.add))
            pool.sem_inc(extra_done, 1)

        def dense_used():
            out, n_w = [], 0
            for n in range(MOE_BASE):
                b = next(x for x in (MIX_BASE[1], FFN_BASE, 0) if n >= x)
                if b == FFN_BASE and n >= DOWN_BASE:
                    ends = [sum(len(x) for x in DOWN_PARTS[:c + 1]) - 1 for c in range(4)]
                    if n - DOWN_BASE in ends:
                        out.append((mm_done, GROUP[("down", 2 * ends.index(n - DOWN_BASE) + 1)] + 1))
                    else:
                        n_w += 1
                        out.append((w_used, n_w))
                elif b == FFN_BASE:
                    u, i = divmod(n - b, 2)
                    out.append((mm_done, GROUP[("gu", u, 2 * i + 1)] + 1))
                else:
                    l, i = MIX_BASE.index(b), n - b
                    if S_DIAG <= i < S_POOL_W and (i - S_DIAG) % 2 == 0:
                        n_w += 1
                        out.append((w_used, n_w))
                        continue
                    last = (("win", l, 2 * WIN_ORDER[i] + 1) if i < S_DIAG else
                            ("conv", l, PE_TILES[(i - S_DIAG) // 2]) if i < S_POOL_W else
                            ("pool", l, NG - 1) if i == S_POOL_W else
                            ("pw", l, KC - 1) if i == S_PW else ("wout", l, 2 * (i - S_OUT) + 1))
                    out.append((mm_done, GROUP[last] + 1))
            return out, n_w

        DENSE_USED, W_BASE = dense_used()
        PASS_USED = [None] * ES
        for j in range(NJ):
            PASS_USED[gate_slot(j) + 1] = (g_done, NJ, j + 1)
            PASS_USED[up_slot(j) + 1] = (u_done, NJ, j + 1)
        PASS_USED[down_slot(NJ - 1) + 1] = (d_done, 1, 2)
        W_PASS = PASS_USED.count(None)
        N_W = 0
        for i in range(ES):
            if PASS_USED[i] is None:
                N_W += 1
                PASS_USED[i] = (w_used, W_PASS, W_BASE + N_W)

        def wait_used_dense(eng, n):
            s, v = DENSE_USED[n]
            eng.wait_ge(s, v)

        def wait_used_pass(eng, p, i):
            s, per, v = PASS_USED[i % ES]
            if i < 0:
                v -= per
            eng.wait_ge(s, p * per + v)

        def parts(n, size=SLOT):
            return raw[:, n % RAW, 0:size], w_hi[:, n % SPLIT, 0:size], w_lo[:, n % SPLIT, 0:size]

        def split_hi_dense(act, n):
            r, hi, _ = parts(n, slot_size(n))
            act.wait_ge(landed[n % RAW], 16 * (n // RAW + 1))
            if n >= SPLIT:
                wait_used_dense(act, n - SPLIT)
            nc.scalar.activation(hi, r, ACT.Copy).then_inc(hi_done, 1)

        def split_lo_dense(dve, n):
            r, hi, lo = parts(n, slot_size(n))
            dve.wait_ge(hi_done, n + 1)
            nc.vector.tensor_tensor(lo, r, hi.bitcast(F32), ALU.subtract).then_inc(lo_done, 1)

        def split_hi_pass(act, p, i):
            n = MOE_BASE + i
            r, hi, _ = parts(n)
            act.wait_ge(landed[n % RAW], p * (16 * ES // RAW) + 16 * (n // RAW + 1))
            wait_used_pass(act, p, i - SPLIT)
            nc.scalar.activation(hi, r, ACT.Copy).then_inc(hi_done, 1)

        def split_lo_pass(dve, p, i):
            r, hi, lo = parts(MOE_BASE + i)
            dve.wait_ge(hi_done, p * ES + (MOE_BASE + i + 1))
            nc.vector.tensor_tensor(lo, r, hi.bitcast(F32), ALU.subtract).then_inc(lo_done, 1)

        def splitter(eng, split):
            at = [0]

            def to(n):
                while at[0] <= min(n, MOE_BASE - 1):
                    split(eng, at[0])
                    at[0] += 1

            return to, at

        FU = FF // 256
        LOOPS = FU // 3
        GU0 = GROUP[("gu", 0, 0)]

        def gu_bank(uu, x):
            return ps[:, (GU0 + 4 * uu + x) % MM_BANKS, 0:T]

        def split_hi_gu(act, i, s):
            r, hi, _ = parts(FFN_BASE + s)
            act.wait_ge(landed[(FFN_BASE + s) % RAW], i * 16 + 16 * ((FFN_BASE + s) // RAW + 1))
            act.wait_ge(mm_done, i * 12 + (GU0 + 2 * (s - SPLIT + 1)))
            nc.scalar.activation(hi, r, ACT.Copy).then_inc(hi_done, 1)

        def split_lo_gu(dve, i, s):
            r, hi, lo = parts(FFN_BASE + s)
            dve.wait_ge(hi_done, i * 6 + (FFN_BASE + s + 1))
            nc.vector.tensor_tensor(lo, r, hi.bitcast(F32), ALU.subtract).then_inc(lo_done, 1)

        @block.scalar
        def _(act):
            split_to, split_at = splitter(act, split_hi_dense)
            step = [0]

            for l in range(L):
                for at, n, w in ((NG1, 8, norm1_g), (NG2, 8, norm2_g), (PSC, 4, pool_scale), (DWB, 4, conv_dw_b),
                                 (LNG, 4, conv_ln_g), (LNB, 4, conv_ln_b)):
                    act.dma_start(par_rows[32 * l + at:32 * l + at + n, :], w[l].rearrange("(k p) -> k p", p=P)
                                  ).then_inc(par_landed, 16)
                act.dma_start(dw_rows[:, l, :], conv_dw_w[l]).then_inc(par_landed, 16)
            act.dma_start(rw[:], router_w[0].rearrange("(k p) e -> p k e", p=P)).then_inc(rw_landed, 16)

            def x_hi_parts(i, l, which):
                for k in range(KD):
                    if k == 0:
                        act.wait_ge(evac, max(h_group(i, 0), GROUP[("params",)] + 1))
                    act.wait_ge(evac, h_group(i, k))
                    nc.scalar.activation(x_hi[:, k, :], h[:, k, :], ACT.Copy, scale=col(l, which, k)
                                         ).then_inc(x_hi_done, 1)

            def mixer_layer(l):
                b = MIX_BASE[l]
                x_hi_parts(2 * l, l, NG1)
                split_to(b + 2)
                for half in (0, 1):
                    split_to(b + 3 + 2 * half)
                    for i in (0, 1):
                        c = 2 * half + i
                        act.wait_ge(z_scaled, KC * l + c + 1)
                        nc.scalar.activation(z[:, 2 + i, :], z[:, 2 + i, :], ACT.Tanh, scale=0.5
                                             ).then_inc(tanh_done, 1)
                    act.wait_ge(v_done, 8 * l + 4 * half + 2)
                    act.wait_ge(ext_zero, l + 1)
                    act.wait_ge(evac, GROUP[("past_conv", l, half)] + 1)
                    nc.scalar.activation(e_hi[:, half, :], conv_ext[:, PE_TILES[half], :], ACT.Copy
                                         ).then_inc(e_hi_done, 1)
                for i in range(S_DIAG, S_DIAG + 4):
                    split_to(b + i)
                for g in range(NG):
                    if g == 0:
                        act.wait_ge(mm_done, GROUP[("win", l, 2 * WIN_ORDER[-1] + 1)] + 1)
                    act.wait_ge(pooled, NG * l + g + 1)
                    nc.scalar.activation(x_hi[:, 4 + g, :], y_pool[:, g, :], ACT.Copy).then_inc(pooled_hi, 1)
                for i in range(S_POOL_W, S_PW + 2):
                    split_to(b + i)
                for g in range(NG):
                    act.wait_ge(mm_done, GROUP[("pool", l, g)] + 1)
                    nc.scalar.activation(m_hi[:, g, :], ps[:, GROUP[("pool", l, g)] % MM_BANKS, 0:T], ACT.Copy,
                                         scale=col(l, PSC, g)).then_inc(m_hi_done, 1)
                split_to(b + S_PW + 2)
                for c in range(KC):
                    act.wait_ge(ln_centred, KC * l + c + 1)
                    nc.scalar.activation(z[:, c, :], y[:, c, :], ACT.Square).then_inc(ln_sq, 1)
                for c in range(KC):
                    act.wait_ge(ln_scaled, KC * l + c + 1)
                    step[0] += 1
                    nc.scalar.activation(z[:, c, :], y[:, c, :], ACT.Silu, scale=col(l, LNG, c), bias=col(l, LNB, c)
                                         ).then_inc(act_step, 1)
                    act.wait_ge(act_step, step[0])
                    nc.scalar.activation(x_hi[:, c, :], z[:, c, :], ACT.Copy).then_inc(ln_act, 1)
                for m in range(KC):
                    act.wait_ge(mm_done, GROUP[("pw", l, m)] + 1)
                    nc.scalar.activation(m_hi[:, NG + m, :], ps[:, GROUP[("pw", l, m)] % MM_BANKS, 0:T], ACT.Copy
                                         ).then_inc(m_hi_done, 1)
                for s in range(4):
                    split_to(b + S_OUT + 2 + s)

            split_to(1)
            mixer_layer(0)

            x_hi_parts(1, 0, NG2)

            def gate_up(i, uu, split):
                u = i * 3 + uu
                split(2 * uu + 2)
                for x in (0, 1):
                    act.wait_ge(gate_scaled, u * 2 + (x + 1))
                    nc.scalar.activation(gs[:, x, :], gs[:, x, :], ACT.Silu).then_inc(silu_done, 1)
                split(2 * uu + 3)
                for x in (0, 1):
                    act.wait_ge(f_ready, u * 2 + (x + 1))
                    nc.scalar.activation(f_hi[:, ds(u * 2 + x, 1), :], us[:, x:x + 1, :], ACT.Copy
                                         ).then_inc(f_hi_done, 1)

            with act.Fori(0, LOOPS) as i:
                for uu in range(3):
                    gate_up(i, uu, lambda s, i=i: split_hi_gu(act, i, s))
            split_at[0] = FFN_BASE + 6 * LOOPS + 2
            for uu in range(FU - 3 * LOOPS):
                gate_up(LOOPS, uu, lambda s: split_to(FFN_BASE + 6 * LOOPS + s))
            split_to(MIX_BASE[1] + 1)
            mixer_layer(1)

            def token_squares(ready, done):
                for t in range(3):
                    ready(t)
                    nc.scalar.activation(hn[:, t, :], yt[:, t, :], ACT.Square, accum_out=nt[0:TT, t, 3:4]
                                         ).then_inc(done, 1)

            token_squares(lambda t: act.wait_ge(evac, GROUP[("htok", t, 1)] + 1), hn_sq)
            act.wait_ge(tok_rstd, 1)
            for t in range(3):
                nc.scalar.activation(hn[:, t, :], yt[:, t, :], ACT.Copy, scale=nt[0:TT, t, 1:2]).then_inc(hn_scaled, 1)
            act.wait_ge(gap_done, 1)
            nc.scalar.activation(gt[:, :, 1], gt[:, :, 0], ACT.Exp).then_inc(exp_done, 1)
            for t in range(3):
                act.wait_ge(hn_done, t + 1)
                nc.scalar.activation(hn_hi[:, t, :], hn[:, t, :], ACT.Copy).then_inc(hn_hi_done, 1)

            def gathered_hi(p):
                act.wait_ge(gather_done, p + 1)
                for i, x in enumerate((X0, X1)):
                    nc.scalar.activation(xg_hi[:, 4 * i:4 * i + 4, :], x.rearrange("p (k s) -> p k s", k=4), ACT.Copy
                                         ).then_inc(xg_hi_done, 1)

            def out_hi(p):
                act.wait_ge(d_done, p + 1)
                act.wait_ge(selt_read, p * 2 + 2)
                act.wait_ge(comb_read, p * 6 + 1)
                for i in (0, 1):
                    nc.scalar.activation(o_hi[:, 512 * i:512 * (i + 1)], D_[:, i, :], ACT.Copy, scale=slot_gate[:, 0:1]
                                         ).then_inc(o_hi_done, 1)

            def expert_pass(p):
                def after(i):
                    for j in range(NJ):
                        c = p * NJ + j
                        if i == gate_slot(j) + 1:
                            act.wait_ge(g_done, c + 1)
                            act.wait_ge(e_f, c + 1)
                            nc.scalar.activation(act_s[:], G_, ACT.Silu).then_inc(e_silu, 1)
                        if i == (up_slot(0) + 1 if j == 0 else down_slot(j - 1) + 1):
                            act.wait_ge(t_done, c + 2)
                            nc.scalar.activation(ft_hi[:], T_.rearrange("p (k s) -> p k s", k=4), ACT.Copy
                                                 ).then_inc(ft_hi_done, 1)
                    if i == -1:
                        out_hi(p)

                for i in range(ES):
                    split_hi_pass(act, p, i)
                    if i >= 1:
                        after(i - 2)
                gathered_hi(p + 1)

            gathered_hi(0)
            with act.Fori(0, NE) as p:
                expert_pass(p)
            act.wait_ge(extra_done, 1)
            n_over = act.value_load(eids[0:1, 6:7], min_val=0, max_val=5)
            with act.If(n_over > 0):
                with act.Fori(0, n_over) as i:
                    expert_pass(i + NE)
                act.nop()
            n_pass = n_over + NE
            out_hi(n_pass)
            token_squares(lambda t: act.wait_ge(comb_read, n_pass * 6 + (2 * t + 3)), fin_sq)

        @block.vector
        def _(dve):
            split_to, split_at = splitter(dve, split_lo_dense)
            step = [0]

            def link(ins):
                step[0] += 1
                ins.then_inc(dve_step, 1)
                dve.wait_ge(dve_step, step[0])

            def bank(name):
                return ps[:, GROUP[name] % MM_BANKS, :]

            def made(name):
                dve.wait_ge(mm_done, GROUP[name] + 1)

            def rsqrt(a, yy, tt):
                link(nc.vector.tensor_scalar(yy.bitcast(I32), a.bitcast(I32), 1, None, ALU.logical_shift_right))
                link(nc.vector.tensor_scalar(yy.bitcast(I32), yy.bitcast(I32), -1.0, RSQRT_SEED, ALU.mult, ALU.add))
                for _ in range(3):
                    link(nc.vector.tensor_tensor(tt, yy, yy, ALU.mult))
                    link(nc.vector.scalar_tensor_tensor(tt, tt, -0.5, a, ALU.mult, ALU.mult))
                    link(nc.vector.scalar_tensor_tensor(yy, tt, 1.5, yy, ALU.add, ALU.mult))

            def rstd_from_sum(name, n, eps):
                dve.wait_ge(sums_done, SUMS[name] + 1)
                link(nc.vector.tensor_scalar(nrm_a, SUM_BANK, 1.0 / n, eps, ALU.mult, ALU.add))
                dve.sem_inc(sums_read, 1)
                rsqrt(nrm_a, rstd[:], nrm_t)

            def x_lo_parts(i, l, which):
                for k in range(KD):
                    dve.wait_ge(x_hi_done, KD * i + k + 1)
                    nc.vector.scalar_tensor_tensor(x_lo[:, k, :], h[:, k, :], col(l, which, k),
                                                   x_hi[:, k, :].bitcast(F32), ALU.mult, ALU.subtract
                                                   ).then_inc(x_lo_done, 1)

            for k in range(KD):
                made(("x", k))
                nc.vector.tensor_copy(h[:, k, :], bank(("x", k))[:, 0:T]).then_inc(evac, 1)
            made(("params",))
            n_par = 64 + L * KC * TAPS
            nc.vector.tensor_copy(params[:], bank(("params",))[:, 0:n_par]).then_inc(evac, 1)
            dve.wait_ge(evac, GROUP[("params",)] + 1)
            dve.wait_ge(rw_landed, 16)
            for k in range(KD):
                nc.vector.tensor_scalar(rwg[:, k, :], rw[:, k, :], col(1, NG2, k), None, ALU.mult).then_inc(rwg_done, 1)

            def mixer_layer(l):
                b = MIX_BASE[l]

                def conv(taps):
                    for j in taps:
                        for c in DVE_TILES:
                            for src, dst in (
                                    (conv_ext[:, c, j:j + TP], y[:, c, 0:TP]),
                                    (samples(conv_ext[:, c, CSEG:CEXT])[:, :, j:j + DS], samples(y[:, c, TP:T]))):
                                if j == 0:
                                    ins = nc.vector.tensor_scalar(dst, src, tap(l, c, 0), col(l, DWB, c), ALU.mult, ALU.add)
                                else:
                                    dve.wait_ge(conv_step, conv_n[0] - 2 * len(DVE_TILES) + 1)
                                    ins = nc.vector.scalar_tensor_tensor(dst, src, tap(l, c, j), dst, ALU.mult, ALU.add)
                                ins.then_inc(conv_step, 1)
                                conv_n[0] += 1

                x_lo_parts(2 * l, l, NG1)
                split_to(b + 3)
                rstd_from_sum(("norm", 2 * l), D, 1e-6)
                for half in (0, 1):
                    s0 = 2 * half
                    split_to(b + s0 + 2)
                    for i in (0, 1):
                        g = ("win", l, 2 * WIN_ORDER[s0] + i)
                        made(g)
                        nc.vector.scalar_tensor_tensor(z[:, i, :], bank(g)[:, 0:T], 0.5, rstd[:], ALU.mult, ALU.mult
                                                       ).then_inc(evac, 1)
                    split_to(b + s0 + 3)
                    for i in (0, 1):
                        g = ("win", l, 2 * WIN_ORDER[s0 + 1] + i)
                        made(g)
                        link(nc.vector.tensor_tensor(z[:, 2 + i, :], bank(g)[:, 0:T], rstd[:], ALU.mult))
                        dve.sem_inc(z_scaled, 1)
                        dve.sem_inc(evac, 1)
                    if half == 0:
                        made(("past_pool", l))
                        nc.vector.tensor_copy(
                            pool_ext[:, :, PSEG:PEXT].rearrange("p g (b t) -> p g b t", b=DB)[:, :, :, 0:PB],
                            bank(("past_pool", l))[:, 0:NG * DB * PB].rearrange("p (g b t) -> p g b t", g=NG, b=DB)
                        ).then_inc(evac, 1)
                        for i in (0, 1):
                            made(("past_conv", l, i))
                            nc.vector.tensor_copy(
                                conv_ext[:, 2 * i:2 * i + 2, CSEG:CEXT].rearrange("p g (b t) -> p g b t", b=DB)[:, :, :, 0:CB],
                                bank(("past_conv", l, i))[:, 0:2 * DB * CB].rearrange("p (g b t) -> p g b t", g=2, b=DB)
                            ).then_inc(evac, 1)
                        dve.wait_ge(ext_zero, l + 1)
                    for i in (0, 1):
                        c = 2 * half + i
                        dve.wait_ge(tanh_done, KC * l + c + 1)
                        nc.vector.scalar_tensor_tensor(conv_ext[:, c, CB:CSEG], z[:, 2 + i, 0:TP], 1.0, z[:, i, 0:TP],
                                                       ALU.add, ALU.mult).then_inc(v_done, 1)
                        nc.vector.scalar_tensor_tensor(samples(conv_ext[:, c, CSEG:CEXT])[:, :, CB:CS1],
                                                       samples(z[:, 2 + i, TP:T]), 1.0, samples(z[:, i, TP:T]),
                                                       ALU.add, ALU.mult).then_inc(v_done, 1)
                    dve.wait_ge(v_done, 8 * l + 4 * (half + 1))
                    dve.wait_ge(e_hi_done, 2 * l + half + 1)
                    nc.vector.tensor_tensor(e_lo[:, half, :], conv_ext[:, PE_TILES[half], :], e_hi[:, half, :].bitcast(F32),
                                            ALU.subtract).then_inc(e_lo_done, 1)

                def pool_in(s):
                    for i in (0, 1):
                        g = 2 * WIN_ORDER[s] + i
                        made(("win", l, g))
                        link(nc.vector.tensor_tensor(pool_ext[:, g, PB:PSEG], bank(("win", l, g))[:, 0:TP],
                                                     rstd[:, 0:TP], ALU.mult))
                        nc.vector.tensor_tensor(samples(pool_ext[:, g, PSEG:PEXT])[:, :, PB:PS1],
                                                samples(bank(("win", l, g))[:, TP:T]), samples(rstd[:, TP:T]),
                                                ALU.mult).then_inc(evac, 1)

                def conv_from_pe(c):
                    made(("conv", l, c))
                    link(nc.vector.tensor_scalar(y[:, c, :], bank(("conv", l, c))[:, 0:T], col(l, DWB, c), None, ALU.add))
                    dve.sem_inc(evac, 1)

                for p in (4, 5):
                    split_to(b + p + 2)
                    pool_in(p)
                n_pieces = 2 * len(DIAG_PARTS)
                for i in range(n_pieces):
                    split_to(b + S_DIAG + 2 + i)
                    conv(range(TAPS * i // n_pieces, TAPS * (i + 1) // n_pieces))
                    if i % 2:
                        conv_from_pe(PE_TILES[i // 2])
                split_to(b + S_PW + 1)
                dve.wait_ge(conv_step, conv_n[0])
                dve.sem_inc(y_ready, 1)
                dve.wait_ge(sums_done, SUMS[("mean", l)] + 1)
                for c in range(KC):
                    nc.vector.scalar_tensor_tensor(y[:, c, :], SUM_BANK, -1.0 / CW, y[:, c, :], ALU.mult, ALU.add
                                                   ).then_inc(ln_centred, 1)
                dve.wait_ge(ln_centred, KC * (l + 1))
                dve.sem_inc(sums_read, 1)
                for g in range(NG):
                    name = ("pool", l, g)
                    dve.wait_ge(m_hi_done, KD * l + g + 1)
                    nc.vector.scalar_tensor_tensor(m_lo[:, g, :], bank(name)[:, 0:T], col(l, PSC, g),
                                                   m_hi[:, g, :].bitcast(F32), ALU.mult, ALU.subtract).then_inc(evac, 1)
                split_to(b + S_PW + 2)
                rstd_from_sum(("var", l), CW, 1e-5)
                for c in range(KC):
                    nc.vector.tensor_tensor(y[:, c, :], y[:, c, :], rstd[:], ALU.mult).then_inc(ln_scaled, 1)
                for c in range(KC):
                    dve.wait_ge(ln_act, KC * l + c + 1)
                    nc.vector.tensor_tensor(x_lo[:, c, :], z[:, c, :], x_hi[:, c, :].bitcast(F32), ALU.subtract
                                            ).then_inc(ln_lo, 1)
                for m in range(KC):
                    name = ("pw", l, m)
                    dve.wait_ge(m_hi_done, KD * l + NG + m + 1)
                    nc.vector.tensor_tensor(m_lo[:, NG + m, :], bank(name)[:, 0:T], m_hi[:, NG + m, :].bitcast(F32),
                                            ALU.subtract).then_inc(evac, 1)
                for s in range(4):
                    split_to(b + S_OUT + 2 + s)
                    for i in (0, 1):
                        name = ("wout", l, 2 * s + i)
                        made(name)
                        hh = h[:, 2 * s + i, :]
                        nc.vector.tensor_tensor(hh, hh, bank(name)[:, 0:T], ALU.add).then_inc(evac, 1)
                if l == 1:
                    for t in range(3):
                        for i in (0, 1):
                            made(("htok", t, i))
                            nc.vector.tensor_copy(yt[:, t, 512 * i:512 * (i + 1)], bank(("htok", t, i))[0:TT, :]
                                                  ).then_inc(evac, 1)
                for i, (_, rows) in enumerate(state_dsts(l)):
                    made(("state", l, i))
                    nc.vector.tensor_copy(state_io[0:rows, i, :], bank(("state", l, i))[0:rows, :]).then_inc(evac, 1)

            conv_n = [0]
            split_to(1)
            mixer_layer(0)

            x_lo_parts(1, 0, NG2)
            rstd_from_sum(("norm", 1), D, 1e-6)

            def gate_up(i, uu, split):
                u = i * 3 + uu
                split(2 * uu + 2)
                for x in (0, 1):
                    dve.wait_ge(mm_done, u * 4 + (GU0 + x + 1))
                    nc.vector.tensor_tensor(gs[:, x, :], gu_bank(uu, x), rstd[:], ALU.mult).then_inc(gate_scaled, 1)
                dve.wait_ge(gate_scaled, u * 2 + 2)
                dve.sem_inc(evac, 2)
                split(2 * uu + 3)
                for x in (0, 1):
                    dve.wait_ge(mm_done, u * 4 + (GU0 + x + 3))
                    nc.vector.tensor_tensor(us[:, x, :], gu_bank(uu, 2 + x), rstd[:], ALU.mult).then_inc(evac, 1)
                dve.wait_ge(evac, u * 4 + (GU0 + 4))
                for x in (0, 1):
                    dve.wait_ge(silu_done, u * 2 + (x + 1))
                    nc.vector.tensor_tensor(us[:, x, :], us[:, x, :], gs[:, x, :], ALU.mult).then_inc(f_ready, 1)
                for x in (0, 1):
                    dve.wait_ge(f_hi_done, u * 2 + (x + 1))
                    nc.vector.tensor_tensor(f_lo[:, ds(u * 2 + x, 1), :], us[:, x:x + 1, :],
                                            f_hi[:, ds(u * 2 + x, 1), :].bitcast(F32), ALU.subtract
                                            ).then_inc(f_lo_done, 1)

            with dve.Fori(0, LOOPS) as i:
                for uu in range(3):
                    gate_up(i, uu, lambda s, i=i: split_lo_gu(dve, i, s))
            split_at[0] = FFN_BASE + 6 * LOOPS + 2
            for uu in range(FU - 3 * LOOPS):
                gate_up(LOOPS, uu, lambda s: split_to(FFN_BASE + 6 * LOOPS + s))
            n = DOWN_BASE
            for c, ks in enumerate(DOWN_PARTS):
                for _ in ks:
                    split_to(n + 2)
                    n += 1
                for i in (0, 1):
                    name = ("down", 2 * c + i)
                    made(name)
                    hh = h[:, 2 * c + i, :]
                    nc.vector.tensor_tensor(hh, hh, bank(name)[:, 0:T], ALU.add).then_inc(evac, 1)
            mixer_layer(1)

            def rstd_tokens():
                link(nc.vector.tensor_scalar(nt[0:TT, :, 0], nt[0:TT, :, 3], 1.0 / D, 1e-6, ALU.mult, ALU.add))
                rsqrt(nt[0:TT, :, 0], nt[0:TT, :, 1], nt[0:TT, :, 2])

            def over_experts(ap):
                return ap.unsqueeze(2).broadcast_to([TT, 3, NE])

            dve.wait_ge(hn_sq, 3)
            rstd_tokens()
            dve.sem_inc(tok_rstd, 1)
            dve.wait_ge(logits_done, 1)
            dve.wait_ge(evac, N_GROUPS)
            link(nc.vector.tensor_tensor(lg[:], ps[0:TT, 6, 0:3 * NE].rearrange("p (t e) -> p t e", t=3),
                                         over_experts(nt[0:TT, :, 1]), ALU.mult))
            for t in range(3):
                ins = nc.vector.max(out=top[:, t, :], in_=lg[:, t, :])
                if t < 2:
                    ins.then_inc(top_done, 1)
                else:
                    link(ins)
            dve.wait_ge(top_done, 2)
            nc.vector.tensor_tensor(gt[:, :, 0], top[:, :, 1], top[:, :, 0], ALU.subtract).then_inc(gap_done, 1)
            for t in range(3):
                nc.vector.max_index(out=top_i[:, t, :], in_max=top[:, t, :], in_values=lg[:, t, :]).then_inc(top_done, 1)
            dve.wait_ge(top_done, 5)
            link(nc.vector.tensor_copy(top_f[:], top_i[:, :, 0:2]))
            experts = iota_e[0:TT].unsqueeze(1).broadcast_to([TT, 3, NE])
            link(nc.vector.tensor_tensor(hot1[:], experts, over_experts(top_f[:, :, 0]), ALU.is_equal))
            link(nc.vector.tensor_tensor(hot2[:], experts, over_experts(top_f[:, :, 1]), ALU.is_equal))
            nc.vector.tensor_tensor(hot[:], hot1[:], hot2[:], ALU.add).then_inc(hot_done, 1)
            dve.wait_ge(hot_done, 1)
            dve.wait_ge(exp_done, 1)
            link(nc.vector.tensor_scalar(gt[:, :, 2], gt[:, :, 1], 1.0, None, ALU.add))
            link(nc.vector.reciprocal(gt[:, :, 2], gt[:, :, 2]))
            link(nc.vector.tensor_tensor(gt[:, :, 3], gt[:, :, 1], gt[:, :, 2], ALU.mult))
            link(nc.vector.tensor_tensor(gates[:, :, 0, :], hot1[:], over_experts(gt[:, :, 2]), ALU.mult))
            link(nc.vector.tensor_tensor(gates[:, :, 1, :], hot2[:], over_experts(gt[:, :, 3]), ALU.mult))
            link(nc.vector.tensor_tensor(gates[:, :, 0, :], gates[:, :, 0, :], gates[:, :, 1, :], ALU.add))
            dve.wait_ge(ranks_done, 1)
            link(nc.vector.scalar_tensor_tensor(posm[:].rearrange("p t e -> p (t e)"), ps[0:TT, 7, 0:3 * NE], 1.0,
                                                hot[:].rearrange("p t e -> p (t e)"), ALU.add, ALU.mult))
            link(nc.vector.tensor_scalar(posm[:], posm[:], -1.0, None, ALU.add))
            link(nc.vector.tensor_copy(POS[:, :, 0:NE], posm[:]))

            def select(p):
                for t in range(3):
                    nc.vector.tensor_scalar(sel[:, t, :], iota_slot[0:TT, :], POS[:, t, ds(p, 1)], None, ALU.is_equal
                                            ).then_inc(sel_ready, 1)

            select(0)
            for t in range(3):
                dve.wait_ge(hn_hi_done, t + 1)
                nc.vector.tensor_tensor(hn_lo[:, t, :], hn[:, t, :], hn_hi[:, t, :].bitcast(F32), ALU.subtract
                                        ).then_inc(hn_lo_done, 1)

            nc.vector.tensor_copy(gates[:, :, 1, :], gates[:, :, 0, :]).then_inc(route_step, 1)
            nc.vector.tensor_copy(GT[:, :, 0:NE], gates[:, :, 0, :]).then_inc(route_step, 1)
            nc.vector.tensor_copy(cnt[:], ps[:, 7, 3 * NE:4 * NE]).then_inc(route_step, 1)
            nc.vector.memset(sel_t[:].bitcast(F32), 0.0).then_inc(route_step, 1)
            nc.vector.memset(slot_gate[:], 0.0).then_inc(route_step, 1)
            nc.vector.memset(D_, 0.0).then_inc(route_step, 1)
            dve.wait_ge(route_step, 6)
            dve.sem_inc(routed, 1)
            dve.sem_inc(selt_read, 2)
            dve.sem_inc(d_done, 1)
            for s in (e_silu, e_f, t_done, ft_lo_done, comb_read):
                dve.sem_inc(s, 1)

            def gathered_lo(p):
                for i, x in enumerate((X0, X1)):
                    dve.wait_ge(xg_hi_done, p * 2 + (i + 1))
                    nc.vector.tensor_tensor(xg_lo[:, 4 * i:4 * i + 4, :], x.rearrange("p (k s) -> p k s", k=4),
                                            xg_hi[:, 4 * i:4 * i + 4, :].bitcast(F32), ALU.subtract).then_inc(xg_lo_done, 1)

            def out_lo(p):
                for i in (0, 1):
                    dve.wait_ge(o_hi_done, p * 2 + (i + 1))
                    cols = slice(512 * i, 512 * (i + 1))
                    nc.vector.scalar_tensor_tensor(o_lo[:, cols], D_[:, i, :], slot_gate[:, 0:1],
                                                   o_hi[:, cols].bitcast(F32), ALU.mult, ALU.subtract).then_inc(o_lo_done, 1)

            def add_outputs(p, parts_):
                for i in parts_:
                    t, half = divmod(i, 2)
                    dve.wait_ge(comb_done, p * 6 + (i + 1))
                    cols = yt[:, t, 512 * half:512 * (half + 1)]
                    nc.vector.tensor_tensor(cols, cols, (X0, X1, X2)[i % 3][0:TT, :], ALU.add).then_inc(comb_read, 1)

            def expert_pass(p):
                def after(i):
                    for j in range(NJ):
                        c = p * NJ + j
                        if i == up_slot(j) + 1:
                            dve.wait_ge(u_done, c + 1)
                            dve.wait_ge(e_silu, c + 2)
                            dve.wait_ge(t_done, c + 1)
                            nc.vector.tensor_tensor(act_f[:], act_s[:], U_, ALU.mult).then_inc(e_f, 1)
                        if i == (up_slot(0) + 1 if j == 0 else down_slot(j - 1) + 1):
                            if j < 2:
                                add_outputs(p, range(3 * j, 3 * j + 3))
                            dve.wait_ge(ft_hi_done, c + 1)
                            nc.vector.tensor_tensor(ft_lo[:], T_.rearrange("p (k s) -> p k s", k=4),
                                                    ft_hi[:].bitcast(F32), ALU.subtract).then_inc(ft_lo_done, 1)
                    if i == -1:
                        out_lo(p)
                    if i == gate_slot(4) + 1:
                        dve.wait_ge(selt_done, p + 1)
                        nc.vector.tensor_copy(sel_t[:], X0[:, 0:T]).then_inc(selt_read, 1)
                        nc.vector.tensor_copy(slot_gate[:], X1[:, 0:1]).then_inc(selt_read, 1)
                    if i == up_slot(5) + 1:
                        dve.wait_ge(extra_done, 1)
                        select(p + 1)

                for i in range(ES):
                    split_lo_pass(dve, p, i)
                    if i >= 1:
                        after(i - 2)
                gathered_lo(p + 1)

            gathered_lo(0)
            with dve.Fori(0, NE) as p:
                expert_pass(p)
            n_over = dve.value_load(eids[0:1, 6:7], min_val=0, max_val=5)
            with dve.If(n_over > 0):
                with dve.Fori(0, n_over) as i:
                    expert_pass(i + NE)
                dve.nop()
            n_pass = n_over + NE
            out_lo(n_pass)
            add_outputs(n_pass, range(6))
            dve.wait_ge(fin_sq, 3)
            rstd_tokens()
            for t in range(3):
                nc.vector.scalar_tensor_tensor(yt[:, t, :], yt[:, t, :], nt[0:TT, t, 1:2], gb[:, 1, :], ALU.mult, ALU.mult
                                               ).then_inc(fin_out, 1)

        @block.tensor
        def _(pe):
            def bank(name):
                return ps[:, GROUP[name] % MM_BANKS, :]

            def group(name):
                q = GROUP[name]
                if q >= MM_BANKS:
                    pe.wait_ge(evac, q - MM_BANKS + 1)
                return ps[:, q % MM_BANKS, :]

            def mm3(out, a_hi, a_lo, b_hi, b_lo, start, stop):
                nc.tensor.matmul(out, a_hi, b_hi, start=start, stop=False)
                nc.tensor.matmul(out, a_hi, b_lo, start=False, stop=False)
                return nc.tensor.matmul(out, a_lo, b_hi, start=False, stop=stop)

            def dense_slot(n, ncol):
                size = slot_size(n)
                _, hi, lo = parts(n, size)
                return (x.rearrange("p (k n) -> p k n", n=ncol) for x in (hi, lo))

            def sums(name, rhs, ready, count):
                i = SUMS[name]
                if i:
                    pe.wait_ge(sums_read, i)
                for c, x in enumerate(rhs):
                    pe.wait_ge(ready, count(c))
                    ins = nc.tensor.matmul(SUM_BANK, ones[:], x, start=(c == 0), stop=(c == len(rhs) - 1))
                ins.then_inc(sums_done, 1)

            pe.wait_ge(consts, 1)
            pe.wait_ge(x_landed, 16 * len(PIECES))
            for k in range(KD):
                out = group(("x", k))
                for t in range(3):
                    ins = nc.tensor.transpose(out[:, TT * t:TT * (t + 1)], x_tok[:, t, P * k:P * (k + 1)], ident[0:TT, 0:TT])
                ins.then_inc(mm_done, 1)
            pe.wait_ge(par_landed, 16 * 7 * L)
            out = group(("params",))
            nc.tensor.transpose(out[:, 0:64], par_rows[:], ident[0:64, 0:64])
            for l in range(L):
                for c in range(KC):
                    o = 64 + (l * KC + c) * TAPS
                    ins = nc.tensor.transpose(out[:, o:o + TAPS], dw_rows[:, l, P * c:P * (c + 1)], ident[0:TAPS, 0:TAPS])
            ins.then_inc(mm_done, 1)

            def project(name_of, n, i, ncol, k_ready):
                out = group(name_of)
                hi, lo = dense_slot(n, ncol)
                nk = slot_size(n) // ncol
                for k in range(nk):
                    if k_ready:
                        k_ready(k)
                    cols = slice(P * i, P * (i + 1))
                    ins = mm3(out[:, 0:T], hi[:, k, cols], lo[:, k, cols], x_hi[:, k, :], x_lo[:, k, :],
                              k == 0, k == nk - 1)
                ins.then_inc(mm_done, 1)

            def split_ready(n):
                pe.wait_ge(lo_done, n + 1)

            def mixer_layer(l):
                b = MIX_BASE[l]

                def w_in_slot(s):
                    split_ready(b + s)
                    for i in (0, 1):
                        ready = (lambda k: pe.wait_ge(x_lo_done, KD * 2 * l + k + 1)) if s == 0 and i == 0 else None
                        project(("win", l, 2 * WIN_ORDER[s] + i), b + s, i, 256, ready)

                w_in_slot(0)
                w_in_slot(1)
                sums(("norm", 2 * l), [sqs], sq_ready, lambda c: 2 * l + 1)
                pe.wait_ge(past_landed, 16 * 3 * (l + 1))
                n_rows = DB * PB
                out = group(("past_pool", l))
                for g in range(NG):
                    ins = nc.tensor.transpose(out[:, n_rows * g:n_rows * (g + 1)], state_io[:, 0, P * g:P * (g + 1)],
                                              ident[0:n_rows, 0:n_rows])
                ins.then_inc(mm_done, 1)
                for i in (0, 1):
                    out = group(("past_conv", l, i))
                    for c in (0, 1):
                        for hb in (0, 1):
                            at = n_rows * (2 * c + hb)
                            ins = nc.tensor.transpose(out[:, at:at + n_rows],
                                                      state_io[:, 1 + hb, P * (2 * i + c):P * (2 * i + c + 1)],
                                                      ident[0:n_rows, 0:n_rows])
                    ins.then_inc(mm_done, 1)
                for s in range(2, S_DIAG):
                    w_in_slot(s)
                for half, c in enumerate(PE_TILES):
                    out = group(("conv", l, c))
                    pe.wait_ge(e_lo_done, 2 * l + half + 1)
                    for k, (first, end) in enumerate(DIAG_PARTS):
                        n = b + S_DIAG + 2 * half + k
                        split_ready(n)
                        hi, lo = dense_slot(n, P)
                        for j in range(first, end):
                            for pr in (True, False):
                                def shifted(e):
                                    return e[:, half, j:j + TP] if pr else samples(e[:, half, CSEG:CEXT])[:, :, j:j + DS]
                                o = out[:, 0:TP] if pr else samples(out[:, TP:T])
                                ins = mm3(o, hi[:, j - first, :], lo[:, j - first, :], shifted(e_hi), shifted(e_lo),
                                          j == 0 and pr, j == TAPS - 1 and not pr)
                        ins.then_inc(mm_done if k else w_used, 1)
                split_ready(b + S_POOL_W)
                for g in range(NG):
                    out = group(("pool", l, g))
                    hi, lo = dense_slot(b + S_POOL_W, P)
                    pe.wait_ge(pooled_lo, NG * l + g + 1)
                    mm3(out[:, 0:T], hi[:, g, :], lo[:, g, :], x_hi[:, 4 + g, :], x_lo[:, 4 + g, :], True, True
                        ).then_inc(mm_done, 1)
                sums(("mean", l), [y[:, c, :] for c in range(KC)], y_ready, lambda c: l + 1)
                sums(("var", l), [z[:, c, :] for c in range(KC)], ln_sq, lambda c: KC * l + c + 1)
                split_ready(b + S_PW)
                for m in range(KC):
                    ready = (lambda k: pe.wait_ge(ln_lo, KC * l + k + 1)) if m == 0 else None
                    project(("pw", l, m), b + S_PW, m, CW, ready)
                pe.wait_ge(evac, GROUP[("pw", l, KC - 1)] + 1)
                for s in range(4):
                    split_ready(b + S_OUT + s)
                    hi, lo = dense_slot(b + S_OUT + s, 256)
                    for i in (0, 1):
                        out = group(("wout", l, 2 * s + i))
                        for k in range(KD):
                            cols = slice(P * i, P * (i + 1))
                            ins = mm3(out[:, 0:T], hi[:, k, cols], lo[:, k, cols], m_hi[:, k, :], m_lo[:, k, :],
                                      k == 0, k == KD - 1)
                        ins.then_inc(mm_done, 1)
                if l == 1:
                    pe.wait_ge(evac, GROUP[("wout", 1, KD - 1)] + 1)
                    for t in range(3):
                        for i in (0, 1):
                            out = group(("htok", t, i))
                            for k in range(4):
                                ins = nc.tensor.transpose(out[0:TT, P * k:P * (k + 1)],
                                                          h[:, 4 * i + k, TT * t:TT * (t + 1)], ident[:])
                            ins.then_inc(mm_done, 1)
                    pe.wait_ge(rwg_done, KD)
                    pe.wait_ge(sums_read, SUMS[("var", 1)] + 1)
                    for t in range(3):
                        for k in range(KD):
                            ins = nc.tensor.matmul(ps[0:TT, 6, NE * t:NE * (t + 1)], h[:, k, TT * t:TT * (t + 1)],
                                                   rwg[:, k, :], start=(k == 0), stop=(k == KD - 1))
                    ins.then_inc(logits_done, 1)
                pe.wait_ge(packed, l + 1)
                srcs = [lambda g: z[:, g, 0:DB * PB],
                        lambda g: y[:, g, 0:HB * CB],
                        lambda g: y[:, g, HB * CB:DB * CB],
                        lambda g: pool_ext[:, g, PSEG - PB:PSEG],
                        lambda g: conv_ext[:, g, CSEG - CB:CSEG]]
                for i, (_, rows) in enumerate(state_dsts(l)):
                    out = group(("state", l, i))
                    for g in range(NG):
                        ins = nc.tensor.transpose(out[0:rows, P * g:P * (g + 1)], srcs[i](g), ident[:])
                    ins.then_inc(mm_done, 1)

            mixer_layer(0)

            sums(("norm", 1), [sqs], sq_ready, lambda c: 2)
            pe.wait_ge(x_lo_done, KD * 2)

            def gate_up(i, uu):
                u = i * 3 + uu
                for s in (0, 1):
                    pe.wait_ge(lo_done, u * 2 + (FFN_BASE + s + 1))
                    hi, lo = dense_slot(FFN_BASE + 2 * uu + s, 256)
                    for x in (0, 1):
                        pe.wait_ge(evac, u * 4 + (GU0 + 2 * s + x - MM_BANKS + 1))
                        for k in range(KD):
                            cols = slice(P * x, P * (x + 1))
                            ins = mm3(gu_bank(uu, 2 * s + x), hi[:, k, cols], lo[:, k, cols], x_hi[:, k, :], x_lo[:, k, :],
                                      k == 0, k == KD - 1)
                        ins.then_inc(mm_done, 1)

            with pe.Fori(0, LOOPS) as i:
                for uu in range(3):
                    gate_up(i, uu)
            for uu in range(FU - 3 * LOOPS):
                gate_up(LOOPS, uu)
            n = DOWN_BASE
            for c, ks in enumerate(DOWN_PARTS):
                outs = [group(("down", 2 * c + i)) for i in (0, 1)]
                k0 = 0
                for part, nk in enumerate(ks):
                    split_ready(n)
                    hi, lo = dense_slot(n, 256)
                    pe.wait_ge(f_lo_done, min(k0 + nk, NFT))
                    for i in (0, 1):
                        for k in range(nk):
                            cols = slice(P * i, P * (i + 1))
                            ins = mm3(outs[i][:, 0:T], hi[:, k, cols], lo[:, k, cols], f_hi[:, k0 + k, :], f_lo[:, k0 + k, :],
                                      k0 + k == 0, k0 + k == NFT - 1)
                        if part == len(ks) - 1:
                            ins.then_inc(mm_done, 1)
                    if part < len(ks) - 1:
                        ins.then_inc(w_used, 1)
                    k0 += nk
                    n += 1
            mixer_layer(1)

            pe.wait_ge(hot_done, 1)
            for t in range(3):
                for u in range(t + 1):
                    nc.tensor.matmul(ps[0:TT, 7, NE * t:NE * (t + 1)], (before if u == t else ones)[0:TT, 0:TT],
                                     hot[:, u, :], start=(u == 0), stop=(u == t))
            for u in range(3):
                ins = nc.tensor.matmul(ps[:, 7, 3 * NE:4 * NE], ones[0:TT, :], hot[:, u, :], start=(u == 0), stop=(u == 2))
            ins.then_inc(ranks_done, 1)

            def gather(p):
                pe.wait_ge(sel_ready, p * 3 + 3)
                for m in range(KD):
                    for t in range(3):
                        for src in (hn_hi, hn_lo):
                            ins = nc.tensor.matmul((X0, X1)[m // 4][:, P * (m % 4):P * (m % 4 + 1)],
                                                   src[:, t, P * m:P * (m + 1)], sel[:, t, :],
                                                   start=(t == 0 and src is hn_hi), stop=(t == 2 and src is hn_lo))
                ins.then_inc(gather_done, 1)

            def combine(p, outputs):
                pe.wait_ge(o_lo_done, p * 2 + 2)
                pe.wait_ge(selt_read, p * 2 + 2)
                for i in outputs:
                    t, half = divmod(i, 2)
                    pe.wait_ge(comb_read, p * 6 + max(i - 1, 1))
                    for o in (o_hi, o_lo):
                        ins = nc.tensor.matmul((X0, X1, X2)[i % 3][0:TT, :], sel_t[:, TT * t:TT * (t + 1)],
                                               o[:, 512 * half:512 * (half + 1)], start=(o is o_hi), stop=(o is o_lo))
                    ins.then_inc(comb_done, 1)

            def expert_pass(p):
                def hidden(j, slot0, out, done):
                    for half in (0, 1):
                        i = slot0 + half
                        pe.wait_ge(lo_done, p * ES + (MOE_BASE + i + 1))
                        _, hi, lo = (x.rearrange("p (k n) -> p k n", k=4) for x in parts(MOE_BASE + i))
                        for k in range(4):
                            kk = 4 * half + k
                            ins = mm3(out, xg_hi[:, kk, :], xg_lo[:, kk, :], hi[:, k, :], lo[:, k, :], kk == 0, kk == 7)
                        ins.then_inc(done if half else w_used, 1)

                def down(j):
                    pe.wait_ge(ft_lo_done, p * NJ + (j + 2))
                    if j == 0:
                        pe.wait_ge(o_lo_done, p * 2 + 2)
                    for half in (0, 1):
                        i = down_slot(j) + half
                        pe.wait_ge(lo_done, p * ES + (MOE_BASE + i + 1))
                        _, hi, lo = (x.rearrange("p (k n) -> p k n", k=2) for x in parts(MOE_BASE + i))
                        for k in range(2):
                            for d in (0, 1):
                                cols = slice(512 * d, 512 * (d + 1))
                                kk = 2 * half + k
                                ins = mm3(D_[:, d, :], ft_hi[:, kk, :], ft_lo[:, kk, :], hi[:, k, cols], lo[:, k, cols],
                                          j == 0 and kk == 0, j == NJ - 1 and kk == 3)
                        ins.then_inc(d_done if j == NJ - 1 and half else w_used, 1)

                pe.wait_ge(xg_lo_done, p * 2 + 2)
                for j in range(NJ):
                    c = p * NJ + j
                    pe.wait_ge(e_silu, c + 1)
                    hidden(j, gate_slot(j), G_, g_done)
                    pe.wait_ge(e_f, c + 1)
                    hidden(j, up_slot(j), U_, u_done)
                    if j:
                        down(j - 1)
                    if j < 2:
                        combine(p, range(3 * j, 3 * j + 3))
                    pe.wait_ge(e_f, c + 2)
                    pe.wait_ge(ft_lo_done, c + 1)
                    for k in range(4):
                        ins = nc.tensor.transpose(T_[:, P * k:P * (k + 1)], act_f[:, P * k:P * (k + 1)], ident[:])
                    ins.then_inc(t_done, 1)
                    if j == 3:
                        pe.wait_ge(comb_read, p * 6 + 7)
                        for t in range(3):
                            nc.tensor.transpose(X0[:, TT * t:TT * (t + 1)], sel[:, t, :].bitcast(F32), ident[0:TT, 0:TT])
                        for t in range(3):
                            ins = nc.tensor.matmul(X1[:, 0:1], sel[:, t, :].bitcast(F32), GT[:, t, ds(p, 1)],
                                                   start=(t == 0), stop=(t == 2))
                        ins.then_inc(selt_done, 1)
                pe.wait_ge(selt_read, p * 2 + 4)
                gather(p + 1)
                down(NJ - 1)

            pe.wait_ge(routed, 1)
            pe.wait_ge(hn_lo_done, 3)
            gather(0)
            with pe.Fori(0, NE) as p:
                expert_pass(p)
            pe.wait_ge(extra_done, 1)
            n_over = pe.value_load(eids[0:1, 6:7], min_val=0, max_val=5)
            with pe.If(n_over > 0):
                with pe.Fori(0, n_over) as i:
                    expert_pass(i + NE)
                pe.nop()
            combine(n_over + NE, range(6))


_INS = ['x_prompt', 'x_sample', 'state_pool', 'state_conv', 'meta_tokens', 'norm1_g', 'w_in', 'pool_w', 'pool_scale',
        'conv_dw_w', 'conv_dw_b', 'conv_ln_g', 'conv_ln_b', 'conv_pw_w', 'w_out', 'norm2_g', 'ffn_w_gate', 'ffn_w_up',
        'ffn_w_down', 'router_w', 'moe_w_gate', 'moe_w_up', 'moe_w_down', 'final_norm_g']


def kernel(**inputs):
    import numpy as _np
    import concourse.bacc as _bacc
    from concourse import mybir as _mybir
    from concourse.bass_utils import run_bass_kernel_spmd as _run

    nc = _bacc.Bacc("TRN2", target_bir_lowering=False, num_devices=1)
    arrays, args = {}, []
    for name in _INS:
        a = _np.ascontiguousarray(inputs[name])
        arrays[f"in_{name}_dram"] = a
        args.append(nc.dram_tensor(f"in_{name}_dram", a.shape, _mybir.dt.from_np(a.dtype), kind="ExternalInput").ap())
    layers, prompts = inputs["w_in"].shape[0], inputs["x_prompt"].shape[0]
    pool_state, conv_state = inputs["state_pool"].shape, inputs["state_conv"].shape
    outs = [inputs["x_prompt"].shape, inputs["x_sample"].shape,
            (layers, prompts) + tuple(pool_state[2:]), (layers, prompts) + tuple(conv_state[2:]),
            pool_state, conv_state]
    for i, shape in enumerate(outs):
        args.append(nc.dram_tensor(f"out_{i}_dram", tuple(shape), _mybir.dt.float32, kind="ExternalOutput").ap())
    hybrid_trunk(nc, *args)
    r = _run(nc, [arrays], core_ids=[0])
    return tuple(r.results[0][f"out_{i}_dram"] for i in range(len(outs)))
```

```python
from contextlib import ExitStack

import concourse.bass as bass
from concourse import mybir

F32 = mybir.dt.float32
F32R = mybir.dt.float32r
I32 = mybir.dt.int32
U32 = mybir.dt.uint32
ALU = mybir.AluOpType
ACT = mybir.ActivationFunctionType
ds = bass.ds

P = 128
MM_BANKS = 6
RAW = 6
SPLIT = 3
SLOT = 2048
RSQRT_SEED = float(0x5F3759DF)


def hybrid_trunk(nc, x_prompt, x_sample, state_pool, state_conv, meta_tokens, norm1_g, w_in, pool_w,
                 pool_scale, conv_dw_w, conv_dw_b, conv_ln_g, conv_ln_b, conv_pw_w, w_out, norm2_g,
                 ffn_w_gate, ffn_w_up, ffn_w_down, router_w, moe_w_gate, moe_w_up, moe_w_down,
                 final_norm_g, y_prompt, y_sample, pool_p, conv_p, pool_s, conv_s):
    D = x_prompt.shape[2]
    SEQ, META = x_prompt.shape[1], meta_tokens.shape[0]
    DB, DS = x_sample.shape[0], x_sample.shape[1]
    L = w_in.shape[0]
    PW = state_pool.shape[3]
    CW = state_conv.shape[3]
    PB, CB = state_pool.shape[2], state_conv.shape[2]
    TAPS = conv_dw_w.shape[1]
    FF = ffn_w_gate.shape[2]
    NE = router_w.shape[2]
    EF = moe_w_gate.shape[3]
    KD = D // P
    TP = META + SEQ
    T = TP + DB * DS
    TT = T // 3
    KC = CW // P
    NG = PW // P
    NFT = FF // P
    WINDOWS = [2 << g for g in range(NG)]
    assert (L, KD, KC, NG, T % 3) == (2, 8, 4, 4, 0) and TT <= P
    PSEG, CSEG = PB + TP, CB + TP
    PS1, CS1 = PB + DS, CB + DS
    PEXT, CEXT = PSEG + DB * PS1, CSEG + DB * CS1
    HB = DB // 2

    WIN_ORDER = [2, 4, 3, 5, 1, 0]
    POOL_ORDER = (2, 3, 0, 1)
    PE_TILES, DVE_TILE = (0, 2, 3), 1
    Y_ORDER = (1, 0, 2, 3)
    DIAG_TAPS = SLOT // P
    PE_TAPS = (TAPS, TAPS, TAPS - 1)
    DIAG_PARTS = [[(0, DIAG_TAPS), (DIAG_TAPS, n)] for n in PE_TAPS]
    N_DIAG = 2 * len(PE_TILES)
    S_DIAG, S_LATE = 5, 5 + N_DIAG
    S_POOL_W, S_PW, S_OUT = S_LATE + 1, S_LATE + 2, S_LATE + 3
    MIX_SLOTS = 12 + N_DIAG
    DOWN_PARTS = [[6, 6, 5, 5], [6, 6, 5, 5], [8, 8, 6], [8, 8, 6]]
    FFN_BASE = MIX_SLOTS
    N_GU = 2 * (FF // 256)
    DOWN_BASE = FFN_BASE + N_GU
    MIX_BASE = [0, DOWN_BASE + sum(len(x) for x in DOWN_PARTS)]
    MOE_BASE = MIX_BASE[1] + MIX_SLOTS
    NJ = EF // 512
    ES = 6 * NJ
    assert ES % RAW == 0
    NSEL = NE + 6

    def gate_slot(j):
        return 0 if j == 0 else 6 * j - 2

    def up_slot(j):
        return gate_slot(j) + 2

    def down_slot(j):
        return 6 * j + 8 if j < NJ - 1 else 6 * j + 4

    HALF_DONE = (5, KD - 1)

    GROUP = {}

    def plan(*names):
        for name in names:
            GROUP[name] = len(GROUP)

    plan(*[("x", k) for k in range(KD)], ("params",))
    for l in range(L):
        plan(*[("win", l, 2 * s + i) for s in WIN_ORDER[:2] for i in (0, 1)])
        plan(("past_pool", l), ("past_conv", l, 0), ("past_conv", l, 1))
        plan(*[("win", l, 2 * s + i) for s in WIN_ORDER[2:5] for i in (0, 1)])
        plan(*[("conv", l, c) for c in PE_TILES])
        plan(*[("win", l, g) for g in POOL_ORDER[2:]], *[("pool", l, g) for g in POOL_ORDER[:2]])
        plan(*[("pw", l, m) for m in range(KC)], *[("pool", l, g) for g in POOL_ORDER[2:]])
        for m in range(KD):
            plan(("wout", l, m))
            if l == 1 and m in HALF_DONE:
                plan(*[("htok", t, HALF_DONE.index(m)) for t in range(3)])
        plan(*[("state", l, i) for i in range(5)])
        if l == 0:
            plan(*[("gu", u, i) for u in range(FF // 256) for i in range(4)])
            plan(*[("down", m) for m in range(KD)])
    N_GROUPS = len(GROUP)

    with ExitStack() as ctx:
        def sem(name):
            return ctx.enter_context(nc.semaphore(name))

        def sb(name, shape, dt=F32, at=ctx):
            return at.enter_context(nc.sbuf_tensor(name, shape, dt))

        raw = sb("raw", [P, RAW, SLOT])
        w_hi = sb("w_hi", [P, SPLIT, SLOT], F32R)
        w_lo = sb("w_lo", [P, SPLIT, SLOT], F32R)
        h = sb("h", [P, KD, T])
        ident = sb("ident", [P, P])
        ones = sb("ones", [P, P])
        before = sb("before", [P, P])
        iota_slot = sb("iota_slot", [P, P])
        iota_e = sb("iota_e", [P, NE])
        inv_cnt = sb("inv_cnt", [P, 16])
        state_io = sb("state_io", [DB * PB, 5, 512])
        params = sb("params", [P, 64 + L * KC * TAPS])
        rw = sb("rw", [P, KD, NE])
        rwg = sb("rwg", [P, KD, NE])
        nt = sb("nt", [P, 3, 4])
        NG1, NG2, PSC, DWB, LNG, LNB = (0, KD), (16, KD), (32, NG), (40, KC), (48, KC), (56, KC)

        def col(l, which, k):
            c = which[0] + l * which[1] + k
            return params[:, c:c + 1]

        def tap(l, c, j):
            at = 64 + (l * KC + c) * TAPS + j
            return params[:, at:at + 1]

        dense = ExitStack()
        tap_hi = sb("tap_hi", [P, L * KC * TAPS], F32R, dense)
        tap_lo = sb("tap_lo", [P, L * KC * TAPS], F32, dense)
        x_hi = sb("x_hi", [P, KD, T], F32R, dense)
        x_lo = sb("x_lo", [P, KD, T], F32R, dense)
        rstd = sb("rstd", [P, T], F32, dense)
        scratch = sb("scratch", [P, 4, T], F32, dense)
        nrm_a, nrm_t = scratch[:, 0, :], scratch[:, 1, :]
        sqs, sq = scratch[:, 2, :], scratch[:, 3, :]
        mixer = ExitStack()
        m_hi = sb("m_hi", [P, KD, T], F32R, mixer)
        m_lo = sb("m_lo", [P, KD, T], F32R, mixer)
        pool_ext = sb("pool_ext", [P, NG, PEXT], F32, mixer)
        win_sum = sb("win_sum", [P, 2, PEXT], F32, mixer)
        conv_ext = sb("conv_ext", [P, KC, CEXT], F32, mixer)
        y = sb("y", [P, KC, T], F32, mixer)
        z = sb("z", [P, 4, T], F32, mixer)
        y_pool = sb("y_pool", [P, NG, T], F32, mixer)
        mixer.close()
        spread_in = scratch[0:TT, 0, :]
        e_hi = m_hi[:, KC:, :].rearrange("p k t -> p (k t)")[:, 0:3 * CSEG].rearrange("p (c t) -> p c t", c=3)
        e_lo = m_lo[:, KC:, :].rearrange("p k t -> p (k t)")[:, 0:3 * CSEG].rearrange("p (c t) -> p c t", c=3)
        ffn = ExitStack()
        f_hi = sb("f_hi", [P, NFT, T], F32R, ffn)
        f_lo = sb("f_lo", [P, NFT, T], F32R, ffn)
        gs, us = scratch[:, 0:2, :], scratch[:, 2:4, :]
        ffn.close()
        first = ExitStack()
        x_tok = sb("x_tok", [TT, 3, D], F32, first)
        par_rows = sb("par_rows", [64, P], F32, first)
        dw_rows = sb("dw_rows", [TAPS, L, CW], F32, first)
        first.close()
        dense.close()
        moe = ctx
        gb = sb("gb", [TT, 2, D], F32, moe)
        yt = sb("yt", [TT, 3, D], F32, moe)
        hn = sb("hn", [TT, 3, D], F32, moe)
        hn_hi = sb("hn_hi", [TT, 3, D], F32R, moe)
        hn_lo = sb("hn_lo", [TT, 3, D], F32R, moe)
        xg_hi = sb("xg_hi", [P, KD, P], F32R, moe)
        xg_lo = sb("xg_lo", [P, KD, P], F32R, moe)
        act_s = sb("act_s", [P, 512], F32, moe)
        act_f = sb("act_f", [P, 512], F32, moe)
        ft_hi = sb("ft_hi", [P, 4, P], F32R, moe)
        ft_lo = sb("ft_lo", [P, 4, P], F32R, moe)
        o_hi = sb("o_hi", [P, D], F32R, moe)
        o_lo = sb("o_lo", [P, D], F32R, moe)
        sel = sb("sel", [TT, 3, P], F32R, moe)
        sel_t = sb("sel_t", [P, T], F32R, moe)
        slot_gate = sb("slot_gate", [P, 1], F32, moe)
        lg = sb("lg", [TT, 3, NE], F32, moe)
        top = sb("top", [TT, 3, 8], F32, moe)
        top_i = sb("top_i", [TT, 3, 8], U32, moe)
        top_f = sb("top_f", [TT, 3, 2], F32, moe)
        gt = sb("gt", [TT, 3, 4], F32, moe)
        hot1 = sb("hot1", [TT, 3, NE], F32, moe)
        hot2 = sb("hot2", [TT, 3, NE], F32, moe)
        hot = sb("hot", [TT, 3, NE], F32, moe)
        gates = sb("gates", [TT, 3, 2, NE], F32, moe)
        posm = sb("posm", [TT, 3, NE], F32, moe)
        posc = sb("posc", [TT, 3, 2, NE], F32, moe)
        POS = sb("POS", [TT, 3, NSEL], F32, moe)
        GT = sb("GT", [TT, 3, NSEL], F32, moe)
        cnt = sb("cnt", [P, NE], F32, moe)
        over = sb("over", [P, 2, NE], F32, moe)
        n_chunks = sb("n_chunks", [P, NE], F32, moe)
        key = sb("key", [P, 2, NE], F32, moe)
        pick = sb("pick", [P, 6, 2 * NE], F32, moe)
        prod = sb("prod", [P, 6, 2 * NE], F32, moe)
        key_sum = sb("key_sum", [P, 1], F32, moe)
        prod3 = sb("prod3", [TT, 3, 2 * NE], F32, moe)
        eids_f = sb("eids_f", [P, 8], F32, moe)
        table_load = sb("table_load", [1, 1], F32, moe)
        eids = sb("eids", [P, 8], I32, moe)

        ps = ctx.enter_context(nc.psum_tensor("ps", [P, 8, 512], F32))
        SUM_BANK, TOKEN_SUMS = ps[:, 6, 0:T], ps[0:TT, 7, 0:3]
        G_, U_, T_, X0, X1, X2 = (ps[:, i, :] for i in (0, 1, 2, 5, 6, 7))
        D_ = ps[:, 3:5, :]

        landed = [sem(f"landed{i}") for i in range(RAW)]
        hi_done, lo_done, w_used = sem("hi_done"), sem("lo_done"), sem("w_used")
        mm_done, evac = sem("mm_done"), sem("evac")
        consts = sem("consts")
        x_landed, par_landed, past_landed = sem("x_landed"), sem("par_landed"), sem("past_landed")
        x_hi_done, x_lo_done = sem("x_hi_done"), sem("x_lo_done")
        sq_ready, sums_done, sums_read = sem("sq_ready"), sem("sums_done"), sem("sums_read")
        ext_zero = sem("ext_zero")
        z_scaled, tanh_done, v_done = sem("z_scaled"), sem("tanh_done"), sem("v_done")
        pooled, pooled_hi, pooled_lo = sem("pooled"), sem("pooled_hi"), sem("pooled_lo")
        m_hi_done = sem("m_hi_done")
        e_hi_done, e_lo_done, y_ready = sem("e_hi_done"), sem("e_lo_done"), sem("y_ready")
        pool_lo_done = sem("pool_lo_done")
        tap_hi_done, tap_lo_done = sem("tap_hi_done"), sem("tap_lo_done")
        diag_hi_done, diag_lo_done, factors_done = sem("diag_hi_done"), sem("diag_lo_done"), sem("factors_done")
        ln_centred, ln_sq = sem("ln_centred"), sem("ln_sq")
        ln_scaled, ln_act, ln_lo = sem("ln_scaled"), sem("ln_act"), sem("ln_lo")
        sq_pair, sq_sum = sem("sq_pair"), sem("sq_sum")
        packed = sem("packed")
        rw_landed, conv_step = sem("rw_landed"), sem("conv_step")
        gate_scaled, silu_done = sem("gate_scaled"), sem("silu_done")
        f_ready, f_hi_done, f_lo_done = sem("f_ready"), sem("f_hi_done"), sem("f_lo_done")
        state_stored = sem("state_stored")
        gb_landed, hn_sq = sem("gb_landed"), sem("hn_sq")
        rwg_done, logits_done, hot_done, ranks_done = sem("rwg_done"), sem("logits_done"), sem("hot_done"), sem("ranks_done")
        gap_done, exp_done, hn_done, hn_hi_done, hn_lo_done = (sem(n) for n in ("gap_done", "exp_done", "hn_done", "hn_hi_done", "hn_lo_done"))
        tok_rstd = sem("tok_rstd")
        routed, extra_done = sem("routed"), sem("extra_done")
        top_done, route_step = sem("top_done"), sem("route_step")
        sel_ready, gather_done, xg_hi_done, xg_lo_done = (sem(n) for n in ("sel_ready", "gather_done", "xg_hi_done", "xg_lo_done"))
        g_done, u_done, e_silu, e_f, t_done, ft_hi_done, ft_lo_done, d_done = (
            sem(n) for n in ("g_done", "u_done", "e_silu", "e_f", "t_done", "ft_hi_done", "ft_lo_done", "d_done"))
        o_hi_done, o_lo_done, comb_done, comb_read = (sem(n) for n in ("o_hi_done", "o_lo_done", "comb_done", "comb_read"))
        selt_done, selt_read = sem("selt_done"), sem("selt_read")
        fin_sq, fin_out, stored = sem("fin_sq"), sem("fin_out"), sem("stored")
        dve_step, act_step, pool_step = sem("dve_step"), sem("act_step"), sem("pool_step")

        def h_group(i, k):
            return GROUP[[("x", k), ("wout", 0, k), ("down", k)][i]] + 1

        def token_pieces():
            out = []
            for name, start, n in (("meta", 0, META), ("prompt", META, SEQ), ("sample", TP, DB * DS)):
                at = start
                while at < start + n:
                    m = min(start + n, (at // TT + 1) * TT) - at
                    out.append((at // TT, at % TT, m, name, at - start))
                    at += m
            return out

        PIECES = token_pieces()
        SRC = {"meta": meta_tokens, "prompt": x_prompt[0], "sample": x_sample.rearrange("a b d -> (a b) d")}
        DST = {"prompt": y_prompt[0], "sample": y_sample.rearrange("a b d -> (a b) d")}

        def samples(ap):
            return ap.rearrange("p (b t) -> p b t", b=DB)

        def state_dsts(l):
            return [(pool_s[l].rearrange("b r d -> (b r) d"), DB * PB),
                    (conv_s[l, 0:HB].rearrange("b r d -> (b r) d"), DB * PB),
                    (conv_s[l, HB:DB].rearrange("b r d -> (b r) d"), DB * PB),
                    (pool_p[l, 0], PB), (conv_p[l, 0], CB)]

        SUMS = {name: i for i, name in enumerate(
            [("norm", 0), ("spread norm", 0), ("mean", 0), ("var", 0), ("spread var", 0), ("norm", 1),
             ("norm", 2), ("spread norm", 2), ("mean", 1), ("var", 1), ("spread var", 1)])}

        def raw_slot(i):
            return raw[:, i % RAW, :]

        def blk(w, k0, nk, c0, nc_):
            return w[k0 * P:(k0 + nk) * P, c0:c0 + nc_].rearrange("(k p) n -> p k n", p=P), nk, nc_

        def dense_slots():
            out = []
            for l in range(L):
                out += [blk(w_in[l], 0, KD, 256 * s, 256) for s in WIN_ORDER[:5]]
                out += [(("diag", l, c, a), z - a, P) for c, halves in zip(PE_TILES, DIAG_PARTS) for a, z in halves]
                out.append(blk(w_in[l], 0, KD, 256 * WIN_ORDER[5], 256))
                out.append((pool_w[l].rearrange("g p n -> p g n"), NG, P))
                out.append(blk(conv_pw_w[l], 0, KC, 0, CW))
                out += [blk(w_out[l], 0, KD, 256 * s, 256) for s in range(4)]
                if l == 0:
                    for u in range(FF // 256):
                        out.append(blk(ffn_w_gate[0], 0, KD, 256 * u, 256))
                        out.append(blk(ffn_w_up[0], 0, KD, 256 * u, 256))
                    for c, parts in enumerate(DOWN_PARTS):
                        k0 = 0
                        for nk in parts:
                            out.append(blk(ffn_w_down[0], k0, nk, 256 * c, 256))
                            k0 += nk
            return out

        SLOTS = dense_slots()
        assert len(SLOTS) == MOE_BASE

        def slot_size(n):
            return SLOTS[n][1] * SLOTS[n][2]

        def is_diag(n):
            return n < MOE_BASE and isinstance(SLOTS[n][0], tuple)

        def loads(n):
            return 16 * sum(not is_diag(m) for m in range(n % RAW, n + 1, RAW))

        POOL_LOW = [MIX_BASE[l] + i for l in range(L) for i in (S_LATE, S_PW)]
        def pooled_at(g):
            k, hi, lo = (4 + g, x_hi, x_lo) if g in POOL_ORDER[2:] else (g - 2, m_hi, m_lo)
            return hi[:, k, :], lo[:, k, :]

        M_ORDER = (*POOL_ORDER[:2], *range(NG, KD), *POOL_ORDER[2:])
        DIAG = {MIX_BASE[l] + S_DIAG + k: (l, k) for l in range(L) for k in range(N_DIAG)}

        def parts(n, size=SLOT):
            return raw[:, n % RAW, 0:size], w_hi[:, n % SPLIT, 0:size], w_lo[:, n % SPLIT, 0:size]

        def dense_used():
            out, n_w = [], 0
            for n in range(MOE_BASE):
                b = next(x for x in (MIX_BASE[1], FFN_BASE, 0) if n >= x)
                if b == FFN_BASE and n >= DOWN_BASE:
                    ends = [sum(len(x) for x in DOWN_PARTS[:c + 1]) - 1 for c in range(4)]
                    if n - DOWN_BASE in ends:
                        out.append((mm_done, GROUP[("down", 2 * ends.index(n - DOWN_BASE) + 1)] + 1))
                    else:
                        n_w += 1
                        out.append((w_used, n_w))
                elif b == FFN_BASE:
                    u, i = divmod(n - b, 2)
                    out.append((mm_done, GROUP[("gu", u, 2 * i + 1)] + 1))
                else:
                    l, i = MIX_BASE.index(b), n - b
                    if S_DIAG <= i < S_LATE and (i - S_DIAG) % 2 == 0:
                        n_w += 1
                        out.append((w_used, n_w))
                        continue
                    last = (("win", l, 2 * WIN_ORDER[i] + 1) if i < S_DIAG else
                            ("conv", l, PE_TILES[(i - S_DIAG) // 2]) if i < S_LATE else
                            ("win", l, 2 * WIN_ORDER[5] + 1) if i == S_LATE else
                            ("pool", l, POOL_ORDER[-1]) if i == S_POOL_W else
                            ("pw", l, KC - 1) if i == S_PW else ("wout", l, 2 * (i - S_OUT) + 1))
                    out.append((mm_done, GROUP[last] + 1))
            return out, n_w

        DENSE_USED, W_BASE = dense_used()
        PASS_USED = [None] * ES
        for j in range(NJ):
            PASS_USED[gate_slot(j) + 1] = (g_done, NJ, j + 1)
            PASS_USED[up_slot(j) + 1] = (u_done, NJ, j + 1)
        PASS_USED[down_slot(NJ - 1) + 1] = (d_done, 1, 2)
        W_PASS = PASS_USED.count(None)
        N_W = 0
        for i in range(ES):
            if PASS_USED[i] is None:
                N_W += 1
                PASS_USED[i] = (w_used, W_PASS, W_BASE + N_W)

        def wait_used_dense(eng, n):
            s, v = DENSE_USED[n]
            eng.wait_ge(s, v)

        def wait_used_pass(eng, p, i):
            s, per, v = PASS_USED[i % ES]
            if i < 0:
                v -= per
            eng.wait_ge(s, p * per + v)

        def split_hi_dense(act, n):
            r, hi, lo = parts(n, slot_size(n))
            if is_diag(n):
                act.wait_ge(hi_done, n)
                act.sem_inc(hi_done, 1)
                l, k = DIAG[n]
                (_, _, c, a), taps, _ = SLOTS[n]
                if k == 0:
                    act.wait_ge(tap_lo_done, 1)
                wait_used_dense(act, n - SPLIT)
                for j in range(taps):
                    at = (l * KC + c) * TAPS + a + j
                    nc.scalar.activation(lo[:, j * P:(j + 1) * P], ident[:], ACT.Copy, scale=tap_lo[:, at:at + 1]
                                         ).then_inc(diag_lo_done, 1)
                return
            act.wait_ge(landed[n % RAW], loads(n))
            if n >= SPLIT:
                wait_used_dense(act, n - SPLIT)
            nc.scalar.activation(hi, r, ACT.Copy).then_inc(hi_done, 1)

        def split_lo_dense(dve, n):
            r, hi, lo = parts(n, slot_size(n))
            if is_diag(n) or n in POOL_LOW:
                dve.wait_ge(lo_done, n)
                if n in POOL_LOW:
                    dve.wait_ge(pool_lo_done, POOL_LOW.index(n) + 1)
                dve.sem_inc(lo_done, 1)
                return
            dve.wait_ge(hi_done, n + 1)
            nc.vector.tensor_tensor(lo, r, hi.bitcast(F32), ALU.subtract).then_inc(lo_done, 1)

        def split_hi_pass(act, p, i):
            n = MOE_BASE + i
            r, hi, _ = parts(n)
            act.wait_ge(landed[n % RAW], p * (16 * ES // RAW) + loads(n))
            wait_used_pass(act, p, i - SPLIT)
            nc.scalar.activation(hi, r, ACT.Copy).then_inc(hi_done, 1)

        def split_lo_pass(dve, p, i):
            r, hi, lo = parts(MOE_BASE + i)
            dve.wait_ge(hi_done, p * ES + (MOE_BASE + i + 1))
            nc.vector.tensor_tensor(lo, r, hi.bitcast(F32), ALU.subtract).then_inc(lo_done, 1)

        block = ctx.enter_context(nc.Block())

        @block.sync
        def _(sp):
            def reuse(n):
                sp.wait_ge(lo_done, n - RAW + 1)

            for t, r, m, name, row in PIECES:
                sp.dma_start(x_tok[r:r + m, t, :], SRC[name][row:row + m, :]).then_inc(x_landed, 16)
            for n, (src, nk, ncol) in enumerate(SLOTS):
                if is_diag(n):
                    continue
                if n >= RAW:
                    reuse(n)
                dst = raw[:, n % RAW, 0:nk * ncol].rearrange("p (k n) -> p k n", k=nk)
                sp.dma_start(dst, src).then_inc(landed[n % RAW], 16)

            def load_expert(p, e):
                for j in range(NJ):
                    todo = [(gate_slot(j) + i, moe_w_gate, i, j) for i in (0, 1)]
                    todo += [(up_slot(j) + i, moe_w_up, i, j) for i in (0, 1)]
                    for jj in ([j - 1] if j else []) + ([j] if j == NJ - 1 else []):
                        todo += [(down_slot(jj) + i, moe_w_down, i, jj) for i in (0, 1)]
                    for i, w, half, jj in todo:
                        reuse(MOE_BASE + ES * p + i)
                        we = w[0, ds(e, 1)]
                        n = MOE_BASE + i
                        if w is moe_w_down:
                            src = we[:, (4 * jj + 2 * half) * P:(4 * jj + 2 * half + 2) * P, :]
                            src = src.rearrange("a (k p) n -> p (a k) n", p=P)
                            dst = raw_slot(n).rearrange("p (k n) -> p k n", k=2)
                        else:
                            src = we[:, 4 * half * P:4 * (half + 1) * P, 512 * jj:512 * (jj + 1)]
                            src = src.rearrange("a (k p) n -> p (a k) n", p=P)
                            dst = raw_slot(n).rearrange("p (k n) -> p k n", k=4)
                        sp.dma_start(dst, src).then_inc(landed[n % RAW], 16)

            with sp.Fori(0, NE) as p:
                load_expert(p, p)
            sp.wait_ge(extra_done, 1)
            n_over = sp.value_load(eids[0:1, 6:7], min_val=0, max_val=5)
            with sp.If(n_over > 0):
                with sp.Fori(0, n_over) as i:
                    e = sp.value_load(eids[0:1, ds(i, 1)], min_val=0, max_val=NE - 1)
                    load_expert(i + NE, e)
                sp.nop()
            n_out = 0
            for t, r, m, name, row in PIECES:
                if name != "meta":
                    sp.wait_ge(fin_out, t + 1)
                    sp.dma_start(DST[name][row:row + m, :], yt[r:r + m, t, :]).then_inc(stored, 16)
                    n_out += 1
            sp.wait_ge(stored, 16 * n_out)
            sp.wait_ge(state_stored, 16 * 5 * L)

        @block.gpsimd
        def _(pool):
            step = [0]

            def link(ins):
                step[0] += 1
                ins.then_inc(pool_step, 1)
                pool.wait_ge(pool_step, step[0])

            link(nc.gpsimd.memset(ident[:], 0.0))
            link(nc.gpsimd.affine_select(out=ident[:], in_=ident[:], compare_op=ALU.not_equal, fill=1.0,
                                         base=0, pattern=[[-1, P]], channel_multiplier=1))
            link(nc.gpsimd.memset(ones[:], 1.0))
            link(nc.gpsimd.memset(before[:], 0.0))
            link(nc.gpsimd.affine_select(out=before[:], in_=before[:], compare_op=ALU.is_ge, fill=1.0,
                                         base=0, pattern=[[-1, P]], channel_multiplier=1))
            link(nc.gpsimd.iota(iota_slot[:], pattern=[[1, P]], base=0, channel_multiplier=0,
                                allow_small_or_imprecise_dtypes=True))
            link(nc.gpsimd.iota(iota_e[:], pattern=[[1, NE]], base=0, channel_multiplier=0,
                                allow_small_or_imprecise_dtypes=True))
            for t in range(16):
                link(nc.gpsimd.memset(inv_cnt[:, t:t + 1], 1.0 / (t + 1)))
            nc.gpsimd.sem_inc(consts, 1)

            def squares(i):
                if i:
                    pool.wait_ge(sums_done, SUMS[("norm", i - 1)] + 1)
                for k in range(KD):
                    pool.wait_ge(evac, h_group(i, k))
                    if k == 0:
                        link(nc.gpsimd.tensor_tensor(sqs, h[:, 0, :], h[:, 0, :], ALU.mult))
                        continue
                    link(nc.gpsimd.tensor_tensor(sq, h[:, k, :], h[:, k, :], ALU.mult))
                    link(nc.gpsimd.tensor_tensor(sqs, sqs, sq, ALU.add))
                pool.sem_inc(sq_ready, 1)

            def diagonals(l, k):
                n = MIX_BASE[l] + S_DIAG + k
                (_, _, c, a), taps, _ = SLOTS[n]
                if k == 0:
                    pool.wait_ge(tap_hi_done, 1)
                wait_used_dense(pool, n - SPLIT)
                at = (l * KC + c) * TAPS + a
                nc.gpsimd.tensor_tensor(
                    w_hi[:, n % SPLIT, 0:taps * P].rearrange("p (k n) -> p k n", k=taps),
                    ident[:].unsqueeze(1).broadcast_to([P, taps, P]),
                    tap_hi[:, at:at + taps].bitcast(F32).unsqueeze(2).broadcast_to([P, taps, P]), ALU.mult
                ).then_inc(diag_hi_done, 1)

            def mixer_layer(l):
                pool.dma_start(state_io[:, 0, :], state_pool[l].rearrange("b r d -> (b r) d")
                               ).then_inc(past_landed, 16)
                for i in (0, 1):
                    pool.dma_start(state_io[:, 1 + i, :],
                                   state_conv[l, HB * i:HB * (i + 1)].rearrange("b r d -> (b r) d")
                                   ).then_inc(past_landed, 16)
                squares(2 * l)
                if l == 0:
                    pool.wait_ge(evac, GROUP[("params",)] + 1)
                link(nc.gpsimd.memset(pool_ext[:, :, 0:PB], 0.0))
                link(nc.gpsimd.memset(conv_ext[:, :, 0:CB], 0.0))
                pool.sem_inc(ext_zero, 1)

                def low(n):
                    r, hi, lo = parts(n, slot_size(n))
                    pool.wait_ge(hi_done, n + 1)
                    nc.gpsimd.tensor_tensor(lo, r, hi.bitcast(F32), ALU.subtract).then_inc(pool_lo_done, 1)

                for g in POOL_ORDER:
                    for k in {2: (0, 1, 2), 3: (3, 4), 0: (5,), 1: ()}[g]:
                        diagonals(l, k)
                    if g == POOL_ORDER[2]:
                        low(POOL_LOW[2 * l])
                        low(POOL_LOW[2 * l + 1])
                    pool.wait_ge(evac, GROUP[("win", l, g)] + 1)
                    src, shift = pool_ext[:, g, :], 1
                    for s in range(g + 1):
                        dst = win_sum[:, s % 2, :]
                        lo = 2 * shift - 1
                        link(nc.gpsimd.tensor_tensor(dst[:, lo:PEXT], src[:, lo:PEXT],
                                                     src[:, lo - shift:PEXT - shift], ALU.add))
                        src, shift = dst, 2 * shift
                    mean, win = win_sum[:, (g + 1) % 2, :], WINDOWS[g]
                    link(nc.gpsimd.tensor_scalar(mean[:, PB:PEXT], src[:, PB:PEXT], 1.0 / win, 0.0,
                                                 ALU.mult, ALU.add))
                    link(nc.gpsimd.tensor_tensor(mean[:, PB:PB + win - 1], src[:, PB:PB + win - 1],
                                                 inv_cnt[:, 0:win - 1], ALU.mult))
                    link(nc.gpsimd.tensor_tensor(y_pool[:, g, 0:TP], mean[:, PB:PSEG], pool_ext[:, g, PB:PSEG],
                                                 ALU.subtract))
                    link(nc.gpsimd.tensor_tensor(samples(y_pool[:, g, TP:T])[:, :, 0:DS],
                                                 samples(mean[:, PSEG:PEXT])[:, :, PB:PS1],
                                                 samples(pool_ext[:, g, PSEG:PEXT])[:, :, PB:PS1], ALU.subtract))
                    pool.sem_inc(pooled, 1)
                pool.wait_ge(ln_lo, KC * (l + 1))
                for g in range(NG):
                    link(nc.gpsimd.tensor_copy(samples(z[:, g, 0:DB * PB]),
                                               samples(pool_ext[:, g, PSEG:PEXT])[:, :, DS:PS1]))
                    link(nc.gpsimd.tensor_copy(samples(y[:, g, 0:DB * CB]),
                                               samples(conv_ext[:, g, CSEG:CEXT])[:, :, DS:CS1]))
                pool.sem_inc(packed, 1)
                if l == 0:
                    squares(1)
                else:
                    pool.wait_ge(mm_done, GROUP[("pool", 1, POOL_ORDER[-1])] + 1)
                    for i, g in enumerate((norm2_g[1:2, :], final_norm_g.rearrange("(a d) -> a d", a=1))):
                        pool.dma_start(gb[:, i, :], g.broadcast_to([TT, D])
                                       ).then_inc(gb_landed, 16)
                    pool.wait_ge(gb_landed, 32)
                    pool.wait_ge(gb_landed, 32)
                    for t in range(3):
                        pool.wait_ge(hn_sq, 6)
                        nc.gpsimd.tensor_tensor(hn[:, t, :], yt[:, t, :], gb[:, 0, :], ALU.mult).then_inc(hn_done, 1)
                for i, (dst, rows) in enumerate(state_dsts(l)):
                    pool.wait_ge(evac, GROUP[("state", l, i)] + 1)
                    pool.dma_start(dst, state_io[0:rows, i, :]).then_inc(state_stored, 16)

            mixer_layer(0)
            pool.wait_ge(state_stored, 16 * 5)
            mixer_layer(1)

            def fold(x, out):
                n = 2 * NE
                while n > 2:
                    n //= 2
                    link(nc.gpsimd.tensor_tensor(x[:, :, 0:n], x[:, :, 0:n], x[:, :, n:2 * n], ALU.add))
                link(nc.gpsimd.tensor_tensor(out, x[:, :, 0], x[:, :, 1], ALU.add))

            pool.wait_ge(routed, 1)
            for c in (0, 1):
                link(nc.gpsimd.tensor_scalar(over[:, c, :], cnt[:], float(P * (c + 1)), None, ALU.is_gt))
            link(nc.gpsimd.tensor_tensor(n_chunks[:], over[:, 0, :], over[:, 1, :], ALU.add))
            link(nc.gpsimd.memset(key[:, 0, 0:1], 0.0))
            for e in range(1, NE):
                link(nc.gpsimd.tensor_tensor(key[:, 0, e:e + 1], key[:, 0, e - 1:e], n_chunks[:, e - 1:e], ALU.add))
            link(nc.gpsimd.tensor_copy(key_sum[:], key[:, 0, NE - 1:NE]))
            link(nc.gpsimd.tensor_scalar(key[:, 1, :], key[:, 0, :], 2.0, None, ALU.add))
            link(nc.gpsimd.tensor_scalar(key[:, 0, :], key[:, 0, :], 1.0, None, ALU.add))
            link(nc.gpsimd.tensor_tensor(key[:], key[:], over[:], ALU.mult))
            flat = key[:].rearrange("p c e -> p (c e)")
            for i in range(6):
                link(nc.gpsimd.tensor_scalar(pick[:, i, :], flat, float(i + 1), None, ALU.is_equal))
            for i in range(6):
                for c in (0, 1):
                    link(nc.gpsimd.tensor_tensor(prod[:, i, NE * c:NE * (c + 1)], pick[:, i, NE * c:NE * (c + 1)],
                                                 iota_e[:], ALU.mult))
            fold(prod, eids_f[:, 0:6])
            link(nc.gpsimd.tensor_tensor(eids_f[:, 6:7], key_sum[:], n_chunks[:, NE - 1:NE], ALU.add))
            link(nc.gpsimd.tensor_copy(eids[:, 0:7], eids_f[:, 0:7]))
            for c in (0, 1):
                link(nc.gpsimd.tensor_scalar(posc[:, :, c, :], posm[:], 1.0 - P * (c + 1), None, ALU.add))
            for i in range(6):
                for src, dst in ((posc, POS), (gates, GT)):
                    for t in range(3):
                        link(nc.gpsimd.tensor_tensor(prod3[:, t, :], src[:, t].rearrange("p c e -> p (c e)"),
                                                     pick[0:TT, i, :], ALU.mult))
                    fold(prod3, dst[:, :, NE + i])
            link(nc.gpsimd.tensor_scalar(POS[:, :, NE:NSEL], POS[:, :, NE:NSEL], -1.0, None, ALU.add))
            pool.sem_inc(extra_done, 1)

        def splitter(eng, split):
            at = [0]

            def to(n):
                while at[0] <= min(n, MOE_BASE - 1):
                    split(eng, at[0])
                    at[0] += 1

            return to, at

        FU = FF // 256
        LOOPS = FU // 3
        GU0 = GROUP[("gu", 0, 0)]

        def gu_bank(uu, x):
            return ps[:, (GU0 + 4 * uu + x) % MM_BANKS, 0:T]

        def split_hi_gu(act, i, s):
            r, hi, _ = parts(FFN_BASE + s)
            act.wait_ge(landed[(FFN_BASE + s) % RAW], i * 16 + loads(FFN_BASE + s))
            act.wait_ge(mm_done, i * 12 + (GU0 + 2 * (s - SPLIT + 1)))
            nc.scalar.activation(hi, r, ACT.Copy).then_inc(hi_done, 1)

        def split_lo_gu(dve, i, s):
            r, hi, lo = parts(FFN_BASE + s)
            dve.wait_ge(hi_done, i * 6 + (FFN_BASE + s + 1))
            nc.vector.tensor_tensor(lo, r, hi.bitcast(F32), ALU.subtract).then_inc(lo_done, 1)

        @block.scalar
        def _(act):
            split_to, split_at = splitter(act, split_hi_dense)
            step = [0]

            for (at, n), w in ((NG1, norm1_g), (NG2, norm2_g), (PSC, pool_scale), (DWB, conv_dw_b),
                               (LNG, conv_ln_g), (LNB, conv_ln_b)):
                act.dma_start(par_rows[at:at + L * n, :], w.rearrange("l (k p) -> (l k) p", p=P)
                              ).then_inc(par_landed, 16)
            act.dma_start(dw_rows[:], conv_dw_w.rearrange("l t c -> t l c")).then_inc(par_landed, 16)
            act.dma_start(rw[:], router_w[0].rearrange("(k p) e -> p k e", p=P)).then_inc(rw_landed, 16)

            def x_hi_parts(i, l, which, ks=range(KD)):
                for k in ks:
                    if k == 0:
                        act.wait_ge(evac, max(h_group(i, 0), GROUP[("params",)] + 1))
                    act.wait_ge(evac, h_group(i, k))
                    nc.scalar.activation(x_hi[:, k, :], h[:, k, :], ACT.Copy, scale=col(l, which, k)
                                         ).then_inc(x_hi_done, 1)

            def mixer_layer(l):
                b = MIX_BASE[l]
                if l == 0:
                    x_hi_parts(0, 0, NG1)
                    nc.scalar.activation(tap_hi[:], params[:, 64:], ACT.Copy).then_inc(tap_hi_done, 1)
                split_to(b + 2)
                for half in (0, 1):
                    split_to(b + (S_DIAG if half else 3))
                    for i in (0, 1):
                        c = 2 * half + i
                        act.wait_ge(z_scaled, KC * l + c + 1)
                        nc.scalar.activation(z[:, 2 + i, :], z[:, 2 + i, :], ACT.Tanh, scale=0.5
                                             ).then_inc(tanh_done, 1)
                    act.wait_ge(ext_zero, l + 1)
                    for q, c in enumerate(PE_TILES):
                        if c // 2 == half:
                            act.wait_ge(v_done, 8 * l + 2 * c + 1)
                            nc.scalar.activation(e_hi[:, q, :], conv_ext[:, c, 0:CSEG], ACT.Copy
                                                 ).then_inc(e_hi_done, 1)

                def pooled_high(g):
                    q = POOL_ORDER.index(g)
                    act.wait_ge(pooled, NG * l + q + 1)
                    nc.scalar.activation(pooled_at(g)[0], y_pool[:, g, :], ACT.Copy).then_inc(pooled_hi, 1)

                def m_high(name, k, scale):
                    act.wait_ge(mm_done, GROUP[name] + 1)
                    nc.scalar.activation(m_hi[:, k, :], ps[:, GROUP[name] % MM_BANKS, 0:T], ACT.Copy, scale=scale
                                         ).then_inc(m_hi_done, 1)

                split_to(b + S_DIAG + 3)
                pooled_high(POOL_ORDER[0])
                split_to(b + S_DIAG + 5)
                pooled_high(POOL_ORDER[1])
                split_to(b + S_PW)
                for c in range(KC):
                    act.wait_ge(ln_centred, KC * l + c + 1)
                    nc.scalar.activation(z[:, c, :], y[:, c, :], ACT.Square).then_inc(ln_sq, 1)
                for c in range(KC):
                    act.wait_ge(ln_scaled, KC * l + c + 1)
                    step[0] += 1
                    nc.scalar.activation(z[:, c, :], y[:, c, :], ACT.Silu, scale=col(l, LNG, c), bias=col(l, LNB, c)
                                         ).then_inc(act_step, 1)
                    act.wait_ge(act_step, step[0])
                    if c == 0:
                        act.wait_ge(mm_done, GROUP[("win", l, 2 * WIN_ORDER[-1] + 1)] + 1)
                    nc.scalar.activation(x_hi[:, c, :], z[:, c, :], ACT.Copy).then_inc(ln_act, 1)
                for g in POOL_ORDER[:2]:
                    m_high(("pool", l, g), g, col(l, PSC, g))
                split_to(b + S_OUT)
                pooled_high(POOL_ORDER[2])
                for m in range(KC):
                    if m == KC - 1:
                        pooled_high(POOL_ORDER[3])
                    m_high(("pw", l, m), NG + m, 1.0)
                for g in POOL_ORDER[2:]:
                    m_high(("pool", l, g), g, col(l, PSC, g))
                for s in range(4):
                    split_to(b + S_OUT + 2 + s)
                    if l == 0:
                        x_hi_parts(1, 0, NG2, (2 * s, 2 * s + 1))

            split_to(0)
            mixer_layer(0)


            def gate_up(i, uu, split):
                u = i * 3 + uu
                split(2 * uu + 2)
                for x in (0, 1):
                    act.wait_ge(gate_scaled, u * 2 + (x + 1))
                    nc.scalar.activation(gs[:, x, :], gs[:, x, :], ACT.Silu).then_inc(silu_done, 1)
                split(2 * uu + 3)
                for x in (0, 1):
                    act.wait_ge(f_ready, u * 2 + (x + 1))
                    nc.scalar.activation(f_hi[:, ds(u * 2 + x, 1), :], us[:, x:x + 1, :], ACT.Copy
                                         ).then_inc(f_hi_done, 1)

            with act.Fori(0, LOOPS) as i:
                for uu in range(3):
                    gate_up(i, uu, lambda s, i=i: split_hi_gu(act, i, s))
            split_at[0] = FFN_BASE + 6 * LOOPS + 2
            for uu in range(FU - 3 * LOOPS):
                gate_up(LOOPS, uu, lambda s: split_to(FFN_BASE + 6 * LOOPS + s))
            n = DOWN_BASE
            for c, ks in enumerate(DOWN_PARTS):
                for _ in ks:
                    split_to(n + 2)
                    n += 1
                x_hi_parts(2, 1, NG1, (2 * c, 2 * c + 1))
            mixer_layer(1)

            def token_squares(tiles, ready, done):
                for t, i in tiles:
                    ready(t, i)
                    q = 3 * i + t
                    nc.scalar.activation(hn[:, q // 2, 512 * (q % 2):512 * (q % 2 + 1)], yt[:, t, 512 * i:512 * (i + 1)],
                                         ACT.Square, accum_out=nt[0:TT, t, 2 + i:3 + i]).then_inc(done, 1)

            token_squares([(t, i) for i in (0, 1) for t in range(3)],
                          lambda t, i: act.wait_ge(evac, GROUP[("htok", t, i)] + 1), hn_sq)
            act.wait_ge(evac, GROUP[("state", 1, 0)])
            for i, (_, rows) in enumerate(state_dsts(1)):
                q = GROUP[("state", 1, i)]
                act.wait_ge(mm_done, q + 1)
                nc.scalar.activation(state_io[0:rows, i, :], ps[0:rows, q % MM_BANKS, :], ACT.Copy).then_inc(evac, 1)
            act.wait_ge(tok_rstd, 1)
            for t in range(3):
                act.wait_ge(hn_done, t + 1)
                nc.scalar.activation(hn_hi[:, t, :], hn[:, t, :], ACT.Copy, scale=nt[0:TT, t, 1:2]).then_inc(hn_hi_done, 1)
            act.wait_ge(gap_done, 1)
            nc.scalar.activation(gt[:, :, 1], gt[:, :, 0], ACT.Exp).then_inc(exp_done, 1)

            def gathered_hi(p):
                act.wait_ge(gather_done, p * 2 + 2)
                for i, x in enumerate((X0, X1)):
                    nc.scalar.activation(xg_hi[:, 4 * i:4 * i + 4, :], x.rearrange("p (k s) -> p k s", k=4), ACT.Copy
                                         ).then_inc(xg_hi_done, 1)

            def out_hi(p):
                act.wait_ge(d_done, p + 1)
                act.wait_ge(selt_read, p * 2 + 2)
                act.wait_ge(comb_read, p * 6 + 1)
                for i in (0, 1):
                    nc.scalar.activation(o_hi[:, 512 * i:512 * (i + 1)], D_[:, i, :], ACT.Copy, scale=slot_gate[:, 0:1]
                                         ).then_inc(o_hi_done, 1)

            def expert_pass(p):
                def after(i):
                    for j in range(NJ):
                        c = p * NJ + j
                        if i == gate_slot(j) + 1:
                            act.wait_ge(g_done, c + 1)
                            act.wait_ge(e_f, c + 1)
                            nc.scalar.activation(act_s[:], G_, ACT.Silu).then_inc(e_silu, 1)
                        if i == (up_slot(0) + 1 if j == 0 else down_slot(j - 1) + 1):
                            act.wait_ge(t_done, c + 2)
                            nc.scalar.activation(ft_hi[:], T_.rearrange("p (k s) -> p k s", k=4), ACT.Copy
                                                 ).then_inc(ft_hi_done, 1)
                    if i == 0:
                        out_hi(p)

                nc.scalar.activation(table_load[:], ones[0:1, 0:1], ACT.Silu)
                for i in range(ES):
                    split_hi_pass(act, p, i)
                    if i == 0:
                        gathered_hi(p)
                    else:
                        after(i - 2)

            with act.Fori(0, NE) as p:
                expert_pass(p)
            act.wait_ge(extra_done, 1)
            n_over = act.value_load(eids[0:1, 6:7], min_val=0, max_val=5)
            with act.If(n_over > 0):
                with act.Fori(0, n_over) as i:
                    expert_pass(i + NE)
                act.nop()
            n_pass = n_over + NE
            out_hi(n_pass)
            token_squares([(t, i) for t in range(3) for i in (0, 1)],
                          lambda t, i: act.wait_ge(comb_read, n_pass * 6 + (2 * t + i + 2)), fin_sq)

        @block.vector
        def _(dve):
            split_to, split_at = splitter(dve, split_lo_dense)
            step = [0]

            def link(ins):
                step[0] += 1
                ins.then_inc(dve_step, 1)
                dve.wait_ge(dve_step, step[0])

            def bank(name):
                return ps[:, GROUP[name] % MM_BANKS, :]

            def made(name):
                dve.wait_ge(mm_done, GROUP[name] + 1)

            def rsqrt(a, yy, tt):
                link(nc.vector.tensor_scalar(yy.bitcast(I32), a.bitcast(I32), 1, None, ALU.logical_shift_right))
                link(nc.vector.tensor_scalar(yy.bitcast(I32), yy.bitcast(I32), -1.0, RSQRT_SEED, ALU.mult, ALU.add))
                for _ in range(3):
                    link(nc.vector.tensor_tensor(tt, yy, yy, ALU.mult))
                    link(nc.vector.scalar_tensor_tensor(tt, tt, -0.5, a, ALU.mult, ALU.mult))
                    link(nc.vector.scalar_tensor_tensor(yy, tt, 1.5, yy, ALU.add, ALU.mult))

            def rstd_from_sum(name, n, eps):
                dve.wait_ge(sums_done, SUMS[name] + 1)
                link(nc.vector.tensor_scalar(nrm_a, SUM_BANK, 1.0 / n, eps, ALU.mult, ALU.add))
                dve.sem_inc(sums_read, 1)
                rsqrt(nrm_a, rstd[:], nrm_t)

            def rstd_by_token(name, n, eps):
                dve.wait_ge(sums_done, SUMS[name] + 1)
                link(nc.vector.tensor_scalar(nt[0:TT, :, 0], TOKEN_SUMS, 1.0 / n, eps, ALU.mult, ALU.add))
                dve.sem_inc(sums_read, 1)
                rsqrt(nt[0:TT, :, 0], nt[0:TT, :, 1], nt[0:TT, :, 2])
                nc.vector.tensor_tensor(spread_in.rearrange("p (t n) -> p t n", t=3),
                                        ident[0:TT, 0:TT].unsqueeze(1).broadcast_to([TT, 3, TT]),
                                        nt[0:TT, :, 1:2].broadcast_to([TT, 3, TT]), ALU.mult
                                        ).then_inc(factors_done, 1)

            def x_lo_parts(i, l, which, ks=range(KD)):
                for k in ks:
                    dve.wait_ge(x_hi_done, KD * i + k + 1)
                    nc.vector.scalar_tensor_tensor(x_lo[:, k, :], h[:, k, :], col(l, which, k),
                                                   x_hi[:, k, :].bitcast(F32), ALU.mult, ALU.subtract
                                                   ).then_inc(x_lo_done, 1)

            for k in range(KD):
                made(("x", k))
                nc.vector.tensor_copy(h[:, k, :], bank(("x", k))[:, 0:T]).then_inc(evac, 1)
            split_to(0)
            made(("params",))
            n_par = 64 + L * KC * TAPS
            nc.vector.tensor_copy(params[:], bank(("params",))[:, 0:n_par]).then_inc(evac, 1)
            dve.wait_ge(evac, GROUP[("params",)] + 1)

            def mixer_layer(l):
                b = MIX_BASE[l]

                def conv(chains, taps):
                    for j in taps:
                        for c, pr in chains:
                            if pr:
                                src, dst = conv_ext[:, c, j:j + TP], y[:, c, 0:TP]
                            else:
                                src = samples(conv_ext[:, c, CSEG:CEXT])[:, :, j:j + DS]
                                dst = samples(y[:, c, TP:T])
                            if j == (PE_TAPS[-1] if pr and c == PE_TILES[-1] else 0):
                                ins = nc.vector.tensor_scalar(dst, src, tap(l, c, j), col(l, DWB, c), ALU.mult, ALU.add)
                            else:
                                dve.wait_ge(conv_step, conv_n[0] - len(chains) + 1)
                                ins = nc.vector.scalar_tensor_tensor(dst, src, tap(l, c, j), dst, ALU.mult, ALU.add)
                            ins.then_inc(conv_step, 1)
                            conv_n[0] += 1

                OWN = [(DVE_TILE, True), (DVE_TILE, False), (PE_TILES[0], False)]
                OTHERS = [(PE_TILES[1], False), (PE_TILES[2], False)]
                if l == 0:
                    x_lo_parts(0, 0, NG1)
                split_to(b + 1)
                if l == 0:
                    dve.wait_ge(tap_hi_done, 1)
                    nc.vector.tensor_tensor(tap_lo[:], params[:, 64:], tap_hi[:].bitcast(F32), ALU.subtract
                                            ).then_inc(tap_lo_done, 1)
                    dve.wait_ge(rw_landed, 16)
                    for k in range(KD):
                        nc.vector.tensor_scalar(rwg[:, k, :], rw[:, k, :], col(1, NG2, k), None, ALU.mult).then_inc(rwg_done, 1)
                split_to(b + 2)
                rstd_by_token(("norm", 2 * l), D, 1e-6)
                split_to(b + 3)
                dve.wait_ge(sums_done, SUMS[("spread norm", 2 * l)] + 1)
                link(nc.vector.tensor_copy(rstd[:], SUM_BANK))
                dve.sem_inc(sums_read, 1)
                for half in (0, 1):
                    s0 = 2 * half
                    split_to(b + s0 + 2)
                    if half:
                        conv(OWN, range(0, 4))
                    for i in (0, 1):
                        g = ("win", l, 2 * WIN_ORDER[s0] + i)
                        made(g)
                        nc.vector.scalar_tensor_tensor(z[:, i, :], bank(g)[:, 0:T], 0.5, rstd[:], ALU.mult, ALU.mult
                                                       ).then_inc(evac, 1)
                    split_to(b + s0 + 3)
                    if half:
                        conv(OWN, range(4, 8))
                    for i in (0, 1):
                        g = ("win", l, 2 * WIN_ORDER[s0 + 1] + i)
                        made(g)
                        link(nc.vector.tensor_tensor(z[:, 2 + i, :], bank(g)[:, 0:T], rstd[:], ALU.mult))
                        dve.sem_inc(z_scaled, 1)
                        dve.sem_inc(evac, 1)
                    if half == 0:
                        made(("past_pool", l))
                        nc.vector.tensor_copy(
                            pool_ext[:, :, PSEG:PEXT].rearrange("p g (b t) -> p g b t", b=DB)[:, :, :, 0:PB],
                            bank(("past_pool", l))[:, 0:NG * DB * PB].rearrange("p (g b t) -> p g b t", g=NG, b=DB)
                        ).then_inc(evac, 1)
                        for i in (0, 1):
                            made(("past_conv", l, i))
                            nc.vector.tensor_copy(
                                conv_ext[:, 2 * i:2 * i + 2, CSEG:CEXT].rearrange("p g (b t) -> p g b t", b=DB)[:, :, :, 0:CB],
                                bank(("past_conv", l, i))[:, 0:2 * DB * CB].rearrange("p (g b t) -> p g b t", g=2, b=DB)
                            ).then_inc(evac, 1)
                        dve.wait_ge(ext_zero, l + 1)
                    for i in (0, 1):
                        c = 2 * half + i
                        dve.wait_ge(tanh_done, KC * l + c + 1)
                        nc.vector.scalar_tensor_tensor(conv_ext[:, c, CB:CSEG], z[:, 2 + i, 0:TP], 1.0, z[:, i, 0:TP],
                                                       ALU.add, ALU.mult).then_inc(v_done, 1)
                        nc.vector.scalar_tensor_tensor(samples(conv_ext[:, c, CSEG:CEXT])[:, :, CB:CS1],
                                                       samples(z[:, 2 + i, TP:T]), 1.0, samples(z[:, i, TP:T]),
                                                       ALU.add, ALU.mult).then_inc(v_done, 1)
                    dve.wait_ge(v_done, 8 * l + 4 * (half + 1))
                    dve.wait_ge(evac, GROUP[("past_conv", l, 1)] + 1)
                    for q, c in enumerate(PE_TILES):
                        if c // 2 == half:
                            dve.wait_ge(e_hi_done, len(PE_TILES) * l + q + 1)
                            nc.vector.tensor_tensor(e_lo[:, q, :], conv_ext[:, c, 0:CSEG], e_hi[:, q, :].bitcast(F32),
                                                    ALU.subtract).then_inc(e_lo_done, 1)

                def pool_in(s, i):
                    g = 2 * WIN_ORDER[s] + i
                    made(("win", l, g))
                    link(nc.vector.tensor_tensor(pool_ext[:, g, PB:PSEG], bank(("win", l, g))[:, 0:TP],
                                                 rstd[:, 0:TP], ALU.mult))
                    nc.vector.tensor_tensor(samples(pool_ext[:, g, PSEG:PEXT])[:, :, PB:PS1],
                                            samples(bank(("win", l, g))[:, TP:T]), samples(rstd[:, TP:T]),
                                            ALU.mult).then_inc(evac, 1)

                def conv_from_pe(c):
                    made(("conv", l, c))
                    if c == PE_TILES[-1]:
                        link(nc.vector.tensor_tensor(y[:, c, 0:TP], bank(("conv", l, c))[:, 0:TP], y[:, c, 0:TP], ALU.add))
                    else:
                        link(nc.vector.tensor_scalar(y[:, c, 0:TP], bank(("conv", l, c))[:, 0:TP], col(l, DWB, c), None,
                                                     ALU.add))
                    dve.sem_inc(evac, 1)
                    dve.sem_inc(y_ready, 1)

                split_to(b + S_DIAG + 1)
                conv(OWN, range(8, 12))
                for i in (0, 1):
                    pool_in(4, i)
                conv(OWN, range(12, TAPS))
                dve.wait_ge(conv_step, conv_n[0])
                dve.sem_inc(y_ready, 1)
                split_to(b + S_LATE - 1)
                conv_from_pe(PE_TILES[0])

                def pooled_low(g):
                    hi, lo = pooled_at(g)
                    dve.wait_ge(pooled_hi, NG * l + POOL_ORDER.index(g) + 1)
                    nc.vector.tensor_tensor(lo, y_pool[:, g, :], hi.bitcast(F32), ALU.subtract).then_inc(pooled_lo, 1)

                def m_low(name, k, scale=None):
                    dve.wait_ge(m_hi_done, KD * l + M_ORDER.index(k) + 1)
                    src, hi = bank(name)[:, 0:T], m_hi[:, k, :].bitcast(F32)
                    ins = (nc.vector.tensor_tensor(m_lo[:, k, :], src, hi, ALU.subtract) if scale is None else
                           nc.vector.scalar_tensor_tensor(m_lo[:, k, :], src, scale, hi, ALU.mult, ALU.subtract))
                    ins.then_inc(evac, 1)

                conv(OTHERS, range(PE_TAPS[-1]))
                dve.wait_ge(conv_step, conv_n[0])
                conv(OTHERS + [(PE_TILES[-1], True)], range(PE_TAPS[-1], TAPS))
                dve.wait_ge(conv_step, conv_n[0])
                conv_from_pe(PE_TILES[1])
                conv_from_pe(PE_TILES[2])
                split_to(b + S_POOL_W)
                dve.wait_ge(sums_done, SUMS[("mean", l)] + 1)
                for c in range(KC):
                    nc.vector.scalar_tensor_tensor(y[:, c, :], SUM_BANK, -1.0 / CW, y[:, c, :], ALU.mult, ALU.add
                                                   ).then_inc(ln_centred, 1)
                dve.wait_ge(ln_centred, KC * (l + 1))
                dve.sem_inc(sums_read, 1)
                for c in (0, 2):
                    dve.wait_ge(ln_sq, KC * l + c + 2)
                    nc.vector.tensor_tensor(z[:, c, :], z[:, c, :], z[:, c + 1, :], ALU.add).then_inc(sq_pair, 1)
                dve.wait_ge(sq_pair, 2 * l + 2)
                nc.vector.tensor_tensor(z[:, 0, :], z[:, 0, :], z[:, 2, :], ALU.add).then_inc(sq_sum, 1)
                for g in POOL_ORDER[:2]:
                    pooled_low(g)
                rstd_by_token(("var", l), CW, 1e-5)
                pool_in(5, 0)
                split_to(b + S_PW)
                dve.wait_ge(sums_done, SUMS[("spread var", l)] + 1)
                for c in range(KC):
                    nc.vector.tensor_tensor(y[:, c, :], y[:, c, :], SUM_BANK, ALU.mult).then_inc(ln_scaled, 1)
                pool_in(5, 1)
                for c in range(KC):
                    dve.wait_ge(ln_act, KC * l + c + 1)
                    nc.vector.tensor_tensor(x_lo[:, c, :], z[:, c, :], x_hi[:, c, :].bitcast(F32), ALU.subtract
                                            ).then_inc(ln_lo, 1)
                dve.sem_inc(sums_read, 1)
                for g in POOL_ORDER[:2]:
                    m_low(("pool", l, g), g, col(l, PSC, g))
                split_to(b + S_OUT)
                pooled_low(POOL_ORDER[2])
                for m in range(KC):
                    if m == KC - 1:
                        pooled_low(POOL_ORDER[3])
                    m_low(("pw", l, m), NG + m)
                for g in POOL_ORDER[2:]:
                    m_low(("pool", l, g), g, col(l, PSC, g))
                split_to(b + S_OUT + 1)
                for s in range(4):
                    for i in (0, 1):
                        m = 2 * s + i
                        made(("wout", l, m))
                        nc.vector.tensor_tensor(h[:, m, :], h[:, m, :], bank(("wout", l, m))[:, 0:T], ALU.add
                                                ).then_inc(evac, 1)
                    if l == 1 and m in HALF_DONE:
                        i = HALF_DONE.index(m)
                        for t in range(3):
                            made(("htok", t, i))
                            nc.vector.tensor_copy(yt[:, t, 512 * i:512 * (i + 1)], bank(("htok", t, i))[0:TT, :]
                                                  ).then_inc(evac, 1)
                    if s < 3:
                        split_to(b + S_OUT + 2 + s)
                    if l == 0:
                        x_lo_parts(1, 0, NG2, (2 * s, 2 * s + 1))
                if l == 0:
                    for i, (_, rows) in enumerate(state_dsts(0)):
                        made(("state", 0, i))
                        nc.vector.tensor_copy(state_io[0:rows, i, :], bank(("state", 0, i))[0:rows, :]).then_inc(evac, 1)
                split_to(b + S_OUT + 5)

            conv_n = [0]
            mixer_layer(0)

            rstd_from_sum(("norm", 1), D, 1e-6)

            def gate_up(i, uu, split):
                u = i * 3 + uu
                split(2 * uu + 2)
                for x in (0, 1):
                    dve.wait_ge(mm_done, u * 4 + (GU0 + x + 1))
                    nc.vector.tensor_tensor(gs[:, x, :], gu_bank(uu, x), rstd[:], ALU.mult).then_inc(gate_scaled, 1)
                dve.wait_ge(gate_scaled, u * 2 + 2)
                dve.sem_inc(evac, 2)
                split(2 * uu + 3)
                for x in (0, 1):
                    dve.wait_ge(mm_done, u * 4 + (GU0 + x + 3))
                    nc.vector.tensor_tensor(us[:, x, :], gu_bank(uu, 2 + x), rstd[:], ALU.mult).then_inc(evac, 1)
                dve.wait_ge(evac, u * 4 + (GU0 + 4))
                for x in (0, 1):
                    dve.wait_ge(silu_done, u * 2 + (x + 1))
                    nc.vector.tensor_tensor(us[:, x, :], us[:, x, :], gs[:, x, :], ALU.mult).then_inc(f_ready, 1)
                for x in (0, 1):
                    dve.wait_ge(f_hi_done, u * 2 + (x + 1))
                    nc.vector.tensor_tensor(f_lo[:, ds(u * 2 + x, 1), :], us[:, x:x + 1, :],
                                            f_hi[:, ds(u * 2 + x, 1), :].bitcast(F32), ALU.subtract
                                            ).then_inc(f_lo_done, 1)

            with dve.Fori(0, LOOPS) as i:
                for uu in range(3):
                    gate_up(i, uu, lambda s, i=i: split_lo_gu(dve, i, s))
            split_at[0] = FFN_BASE + 6 * LOOPS + 2
            for uu in range(FU - 3 * LOOPS):
                gate_up(LOOPS, uu, lambda s: split_to(FFN_BASE + 6 * LOOPS + s))
            n = DOWN_BASE
            for c, ks in enumerate(DOWN_PARTS):
                for part in range(len(ks)):
                    split_to(n + 2)
                    n += 1
                    if part == 1 and c:
                        x_lo_parts(2, 1, NG1, (2 * c - 2, 2 * c - 1))
                for i in (0, 1):
                    name = ("down", 2 * c + i)
                    made(name)
                    hh = h[:, 2 * c + i, :]
                    nc.vector.tensor_tensor(hh, hh, bank(name)[:, 0:T], ALU.add).then_inc(evac, 1)
            x_lo_parts(2, 1, NG1, (KD - 2, KD - 1))
            mixer_layer(1)

            def rstd_tokens():
                link(nc.vector.tensor_tensor(nt[0:TT, :, 3], nt[0:TT, :, 3], nt[0:TT, :, 2], ALU.add))
                link(nc.vector.tensor_scalar(nt[0:TT, :, 0], nt[0:TT, :, 3], 1.0 / D, 1e-6, ALU.mult, ALU.add))
                rsqrt(nt[0:TT, :, 0], nt[0:TT, :, 1], nt[0:TT, :, 2])

            def over_experts(ap):
                return ap.unsqueeze(2).broadcast_to([TT, 3, NE])

            dve.wait_ge(hn_sq, 6)
            rstd_tokens()
            dve.sem_inc(tok_rstd, 1)
            dve.wait_ge(logits_done, 1)
            link(nc.vector.tensor_tensor(lg[:], ps[0:TT, 6, 0:3 * NE].rearrange("p (t e) -> p t e", t=3),
                                         over_experts(nt[0:TT, :, 1]), ALU.mult))
            for t in range(3):
                ins = nc.vector.max(out=top[:, t, :], in_=lg[:, t, :])
                if t < 2:
                    ins.then_inc(top_done, 1)
                else:
                    link(ins)
            dve.wait_ge(top_done, 2)
            nc.vector.tensor_tensor(gt[:, :, 0], top[:, :, 1], top[:, :, 0], ALU.subtract).then_inc(gap_done, 1)
            for t in range(3):
                nc.vector.max_index(out=top_i[:, t, :], in_max=top[:, t, :], in_values=lg[:, t, :]).then_inc(top_done, 1)
            dve.wait_ge(top_done, 5)
            link(nc.vector.tensor_copy(top_f[:], top_i[:, :, 0:2]))
            experts = iota_e[0:TT].unsqueeze(1).broadcast_to([TT, 3, NE])
            link(nc.vector.tensor_tensor(hot1[:], experts, over_experts(top_f[:, :, 0]), ALU.is_equal))
            link(nc.vector.tensor_tensor(hot2[:], experts, over_experts(top_f[:, :, 1]), ALU.is_equal))
            nc.vector.tensor_tensor(hot[:], hot1[:], hot2[:], ALU.add).then_inc(hot_done, 1)
            dve.wait_ge(hot_done, 1)
            made(("state", 1, 4))

            def hn_low(t):
                dve.wait_ge(hn_hi_done, t + 1)
                nc.vector.scalar_tensor_tensor(hn_lo[:, t, :], hn[:, t, :], nt[0:TT, t, 1:2], hn_hi[:, t, :].bitcast(F32),
                                               ALU.mult, ALU.subtract).then_inc(hn_lo_done, 1)

            hn_low(0)
            hn_low(1)
            dve.wait_ge(ranks_done, 1)
            link(nc.vector.scalar_tensor_tensor(posm[:].rearrange("p t e -> p (t e)"), ps[0:TT, 7, 0:3 * NE], 1.0,
                                                hot[:].rearrange("p t e -> p (t e)"), ALU.add, ALU.mult))
            link(nc.vector.tensor_scalar(posm[:], posm[:], -1.0, None, ALU.add))
            link(nc.vector.tensor_copy(POS[:, :, 0:NE], posm[:]))

            def select(p):
                for t in range(3):
                    nc.vector.tensor_scalar(sel[:, t, :], iota_slot[0:TT, :], POS[:, t, ds(p, 1)], None, ALU.is_equal
                                            ).then_inc(sel_ready, 1)

            select(0)
            hn_low(2)
            dve.wait_ge(evac, N_GROUPS)
            nc.vector.memset(sel_t[:].bitcast(F32), 0.0).then_inc(route_step, 1)
            nc.vector.memset(slot_gate[:], 0.0).then_inc(route_step, 1)
            nc.vector.memset(D_, 0.0).then_inc(route_step, 1)
            dve.wait_ge(exp_done, 1)
            link(nc.vector.tensor_scalar(gt[:, :, 2], gt[:, :, 1], 1.0, None, ALU.add))
            link(nc.vector.reciprocal(gt[:, :, 2], gt[:, :, 2]))
            link(nc.vector.tensor_tensor(gt[:, :, 3], gt[:, :, 1], gt[:, :, 2], ALU.mult))
            link(nc.vector.tensor_tensor(gates[:, :, 0, :], hot1[:], over_experts(gt[:, :, 2]), ALU.mult))
            link(nc.vector.tensor_tensor(gates[:, :, 1, :], hot2[:], over_experts(gt[:, :, 3]), ALU.mult))
            link(nc.vector.tensor_tensor(gates[:, :, 0, :], gates[:, :, 0, :], gates[:, :, 1, :], ALU.add))
            nc.vector.tensor_copy(gates[:, :, 1, :], gates[:, :, 0, :]).then_inc(route_step, 1)
            nc.vector.tensor_copy(GT[:, :, 0:NE], gates[:, :, 0, :]).then_inc(route_step, 1)
            nc.vector.tensor_copy(cnt[:], ps[:, 7, 3 * NE:4 * NE]).then_inc(route_step, 1)
            dve.wait_ge(route_step, 6)
            dve.sem_inc(routed, 1)
            dve.sem_inc(selt_read, 2)
            dve.sem_inc(d_done, 1)
            for s in (e_silu, e_f, t_done, ft_lo_done, comb_read):
                dve.sem_inc(s, 1)

            def gathered_lo(p):
                for i, x in enumerate((X0, X1)):
                    dve.wait_ge(xg_hi_done, p * 2 + (i + 1))
                    nc.vector.tensor_tensor(xg_lo[:, 4 * i:4 * i + 4, :], x.rearrange("p (k s) -> p k s", k=4),
                                            xg_hi[:, 4 * i:4 * i + 4, :].bitcast(F32), ALU.subtract).then_inc(xg_lo_done, 1)

            def out_lo(p):
                for i in (0, 1):
                    dve.wait_ge(o_hi_done, p * 2 + (i + 1))
                    cols = slice(512 * i, 512 * (i + 1))
                    nc.vector.scalar_tensor_tensor(o_lo[:, cols], D_[:, i, :], slot_gate[:, 0:1],
                                                   o_hi[:, cols].bitcast(F32), ALU.mult, ALU.subtract).then_inc(o_lo_done, 1)

            def add_outputs(p, parts_):
                for i in parts_:
                    t, half = divmod(i, 2)
                    dve.wait_ge(comb_done, p * 6 + (i + 1))
                    cols = yt[:, t, 512 * half:512 * (half + 1)]
                    nc.vector.tensor_tensor(cols, cols, (X0, X1, X2)[i % 3][0:TT, :], ALU.add).then_inc(comb_read, 1)

            def hidden(c):
                dve.wait_ge(u_done, c + 1)
                dve.wait_ge(e_silu, c + 2)
                dve.wait_ge(t_done, c + 1)
                nc.vector.tensor_tensor(act_f[:], act_s[:], U_, ALU.mult).then_inc(e_f, 1)

            def expert_pass(p):
                def after(i):
                    for j in range(NJ):
                        c = p * NJ + j
                        if i == up_slot(j) + 1 and j:
                            hidden(c)
                        if i == (up_slot(0) + 1 if j == 0 else down_slot(j - 1) + 1):
                            dve.wait_ge(ft_hi_done, c + 1)
                            nc.vector.tensor_tensor(ft_lo[:], T_.rearrange("p (k s) -> p k s", k=4),
                                                    ft_hi[:].bitcast(F32), ALU.subtract).then_inc(ft_lo_done, 1)
                    if i == 0:
                        out_lo(p)
                    for q in range(3):
                        if i == up_slot(0) + 1 + q:
                            add_outputs(p, [q])
                        if i == down_slot(0) + 1 + q:
                            add_outputs(p, [3 + q])
                    if i == gate_slot(4) + 1:
                        dve.wait_ge(selt_done, p + 1)
                        nc.vector.tensor_copy(sel_t[:], X0[:, 0:T]).then_inc(selt_read, 1)
                        nc.vector.tensor_copy(slot_gate[:], X1[:, 0:1]).then_inc(selt_read, 1)
                    if i == gate_slot(4) + 1:
                        dve.wait_ge(extra_done, 1)
                        select(p + 1)

                for i in range(ES):
                    if i == up_slot(0) + 3:
                        hidden(p * NJ)
                    split_lo_pass(dve, p, i)
                    if i == 0:
                        gathered_lo(p)
                    else:
                        after(i - 2)

            with dve.Fori(0, NE) as p:
                expert_pass(p)
            n_over = dve.value_load(eids[0:1, 6:7], min_val=0, max_val=5)
            with dve.If(n_over > 0):
                with dve.Fori(0, n_over) as i:
                    expert_pass(i + NE)
                dve.nop()
            n_pass = n_over + NE
            out_lo(n_pass)
            add_outputs(n_pass, range(6))
            dve.wait_ge(fin_sq, 6)
            rstd_tokens()
            for t in range(3):
                nc.vector.scalar_tensor_tensor(yt[:, t, :], yt[:, t, :], nt[0:TT, t, 1:2], gb[:, 1, :], ALU.mult, ALU.mult
                                               ).then_inc(fin_out, 1)

        @block.tensor
        def _(pe):
            def bank(name):
                return ps[:, GROUP[name] % MM_BANKS, :]

            def group(name):
                q = GROUP[name]
                if q >= MM_BANKS:
                    pe.wait_ge(evac, q - MM_BANKS + 1)
                return ps[:, q % MM_BANKS, :]

            def mm3(out, a_hi, a_lo, b_hi, b_lo, start, stop):
                nc.tensor.matmul(out, a_hi, b_hi, start=start, stop=False)
                nc.tensor.matmul(out, a_hi, b_lo, start=False, stop=False)
                return nc.tensor.matmul(out, a_lo, b_hi, start=False, stop=stop)

            def dense_slot(n, ncol):
                size = slot_size(n)
                _, hi, lo = parts(n, size)
                return (x.rearrange("p (k n) -> p k n", n=ncol) for x in (hi, lo))

            def sums(name, rhs, ready, count):
                i = SUMS[name]
                if i:
                    pe.wait_ge(sums_read, i)
                for c, x in enumerate(rhs):
                    pe.wait_ge(ready, count(c))
                    ins = nc.tensor.matmul(SUM_BANK, ones[:], x, start=(c == 0), stop=(c == len(rhs) - 1))
                ins.then_inc(sums_done, 1)

            def token_sums(name, x, ready, count):
                if SUMS[name]:
                    pe.wait_ge(sums_read, SUMS[name])
                pe.wait_ge(ready, count)
                for t in range(3):
                    ins = nc.tensor.matmul(TOKEN_SUMS[:, t:t + 1], x[:, TT * t:TT * (t + 1)], ones[:, 0:1],
                                           start=True, stop=True)
                ins.then_inc(sums_done, 1)

            def spread(name, n):
                pe.wait_ge(sums_read, SUMS[name])
                pe.wait_ge(factors_done, n)
                nc.tensor.matmul(SUM_BANK, ones[0:TT, :], spread_in, start=True, stop=True).then_inc(sums_done, 1)

            pe.wait_ge(consts, 1)
            pe.wait_ge(x_landed, 16 * len(PIECES))
            for k in range(KD):
                out = group(("x", k))
                for t in range(3):
                    ins = nc.tensor.transpose(out[:, TT * t:TT * (t + 1)], x_tok[:, t, P * k:P * (k + 1)], ident[0:TT, 0:TT])
                ins.then_inc(mm_done, 1)
            pe.wait_ge(par_landed, 16 * 7)
            out = group(("params",))
            nc.tensor.transpose(out[:, 0:64], par_rows[:], ident[0:64, 0:64])
            for l in range(L):
                for c in range(KC):
                    o = 64 + (l * KC + c) * TAPS
                    ins = nc.tensor.transpose(out[:, o:o + TAPS], dw_rows[:, l, P * c:P * (c + 1)], ident[0:TAPS, 0:TAPS])
            ins.then_inc(mm_done, 1)

            def project(name_of, n, i, ncol, k_ready):
                out = group(name_of)
                hi, lo = dense_slot(n, ncol)
                nk = slot_size(n) // ncol
                for k in range(nk):
                    if k_ready:
                        k_ready(k)
                    cols = slice(P * i, P * (i + 1))
                    ins = mm3(out[:, 0:T], hi[:, k, cols], lo[:, k, cols], x_hi[:, k, :], x_lo[:, k, :],
                              k == 0, k == nk - 1)
                ins.then_inc(mm_done, 1)

            def split_ready(n):
                pe.wait_ge(lo_done, n + 1)

            def mixer_layer(l):
                b = MIX_BASE[l]

                def w_in_slot(s, halves=(0, 1)):
                    n = b + (s if s < S_DIAG else S_LATE)
                    split_ready(n)
                    for i in halves:
                        ready = (lambda k: pe.wait_ge(x_lo_done, KD * 2 * l + k + 1)) if s == 0 and i == 0 else None
                        project(("win", l, 2 * WIN_ORDER[s] + i), n, i, 256, ready)

                w_in_slot(0)
                token_sums(("norm", 2 * l), sqs, sq_ready, 2 * l + 1)
                w_in_slot(1)
                spread(("spread norm", 2 * l), 2 * l + 1)
                pe.wait_ge(past_landed, 16 * 3 * (l + 1))
                n_rows = DB * PB
                out = group(("past_pool", l))
                for g in range(NG):
                    ins = nc.tensor.transpose(out[:, n_rows * g:n_rows * (g + 1)], state_io[:, 0, P * g:P * (g + 1)],
                                              ident[0:n_rows, 0:n_rows])
                ins.then_inc(mm_done, 1)
                for i in (0, 1):
                    out = group(("past_conv", l, i))
                    for c in (0, 1):
                        for hb in (0, 1):
                            at = n_rows * (2 * c + hb)
                            ins = nc.tensor.transpose(out[:, at:at + n_rows],
                                                      state_io[:, 1 + hb, P * (2 * i + c):P * (2 * i + c + 1)],
                                                      ident[0:n_rows, 0:n_rows])
                    ins.then_inc(mm_done, 1)
                for s in range(2, S_DIAG):
                    w_in_slot(s)
                def mean_of(c):
                    pe.wait_ge(y_ready, KC * l + Y_ORDER.index(c) + 1)
                    return nc.tensor.matmul(SUM_BANK, ones[:], y[:, c, :], start=(c == Y_ORDER[0]), stop=(c == Y_ORDER[-1]))

                diag_taps = sum(PE_TAPS) * l
                for q, c in enumerate(PE_TILES):
                    out = group(("conv", l, c))
                    pe.wait_ge(e_lo_done, len(PE_TILES) * l + q + 1)
                    for k, (first, end) in enumerate(DIAG_PARTS[q]):
                        n = b + S_DIAG + 2 * q + k
                        pe.wait_ge(diag_hi_done, N_DIAG * l + 2 * q + k + 1)
                        diag_taps += end - first
                        pe.wait_ge(diag_lo_done, diag_taps)
                        hi, lo = dense_slot(n, P)
                        for j in range(first, end):
                            ins = mm3(out[:, 0:TP], hi[:, j - first, :], lo[:, j - first, :], e_hi[:, q, j:j + TP],
                                      e_lo[:, q, j:j + TP], j == 0, j == PE_TAPS[q] - 1)
                        ins.then_inc(mm_done if k else w_used, 1)
                    if q == 1:
                        pe.wait_ge(sums_read, SUMS[("mean", l)])
                        mean_of(Y_ORDER[0])
                        mean_of(Y_ORDER[1])

                def pool_map(g):
                    out = group(("pool", l, g))
                    hi, lo = dense_slot(b + S_POOL_W, P)
                    pe.wait_ge(pooled_lo, NG * l + POOL_ORDER.index(g) + 1)
                    x = pooled_at(g)
                    mm3(out[:, 0:T], hi[:, g, :], lo[:, g, :], x[0], x[1], True, True).then_inc(mm_done, 1)

                mean_of(Y_ORDER[2])
                mean_of(Y_ORDER[3]).then_inc(sums_done, 1)
                w_in_slot(5, (0,))
                token_sums(("var", l), z[:, 0, :], sq_sum, l + 1)
                w_in_slot(5, (1,))
                spread(("spread var", l), 2 * l + 2)
                split_ready(b + S_POOL_W)
                for g in POOL_ORDER[:2]:
                    pool_map(g)
                split_ready(b + S_PW)
                for m in range(KC):
                    ready = (lambda k: pe.wait_ge(ln_lo, KC * l + k + 1)) if m == 0 else None
                    project(("pw", l, m), b + S_PW, m, CW, ready)
                for g in POOL_ORDER[2:]:
                    pool_map(g)

                def logits(k):
                    pe.wait_ge(evac, GROUP[("wout", 1, k)] + 1)
                    if k == 0:
                        pe.wait_ge(rwg_done, KD)
                        pe.wait_ge(sums_read, SUMS[("spread var", 1)] + 1)
                    for t in range(3):
                        ins = nc.tensor.matmul(ps[0:TT, 6, NE * t:NE * (t + 1)], h[:, k, TT * t:TT * (t + 1)],
                                               rwg[:, k, :], start=(k == 0 and t == 0), stop=(k == KD - 1 and t == 2))
                    return ins

                for s in range(4):
                    split_ready(b + S_OUT + s)
                    hi, lo = dense_slot(b + S_OUT + s, 256)
                    for i in (0, 1):
                        out = group(("wout", l, 2 * s + i))
                        for k in M_ORDER:
                            if s == 0 and i == 0:
                                pe.wait_ge(evac, GROUP[("pool", l, k) if k < NG else ("pw", l, k - NG)] + 1)
                            cols = slice(P * i, P * (i + 1))
                            ins = mm3(out[:, 0:T], hi[:, k, cols], lo[:, k, cols], m_hi[:, k, :], m_lo[:, k, :],
                                      k == M_ORDER[0], k == M_ORDER[-1])
                        ins.then_inc(mm_done, 1)
                    m = 2 * s + 1
                    if l == 1 and s:
                        for k in (m - 3, m - 2):
                            logits(k)
                    if l == 1 and m in HALF_DONE:
                        i = HALF_DONE.index(m)
                        if m == KD - 1:
                            pe.wait_ge(evac, GROUP[("wout", 1, KD - 1)] + 1)
                        for t in range(3):
                            out = group(("htok", t, i))
                            for k in range(4):
                                ins = nc.tensor.transpose(out[0:TT, P * k:P * (k + 1)],
                                                          h[:, 4 * i + k, TT * t:TT * (t + 1)], ident[:])
                            ins.then_inc(mm_done, 1)
                if l == 1:
                    logits(KD - 2)
                    logits(KD - 1).then_inc(logits_done, 1)
                pe.wait_ge(packed, l + 1)
                srcs = [lambda g: z[:, g, 0:DB * PB],
                        lambda g: y[:, g, 0:HB * CB],
                        lambda g: y[:, g, HB * CB:DB * CB],
                        lambda g: pool_ext[:, g, PSEG - PB:PSEG],
                        lambda g: conv_ext[:, g, CSEG - CB:CSEG]]
                for i, (_, rows) in enumerate(state_dsts(l)):
                    out = group(("state", l, i))
                    for g in range(NG):
                        ins = nc.tensor.transpose(out[0:rows, P * g:P * (g + 1)], srcs[i](g), ident[:])
                    ins.then_inc(mm_done, 1)

            mixer_layer(0)

            sums(("norm", 1), [sqs], sq_ready, lambda c: 2)
            pe.wait_ge(x_lo_done, KD * 2)

            def gate_up(i, uu):
                u = i * 3 + uu
                for s in (0, 1):
                    pe.wait_ge(lo_done, u * 2 + (FFN_BASE + s + 1))
                    hi, lo = dense_slot(FFN_BASE + 2 * uu + s, 256)
                    for x in (0, 1):
                        pe.wait_ge(evac, u * 4 + (GU0 + 2 * s + x - MM_BANKS + 1))
                        for k in range(KD):
                            cols = slice(P * x, P * (x + 1))
                            ins = mm3(gu_bank(uu, 2 * s + x), hi[:, k, cols], lo[:, k, cols], x_hi[:, k, :], x_lo[:, k, :],
                                      k == 0, k == KD - 1)
                        ins.then_inc(mm_done, 1)

            with pe.Fori(0, LOOPS) as i:
                for uu in range(3):
                    gate_up(i, uu)
            for uu in range(FU - 3 * LOOPS):
                gate_up(LOOPS, uu)
            n = DOWN_BASE
            for c, ks in enumerate(DOWN_PARTS):
                outs = [group(("down", 2 * c + i)) for i in (0, 1)]
                k0 = 0
                for part, nk in enumerate(ks):
                    split_ready(n)
                    hi, lo = dense_slot(n, 256)
                    pe.wait_ge(f_lo_done, min(k0 + nk, NFT))
                    for i in (0, 1):
                        for k in range(nk):
                            cols = slice(P * i, P * (i + 1))
                            ins = mm3(outs[i][:, 0:T], hi[:, k, cols], lo[:, k, cols], f_hi[:, k0 + k, :], f_lo[:, k0 + k, :],
                                      k0 + k == 0, k0 + k == NFT - 1)
                        if part == len(ks) - 1:
                            ins.then_inc(mm_done, 1)
                    if part < len(ks) - 1:
                        ins.then_inc(w_used, 1)
                    k0 += nk
                    n += 1
            mixer_layer(1)

            pe.wait_ge(hot_done, 1)
            for t in range(3):
                for u in range(t + 1):
                    nc.tensor.matmul(ps[0:TT, 7, NE * t:NE * (t + 1)], (before if u == t else ones)[0:TT, 0:TT],
                                     hot[:, u, :], start=(u == 0), stop=(u == t))
            for u in range(3):
                ins = nc.tensor.matmul(ps[:, 7, 3 * NE:4 * NE], ones[0:TT, :], hot[:, u, :], start=(u == 0), stop=(u == 2))
            ins.then_inc(ranks_done, 1)

            def gather(p, half):
                pe.wait_ge(sel_ready, p * 3 + 3)
                for m in range(4 * half, 4 * half + 4):
                    for t in range(3):
                        for src in (hn_hi, hn_lo):
                            ins = nc.tensor.matmul((X0, X1)[half][:, P * (m % 4):P * (m % 4 + 1)],
                                                   src[:, t, P * m:P * (m + 1)], sel[:, t, :],
                                                   start=(t == 0 and src is hn_hi), stop=(t == 2 and src is hn_lo))
                ins.then_inc(gather_done, 1)

            def combine(p, outputs):
                pe.wait_ge(o_lo_done, p * 2 + 2)
                pe.wait_ge(selt_read, p * 2 + 2)
                for i in outputs:
                    t, half = divmod(i, 2)
                    pe.wait_ge(comb_read, p * 6 + max(i - 1, 1))
                    for o in (o_hi, o_lo):
                        ins = nc.tensor.matmul((X0, X1, X2)[i % 3][0:TT, :], sel_t[:, TT * t:TT * (t + 1)],
                                               o[:, 512 * half:512 * (half + 1)], start=(o is o_hi), stop=(o is o_lo))
                    ins.then_inc(comb_done, 1)

            def expert_pass(p):
                def hidden(j, slot0, out, done):
                    for half in (0, 1):
                        i = slot0 + half
                        pe.wait_ge(lo_done, p * ES + (MOE_BASE + i + 1))
                        _, hi, lo = (x.rearrange("p (k n) -> p k n", k=4) for x in parts(MOE_BASE + i))
                        for k in range(4):
                            kk = 4 * half + k
                            ins = mm3(out, xg_hi[:, kk, :], xg_lo[:, kk, :], hi[:, k, :], lo[:, k, :], kk == 0, kk == 7)
                        ins.then_inc(done if half else w_used, 1)

                def down(j):
                    pe.wait_ge(ft_lo_done, p * NJ + (j + 2))
                    if j == 0:
                        pe.wait_ge(o_lo_done, p * 2 + 2)
                    for half in (0, 1):
                        i = down_slot(j) + half
                        pe.wait_ge(lo_done, p * ES + (MOE_BASE + i + 1))
                        _, hi, lo = (x.rearrange("p (k n) -> p k n", k=2) for x in parts(MOE_BASE + i))
                        for k in range(2):
                            for d in (0, 1):
                                cols = slice(512 * d, 512 * (d + 1))
                                kk = 2 * half + k
                                ins = mm3(D_[:, d, :], ft_hi[:, kk, :], ft_lo[:, kk, :], hi[:, k, cols], lo[:, k, cols],
                                          j == 0 and kk == 0, j == NJ - 1 and kk == 3)
                        ins.then_inc(d_done if j == NJ - 1 and half else w_used, 1)

                pe.wait_ge(xg_lo_done, p * 2 + 2)
                for j in range(NJ):
                    c = p * NJ + j
                    pe.wait_ge(e_silu, c + 1)
                    hidden(j, gate_slot(j), G_, g_done)
                    pe.wait_ge(e_f, c + 1)
                    hidden(j, up_slot(j), U_, u_done)
                    if j:
                        down(j - 1)
                    if j < 2:
                        combine(p, range(3 * j, 3 * j + 3))
                    pe.wait_ge(e_f, c + 2)
                    pe.wait_ge(ft_lo_done, c + 1)
                    for k in range(4):
                        ins = nc.tensor.transpose(T_[:, P * k:P * (k + 1)], act_f[:, P * k:P * (k + 1)], ident[:])
                    ins.then_inc(t_done, 1)
                    if j == 3:
                        pe.wait_ge(comb_read, p * 6 + 7)
                        for t in range(3):
                            nc.tensor.transpose(X0[:, TT * t:TT * (t + 1)], sel[:, t, :].bitcast(F32), ident[0:TT, 0:TT])
                        for t in range(3):
                            ins = nc.tensor.matmul(X1[:, 0:1], sel[:, t, :].bitcast(F32), GT[:, t, ds(p, 1)],
                                                   start=(t == 0), stop=(t == 2))
                        ins.then_inc(selt_done, 1)
                    if j >= NJ - 2:
                        pe.wait_ge(selt_read, p * 2 + 4)
                        gather(p + 1, j - (NJ - 2))
                down(NJ - 1)

            pe.wait_ge(hn_lo_done, 3)
            gather(0, 0)
            gather(0, 1)
            with pe.Fori(0, NE) as p:
                expert_pass(p)
            pe.wait_ge(extra_done, 1)
            n_over = pe.value_load(eids[0:1, 6:7], min_val=0, max_val=5)
            with pe.If(n_over > 0):
                with pe.Fori(0, n_over) as i:
                    expert_pass(i + NE)
                pe.nop()
            combine(n_over + NE, range(6))


_INS = ['x_prompt', 'x_sample', 'state_pool', 'state_conv', 'meta_tokens', 'norm1_g', 'w_in', 'pool_w', 'pool_scale',
        'conv_dw_w', 'conv_dw_b', 'conv_ln_g', 'conv_ln_b', 'conv_pw_w', 'w_out', 'norm2_g', 'ffn_w_gate', 'ffn_w_up',
        'ffn_w_down', 'router_w', 'moe_w_gate', 'moe_w_up', 'moe_w_down', 'final_norm_g']


def kernel(**inputs):
    import numpy as _np
    import concourse.bacc as _bacc
    from concourse import mybir as _mybir
    from concourse.bass_utils import run_bass_kernel_spmd as _run

    nc = _bacc.Bacc("TRN2", target_bir_lowering=False, num_devices=1)
    arrays, args = {}, []
    for name in _INS:
        a = _np.ascontiguousarray(inputs[name])
        arrays[f"in_{name}_dram"] = a
        args.append(nc.dram_tensor(f"in_{name}_dram", a.shape, _mybir.dt.from_np(a.dtype), kind="ExternalInput").ap())
    layers, prompts = inputs["w_in"].shape[0], inputs["x_prompt"].shape[0]
    pool_state, conv_state = inputs["state_pool"].shape, inputs["state_conv"].shape
    outs = [inputs["x_prompt"].shape, inputs["x_sample"].shape,
            (layers, prompts) + tuple(pool_state[2:]), (layers, prompts) + tuple(conv_state[2:]),
            pool_state, conv_state]
    for i, shape in enumerate(outs):
        args.append(nc.dram_tensor(f"out_{i}_dram", tuple(shape), _mybir.dt.float32, kind="ExternalOutput").ap())
    hybrid_trunk(nc, *args)
    r = _run(nc, [arrays], core_ids=[0])
    return tuple(r.results[0][f"out_{i}_dram"] for i in range(len(outs)))
```
